# Optimizing a Trainium2 kernel written in Bass

```python
import jax, jax.numpy as jnp
from jax import lax
import numpy as np
import math
import jax
import jax.numpy as jnp

D_MODEL = 1024
BATCH = 1
SEQ = 256
DEPTH = 1

N_MEM = 256
HEAD_DIM = 64
FOX_HEADS = D_MODEL // HEAD_DIM
FOX_W = FOX_HEADS * HEAD_DIM
SB_HEADS = D_MODEL // HEAD_DIM
SB_W = SB_HEADS * HEAD_DIM
LRU_W = D_MODEL
LRU_BLOCKS = D_MODEL // HEAD_DIM
LRU_BW = LRU_W // LRU_BLOCKS
LRU_CONV = 4
LRU_C = 8.0
MEM_HEADS = 4
MEM_HD = D_MODEL // MEM_HEADS
MEM_W = MEM_HEADS * MEM_HD
N_BRANCH = 4
BRANCH_W = D_MODEL
D_FF = ((8 * D_MODEL // 3 + 255) // 256) * 256
FFN_CONV = 3
Q_BLOCK = 128
EPS = 1e-6
N_IN = 3 * FOX_W + FOX_HEADS + 2 * LRU_W + 3 * SB_W + MEM_W + N_BRANCH * D_MODEL


def _column_slices():
    widths = (("fox_q", FOX_W), ("fox_k", FOX_W), ("fox_v", FOX_W), ("fox_f", FOX_HEADS),
              ("lru_x", LRU_W), ("lru_g", LRU_W),
              ("sb_q", SB_W), ("sb_k", SB_W), ("sb_v", SB_W),
              ("mem_q", MEM_W), ("gates", N_BRANCH * D_MODEL))
    out, start = {}, 0
    for name, w in widths:
        out[name] = (start, start + w)
        start += w
    return out

def _rms(x, g):
    x32 = x.astype(jnp.float32)
    y = x32 * lax.rsqrt(jnp.mean(x32 * x32, axis=-1, keepdims=True) + EPS)
    return (y * g.astype(jnp.float32)).astype(x.dtype)

def _causal_dwconv(x, w, b):
    k, s = w.shape[0], x.shape[1]
    xp = jnp.pad(x, ((0, 0), (k - 1, 0), (0, 0)))
    out = b
    for i in range(k):
        out = out + xp[:, i:i + s] * w[i]
    return out

def _heads(t, n):
    b, s, _ = t.shape
    return t.reshape(b, s, n, -1).transpose(0, 2, 1, 3)

def _merge_heads(t):
    b, h, s, d = t.shape
    return t.transpose(0, 2, 1, 3).reshape(b, s, h * d)

def _fox_attention(q, k, v, log_f):
    b, h, s, d = q.shape
    nb = s // Q_BLOCK
    scale = d ** -0.5
    cum_f = jnp.cumsum(log_f, axis=-1)
    q_blk = q.reshape(b, h, nb, Q_BLOCK, d).transpose(2, 0, 1, 3, 4)
    f_blk = cum_f.reshape(b, h, nb, Q_BLOCK).transpose(2, 0, 1, 3)
    k_pos = jnp.arange(s)

    def block(args):
        qi, fi, bi = args
        q_pos = bi * Q_BLOCK + jnp.arange(Q_BLOCK)
        logits = jnp.einsum('bhqd,bhkd->bhqk', qi, k) * scale + (fi[..., :, None] - cum_f[..., None, :])
        logits = jnp.where(k_pos[None, :] <= q_pos[:, None], logits, -jnp.inf)
        p = jax.nn.softmax(logits, axis=-1)
        return jnp.einsum('bhqk,bhkd->bhqd', p, v)

    out = lax.map(block, (q_blk, f_blk, jnp.arange(nb)))
    return out.transpose(1, 2, 0, 3, 4).reshape(b, h, s, d)

def _stick_breaking_attention(q, k, v):
    b, h, s, d = q.shape
    nb = s // Q_BLOCK
    scale = d ** -0.5
    q_blk = q.reshape(b, h, nb, Q_BLOCK, d).transpose(2, 0, 1, 3, 4)
    k_pos = jnp.arange(s)

    def block(args):
        qi, bi = args
        q_pos = bi * Q_BLOCK + jnp.arange(Q_BLOCK)
        causal = k_pos[None, :] < q_pos[:, None]
        z = jnp.einsum('bhqd,bhkd->bhqk', qi, k) * scale
        log_1m_beta = jnp.where(causal, jax.nn.log_sigmoid(-z), 0.0)
        excl = lax.cumsum(log_1m_beta, axis=3, reverse=True) - log_1m_beta
        weights = jnp.where(causal, jnp.exp(jax.nn.log_sigmoid(z) + excl), 0.0)
        return jnp.einsum('bhqk,bhkd->bhqd', weights, v)

    out = lax.map(block, (q_blk, jnp.arange(nb)))
    return out.transpose(1, 2, 0, 3, 4).reshape(b, h, s, d)

def _mem_attention(q, k, v):
    scale = q.shape[-1] ** -0.5
    p = jax.nn.softmax(jnp.einsum('bhsd,bhmd->bhsm', q, k) * scale, axis=-1)
    return jnp.einsum('bhsm,bhmd->bhsd', p, v)

def _rg_lru_branch(x, gate, conv_w, conv_b, w_a, b_a, w_x, b_x, lam):
    b, s, w = x.shape
    xc = _causal_dwconv(x, conv_w, conv_b).astype(jnp.float32)
    xg = xc.reshape(b, s, LRU_BLOCKS, LRU_BW)
    r = jax.nn.sigmoid(jnp.einsum('bsnd,nde->bsne', xg, w_a).reshape(b, s, w) + b_a)
    i = jax.nn.sigmoid(jnp.einsum('bsnd,nde->bsne', xg, w_x).reshape(b, s, w) + b_x)
    log_a = -LRU_C * r * jax.nn.softplus(-lam)
    a = jnp.exp(log_a)
    u = jnp.sqrt(-jnp.expm1(2.0 * log_a)) * (i * xc)

    def combine(c1, c2):
        a1, h1 = c1
        a2, h2 = c2
        return a1 * a2, a2 * h1 + h2

    _, hs = lax.associative_scan(combine, (a, u), axis=1)
    return hs * jax.nn.gelu(gate.astype(jnp.float32))

def first_inputs(seed: int = 0) -> dict:
    key = jax.random.key(seed)
    ks = jax.random.split(key, 32)
    f32 = jnp.float32

    def nrm(k, shape, scale):
        return jax.random.normal(k, shape, f32) * scale

    def gain(k, shape):
        return 1.0 + 0.02 * jax.random.normal(k, shape, f32)

    res_scale = (2 * DEPTH) ** -0.5
    u = jax.random.uniform(ks[12], (DEPTH, LRU_W), f32, 0.9, 0.999)
    sig = u ** (1.0 / LRU_C)
    lru_lambda = jnp.log(sig) - jnp.log1p(-sig)
    return {
        "x": nrm(ks[0], (BATCH, SEQ, D_MODEL), 1.0),
        "mem": nrm(ks[1], (BATCH, N_MEM, D_MODEL), 1.0),
        "attn_norm_g": gain(ks[2], (DEPTH, D_MODEL)),
        "mem_norm_g": gain(ks[3], (DEPTH, D_MODEL)),
        "w_in": nrm(ks[4], (DEPTH, D_MODEL, N_IN), D_MODEL ** -0.5),
        "b_forget": jax.random.uniform(ks[5], (DEPTH, FOX_HEADS), f32, 2.0, 6.0),
        "fox_q_norm_g": gain(ks[6], (DEPTH, HEAD_DIM)),
        "fox_k_norm_g": gain(ks[7], (DEPTH, HEAD_DIM)),
        "lru_conv_w": nrm(ks[8], (DEPTH, LRU_CONV, LRU_W), LRU_CONV ** -0.5),
        "lru_conv_b": nrm(ks[9], (DEPTH, LRU_W), 0.01),
        "lru_w_a": nrm(ks[10], (DEPTH, LRU_BLOCKS, LRU_BW, LRU_BW), LRU_BW ** -0.5),
        "lru_b_a": nrm(ks[11], (DEPTH, LRU_W), 0.01),
        "lru_w_x": nrm(ks[13], (DEPTH, LRU_BLOCKS, LRU_BW, LRU_BW), LRU_BW ** -0.5),
        "lru_b_x": nrm(ks[14], (DEPTH, LRU_W), 0.01),
        "lru_lambda": lru_lambda,
        "w_mem_kv": nrm(ks[15], (DEPTH, D_MODEL, 2 * MEM_W), D_MODEL ** -0.5),
        "mem_q_norm_g": gain(ks[16], (DEPTH, MEM_HD)),
        "mem_k_norm_g": gain(ks[17], (DEPTH, MEM_HD)),
        "b_gate": nrm(ks[18], (DEPTH, N_BRANCH, D_MODEL), 0.01),
        "w_branch": nrm(ks[19], (DEPTH, N_BRANCH, BRANCH_W, D_MODEL), BRANCH_W ** -0.5),
        "w_out": nrm(ks[20], (DEPTH, D_MODEL, D_MODEL), D_MODEL ** -0.5 * res_scale),
        "ffn_norm_g": gain(ks[21], (DEPTH, D_MODEL)),
        "w_up": nrm(ks[22], (DEPTH, D_MODEL, 2 * D_FF), D_MODEL ** -0.5),
        "ffn_conv_w": nrm(ks[23], (DEPTH, FFN_CONV, D_FF), FFN_CONV ** -0.5),
        "ffn_conv_b": nrm(ks[24], (DEPTH, D_FF), 0.01),
        "w_down": nrm(ks[25], (DEPTH, D_FF, D_MODEL), D_FF ** -0.5 * res_scale),
    }

def first_block(x, mem, attn_norm_g, mem_norm_g, w_in, b_forget, fox_q_norm_g, fox_k_norm_g,
              lru_conv_w, lru_conv_b, lru_w_a, lru_b_a, lru_w_x, lru_b_x, lru_lambda,
              w_mem_kv, mem_q_norm_g, mem_k_norm_g, b_gate, w_branch, w_out,
              ffn_norm_g, w_up, ffn_conv_w, ffn_conv_b, w_down):
    f32 = jnp.float32
    cols = _column_slices()
    b, s, _ = x.shape
    for l in range(DEPTH):
        h = _rms(x, attn_norm_g[l])
        w_l = w_in[l]

        def proj(name):
            lo, hi = cols[name]
            return h @ w_l[:, lo:hi]

        fq = _rms(_heads(proj("fox_q"), FOX_HEADS), fox_q_norm_g[l]).astype(f32)
        fk = _rms(_heads(proj("fox_k"), FOX_HEADS), fox_k_norm_g[l]).astype(f32)
        fv = _heads(proj("fox_v"), FOX_HEADS).astype(f32)
        log_f = jax.nn.log_sigmoid(proj("fox_f").astype(f32) + b_forget[l]).transpose(0, 2, 1)
        y_fox = _merge_heads(_fox_attention(fq, fk, fv, log_f))

        y_lru = _rg_lru_branch(proj("lru_x"), proj("lru_g"), lru_conv_w[l], lru_conv_b[l],
                               lru_w_a[l], lru_b_a[l], lru_w_x[l], lru_b_x[l], lru_lambda[l])

        sq = _heads(proj("sb_q"), SB_HEADS).astype(f32)
        sk = _heads(proj("sb_k"), SB_HEADS).astype(f32)
        sv = _heads(proj("sb_v"), SB_HEADS).astype(f32)
        y_sb = _merge_heads(_stick_breaking_attention(sq, sk, sv))

        mem_n = _rms(mem, mem_norm_g[l])
        w_kv = w_mem_kv[l]
        mk = _rms(_heads(mem_n @ w_kv[:, :MEM_W], MEM_HEADS), mem_k_norm_g[l]).astype(f32)
        mv = _heads(mem_n @ w_kv[:, MEM_W:], MEM_HEADS).astype(f32)
        mq = _rms(_heads(proj("mem_q"), MEM_HEADS), mem_q_norm_g[l]).astype(f32)
        y_mem = _merge_heads(_mem_attention(mq, mk, mv))

        branches = jnp.stack([y_fox, y_lru, y_sb, y_mem], axis=2).astype(x.dtype)
        gates = jax.nn.sigmoid(proj("gates").reshape(b, s, N_BRANCH, D_MODEL) + b_gate[l])
        projected = jnp.einsum('bsnc,ncd->bsnd', branches, w_branch[l])
        mixed = jnp.sum(gates * projected, axis=2)
        x = x + mixed @ w_out[l]

        h2 = _rms(x, ffn_norm_g[l])
        w_u = w_up[l]
        gate_pre = _causal_dwconv(h2 @ w_u[:, :D_FF], ffn_conv_w[l], ffn_conv_b[l])
        val = h2 @ w_u[:, D_FF:]
        x = x + (jax.nn.silu(gate_pre) * val) @ w_down[l]
    return x


DEPTH_2 = 2

GRID_W = 64
CTX_LEN = 256
BRANCH_W_2 = 512
NA_HEADS = 8
NA_DH = BRANCH_W_2 // NA_HEADS
NA_WIN_R = 8
NA_WIN_C = 16
DA_HEADS = 4
DA_DH = 64
DA_VD = 2 * DA_DH
DA_QK = DA_HEADS * 2 * DA_DH
GM_GROUPS = 4
GM_CHUNK = 128
GM_GW = BRANCH_W_2 // GM_GROUPS
N_BRANCH_2 = 3
N_EXPERTS = 16
EC_CAPACITY = 2
EXPERT_FF = 1024
ROPE_THETA = 10000.0
ROPE_AXIS = DA_DH // 2
N_MOD = 6
KV_SIZES = (BRANCH_W_2, BRANCH_W_2, DA_QK, DA_HEADS * DA_VD)
Q_SIZES = (BRANCH_W_2, DA_QK, BRANCH_W_2, BRANCH_W_2, N_BRANCH_2 * D_MODEL)
KV_COLS = sum(KV_SIZES)
PROJ_COLS = KV_COLS + sum(Q_SIZES)


def _split(z, sizes):
    offs = np.cumsum(sizes)[:-1].tolist()
    return jnp.split(z, offs, axis=-1)

def rmsnorm(x, g):
    xf = x.astype(jnp.float32)
    y = xf * lax.rsqrt(jnp.mean(xf * xf, axis=-1, keepdims=True) + EPS)
    return y.astype(x.dtype) * g

def layernorm(x, g, b):
    xf = x.astype(jnp.float32)
    mu = jnp.mean(xf, axis=-1, keepdims=True)
    var = jnp.mean(jnp.square(xf - mu), axis=-1, keepdims=True)
    return ((xf - mu) * lax.rsqrt(var + EPS)).astype(x.dtype) * g + b

def modulate(h, shift, scale):
    return h * (1 + scale) + shift

def rope_tables(n):
    t = jnp.arange(n)
    inv = ROPE_THETA ** (-jnp.arange(0, ROPE_AXIS, 2, dtype=jnp.float32) / ROPE_AXIS)
    ang_r = (t // GRID_W).astype(jnp.float32)[:, None] * inv
    ang_c = (t % GRID_W).astype(jnp.float32)[:, None] * inv
    return (jnp.cos(ang_r), jnp.sin(ang_r), jnp.cos(ang_c), jnp.sin(ang_c))

def _rot(x, cos, sin):
    x1, x2 = jnp.split(x, 2, axis=-1)
    return jnp.concatenate([x1 * cos - x2 * sin, x1 * sin + x2 * cos], axis=-1)

def rope_2d(x, tabs):
    cr, sr, cc, sc = [t.astype(x.dtype)[None, :, None, None, :] for t in tabs]
    xr, xcol = jnp.split(x, 2, axis=-1)
    return jnp.concatenate([_rot(xr, cr, sr), _rot(xcol, cc, sc)], axis=-1)

def dense_attn(q, k, v):
    B, n, H, dh = q.shape
    s = jnp.einsum('bqhd,bkhd->bhqk', q, k) * (dh ** -0.5)
    p = jax.nn.softmax(s.astype(jnp.float32), axis=-1).astype(v.dtype)
    return jnp.einsum('bhqk,bkhd->bqhd', p, v).reshape(B, n, H * dh)

def neighbourhood_attn(q, k, v, kc, vc, rpb):
    B, L, H, dh = q.shape
    Lc = kc.shape[1]
    rows = L // GRID_W
    wr = min(NA_WIN_R, rows)
    scale = dh ** -0.5
    kg = k.reshape(B, rows, GRID_W, H, dh)
    vg = v.reshape(B, rows, GRID_W, H, dh)
    qg = jnp.moveaxis(q.reshape(B, rows, GRID_W, H, dh), 1, 0)
    col = jnp.arange(GRID_W)
    col_start = jnp.clip(col - NA_WIN_C // 2, 0, GRID_W - NA_WIN_C)
    col_idx = col_start[:, None] + jnp.arange(NA_WIN_C)[None, :]
    dc = col_idx - col[:, None] + (NA_WIN_C - 1)

    def row_block(args):
        r, qr = args
        r0 = jnp.clip(r - wr // 2, 0, rows - wr)
        kw = lax.dynamic_slice_in_dim(kg, r0, wr, axis=1)[:, :, col_idx]
        vw = lax.dynamic_slice_in_dim(vg, r0, wr, axis=1)[:, :, col_idx]
        dr = r0 + jnp.arange(wr) - r + (NA_WIN_R - 1)
        bias = jnp.transpose(rpb[:, dr[:, None, None], dc[None]], (0, 2, 1, 3))
        s_loc = jnp.einsum('bqhd,brqjhd->bhqrj', qr, kw) * scale + bias[None]
        s_ctx = jnp.einsum('bqhd,bchd->bhqc', qr, kc) * scale
        s = jnp.concatenate([s_ctx, s_loc.reshape(B, H, GRID_W, wr * NA_WIN_C)], axis=-1)
        p = jax.nn.softmax(s.astype(jnp.float32), axis=-1).astype(v.dtype)
        p_loc = p[..., Lc:].reshape(B, H, GRID_W, wr, NA_WIN_C)
        return (jnp.einsum('bhqc,bchd->bqhd', p[..., :Lc], vc)
                + jnp.einsum('bhqrj,brqjhd->bqhd', p_loc, vw))

    out = lax.map(row_block, (jnp.arange(rows), qg))
    return jnp.moveaxis(out, 0, 1).reshape(B, L, H * dh)

def diff_attend(q, k, v, lam):
    s = jnp.einsum('bqhcd,bkhcd->bhcqk', q, k) * (q.shape[-1] ** -0.5)
    p = jax.nn.softmax(s.astype(jnp.float32), axis=-1)
    a = (p[:, :, 0] - lam * p[:, :, 1]).astype(v.dtype)
    return jnp.einsum('bhqk,bkhd->bqhd', a, v)

def diff_attn_blocks(q, k, v, lam):
    B, L, H, _, dh = q.shape
    nb = L // Q_BLOCK
    qblk = jnp.moveaxis(q.reshape(B, nb, Q_BLOCK, H, 2, dh), 1, 0)
    out = lax.map(lambda qb: diff_attend(qb, k, v, lam), qblk)
    return jnp.moveaxis(out, 0, 1).reshape(B, L, H, v.shape[-1])

def diff_head_norm(o, g, lam_init):
    B, n = o.shape[:2]
    return (rmsnorm(o, g) * (1.0 - lam_init)).reshape(B, n, -1)

def gmlp_gate(u, v, ln_g, ln_b, w_s, b_s):
    B, n, _ = u.shape
    vn = layernorm(v, ln_g, ln_b).reshape(B, n // GM_CHUNK, GM_CHUNK, GM_GROUPS, GM_GW)
    mixed = jnp.einsum('gpq,bnqgc->bnpgc', w_s, vn) + jnp.swapaxes(b_s, 0, 1)[:, :, None]
    return u * mixed.reshape(B, n, BRANCH_W_2)

def branch_merge(ya, yb, yc, gates, w_branch, w_out):
    ga, gb, gc = jnp.split(jax.nn.sigmoid(gates), N_BRANCH_2, axis=-1)
    m = ga * (ya @ w_branch[0]) + gb * (yb @ w_branch[1]) + gc * (yc @ w_branch[2])
    return m @ w_out

def ec_moe(h, w_r, w1, w3, w2):
    B, n, D = h.shape
    cap = max(1, EC_CAPACITY * n // N_EXPERTS)
    aff = jax.nn.softmax((h @ w_r).astype(jnp.float32), axis=-1)
    gate, idx = lax.top_k(jnp.swapaxes(aff, 1, 2), cap)
    xin = jax.vmap(lambda hb, ib: hb[ib])(h, idx)
    hid = jax.nn.silu(jnp.einsum('becd,edf->becf', xin, w1)) * jnp.einsum('becd,edf->becf', xin, w3)
    ye = jnp.einsum('becf,efd->becd', hid, w2) * gate[..., None].astype(h.dtype)
    return jax.vmap(lambda yb, ib: jnp.zeros((n, D), h.dtype).at[ib.reshape(-1)].add(yb.reshape(-1, D)))(ye, idx)

def _na_heads(t):
    return t.reshape(t.shape[0], t.shape[1], NA_HEADS, NA_DH)

def _da_qk(t):
    return t.reshape(t.shape[0], t.shape[1], DA_HEADS, 2, DA_DH)

def _da_v(t):
    return t.reshape(t.shape[0], t.shape[1], DA_HEADS, DA_VD)

def second_inputs(seed: int = 0) -> dict:
    key = jax.random.key(seed)
    ks = jax.random.split(key, 32)
    f32 = jnp.float32

    def nrm(k, shape, scale):
        return jax.random.normal(k, shape, f32) * scale

    D = D_MODEL
    return {
        "x": nrm(ks[0], (BATCH, SEQ, D), 1.0),
        "c": nrm(ks[1], (BATCH, D), 1.0),
        "ctx": nrm(ks[2], (BATCH, CTX_LEN, D), 1.0),
        "c_ctx": nrm(ks[3], (D,), 1.0),
        "w_ada": nrm(ks[4], (DEPTH_2, D, N_MOD * D), 0.5 * D ** -0.5),
        "b_ada": nrm(ks[5], (DEPTH_2, N_MOD * D), 0.02),
        "g_norm1": 1.0 + nrm(ks[6], (DEPTH_2, D), 0.05),
        "g_norm2": 1.0 + nrm(ks[7], (DEPTH_2, D), 0.05),
        "w_in": nrm(ks[8], (DEPTH_2, D, PROJ_COLS), D ** -0.5),
        "na_rpb": nrm(ks[9], (DEPTH_2, NA_HEADS, 2 * NA_WIN_R - 1, 2 * NA_WIN_C - 1), 0.1),
        "da_lam_q1": nrm(ks[10], (DEPTH_2, DA_DH), 0.1),
        "da_lam_k1": nrm(ks[11], (DEPTH_2, DA_DH), 0.1),
        "da_lam_q2": nrm(ks[12], (DEPTH_2, DA_DH), 0.1),
        "da_lam_k2": nrm(ks[13], (DEPTH_2, DA_DH), 0.1),
        "da_subln_g": 1.0 + nrm(ks[14], (DEPTH_2, DA_VD), 0.05),
        "gm_ln_g": 1.0 + nrm(ks[15], (DEPTH_2, BRANCH_W_2), 0.05),
        "gm_ln_b": nrm(ks[16], (DEPTH_2, BRANCH_W_2), 0.02),
        "gm_w_s": nrm(ks[17], (DEPTH_2, GM_GROUPS, GM_CHUNK, GM_CHUNK), GM_CHUNK ** -0.5),
        "gm_b_s": 1.0 + nrm(ks[18], (DEPTH_2, GM_GROUPS, GM_CHUNK), 0.1),
        "w_branch": nrm(ks[19], (DEPTH_2, N_BRANCH_2, BRANCH_W_2, D), BRANCH_W_2 ** -0.5),
        "w_out": nrm(ks[20], (DEPTH_2, D, D), D ** -0.5),
        "w_router": nrm(ks[21], (DEPTH_2, D, N_EXPERTS), D ** -0.5),
        "w_e1": nrm(ks[22], (DEPTH_2, N_EXPERTS, D, EXPERT_FF), D ** -0.5),
        "w_e3": nrm(ks[23], (DEPTH_2, N_EXPERTS, D, EXPERT_FF), D ** -0.5),
        "w_e2": nrm(ks[24], (DEPTH_2, N_EXPERTS, EXPERT_FF, D), EXPERT_FF ** -0.5),
        "g_final": 1.0 + nrm(ks[25], (D,), 0.05),
    }

def second_block(x, c, ctx, c_ctx, w_ada, b_ada, g_norm1, g_norm2, w_in, na_rpb,
              da_lam_q1, da_lam_k1, da_lam_q2, da_lam_k2, da_subln_g,
              gm_ln_g, gm_ln_b, gm_w_s, gm_b_s, w_branch, w_out,
              w_router, w_e1, w_e3, w_e2, g_final):
    L = x.shape[1]
    tabs = rope_tables(L)
    xc = ctx
    for i in range(DEPTH_2):
        last = i == DEPTH_2 - 1
        mod = jax.nn.silu(c) @ w_ada[i] + b_ada[i]
        sh1, sc1, gt1, sh2, sc2, gt2 = jnp.split(mod[:, None, :], N_MOD, axis=-1)
        modc = jax.nn.silu(c_ctx) @ w_ada[i] + b_ada[i]
        sh1c, sc1c, gt1c, sh2c, sc2c, gt2c = jnp.split(modc, N_MOD, axis=-1)
        lam_init = 0.8 - 0.6 * math.exp(-0.3 * i)
        lam = (jnp.exp(jnp.sum(da_lam_q1[i].astype(jnp.float32) * da_lam_k1[i].astype(jnp.float32)))
               - jnp.exp(jnp.sum(da_lam_q2[i].astype(jnp.float32) * da_lam_k2[i].astype(jnp.float32)))
               + lam_init)

        h = modulate(rmsnorm(x, g_norm1[i]), sh1, sc1)
        hc = modulate(rmsnorm(xc, g_norm1[i]), sh1c, sc1c)
        ka, va, kb, vb, qa, qb, u, v, gates = _split(h @ w_in[i], KV_SIZES + Q_SIZES)
        if last:
            kac, vac, kbc, vbc = _split(hc @ w_in[i][:, :KV_COLS], KV_SIZES)
        else:
            kac, vac, kbc, vbc, qac, qbc, uc, vcc, gatesc = _split(hc @ w_in[i], KV_SIZES + Q_SIZES)

        ya = neighbourhood_attn(_na_heads(qa), _na_heads(ka), _na_heads(va),
                                _na_heads(kac), _na_heads(vac), na_rpb[i])
        kb_all = jnp.concatenate([_da_qk(kbc), rope_2d(_da_qk(kb), tabs)], axis=1)
        vb_all = jnp.concatenate([_da_v(vbc), _da_v(vb)], axis=1)
        yb = diff_head_norm(diff_attn_blocks(rope_2d(_da_qk(qb), tabs), kb_all, vb_all, lam),
                            da_subln_g[i], lam_init)
        yc = gmlp_gate(jax.nn.gelu(u), jax.nn.gelu(v), gm_ln_g[i], gm_ln_b[i], gm_w_s[i], gm_b_s[i])
        x = x + gt1 * branch_merge(ya, yb, yc, gates, w_branch[i], w_out[i])
        if not last:
            yac = dense_attn(_na_heads(qac), _na_heads(kac), _na_heads(vac))
            ybc = diff_head_norm(diff_attend(_da_qk(qbc), _da_qk(kbc), _da_v(vbc), lam),
                                 da_subln_g[i], lam_init)
            ycc = gmlp_gate(jax.nn.gelu(uc), jax.nn.gelu(vcc), gm_ln_g[i], gm_ln_b[i], gm_w_s[i], gm_b_s[i])
            xc = xc + gt1c * branch_merge(yac, ybc, ycc, gatesc, w_branch[i], w_out[i])

        h2 = modulate(rmsnorm(x, g_norm2[i]), sh2, sc2)
        x = x + gt2 * ec_moe(h2, w_router[i], w_e1[i], w_e3[i], w_e2[i])
        if not last:
            h2c = modulate(rmsnorm(xc, g_norm2[i]), sh2c, sc2c)
            xc = xc + gt2c * ec_moe(h2c, w_router[i], w_e1[i], w_e3[i], w_e2[i])
    return rmsnorm(x, g_final)


def setup_inputs(seed=0):
    out = dict(first_inputs(seed))
    for name, value in second_inputs(seed + 1).items():
        if name != "x":
            out[name + "_2"] = value
    return out


def reference(
    x, mem, attn_norm_g, mem_norm_g, w_in, b_forget, fox_q_norm_g, fox_k_norm_g, lru_conv_w,
    lru_conv_b, lru_w_a, lru_b_a, lru_w_x, lru_b_x, lru_lambda, w_mem_kv, mem_q_norm_g,
    mem_k_norm_g, b_gate, w_branch, w_out, ffn_norm_g, w_up, ffn_conv_w, ffn_conv_b, w_down,
    c_2, ctx_2, c_ctx_2, w_ada_2, b_ada_2, g_norm1_2, g_norm2_2, w_in_2, na_rpb_2, da_lam_q1_2,
    da_lam_k1_2, da_lam_q2_2, da_lam_k2_2, da_subln_g_2, gm_ln_g_2, gm_ln_b_2, gm_w_s_2,
    gm_b_s_2, w_branch_2, w_out_2, w_router_2, w_e1_2, w_e3_2, w_e2_2, g_final_2,
):
    x = first_block(
        x, mem, attn_norm_g, mem_norm_g, w_in, b_forget, fox_q_norm_g, fox_k_norm_g, lru_conv_w,
        lru_conv_b, lru_w_a, lru_b_a, lru_w_x, lru_b_x, lru_lambda, w_mem_kv, mem_q_norm_g,
        mem_k_norm_g, b_gate, w_branch, w_out, ffn_norm_g, w_up, ffn_conv_w, ffn_conv_b, w_down,
    )
    return second_block(
        x, c_2, ctx_2, c_ctx_2, w_ada_2, b_ada_2, g_norm1_2, g_norm2_2, w_in_2, na_rpb_2,
        da_lam_q1_2, da_lam_k1_2, da_lam_q2_2, da_lam_k2_2, da_subln_g_2, gm_ln_g_2, gm_ln_b_2,
        gm_w_s_2, gm_b_s_2, w_branch_2, w_out_2, w_router_2, w_e1_2, w_e3_2, w_e2_2, g_final_2,
    )


_drawn_inputs = setup_inputs


def setup_inputs(seed=0):
    import zlib

    import numpy as np

    out = dict(_drawn_inputs(seed))
    spreads = {}
    factors = {'attn_norm_g': 5.416,
     'mem_norm_g': 8.0,
     'fox_q_norm_g': 8.0,
     'fox_k_norm_g': 8.0,
     'lru_conv_b': 4.619,
     'lru_b_a': 21.411,
     'lru_b_x': 8.0,
     'mem_q_norm_g': 8.0,
     'mem_k_norm_g': 8.0,
     'b_gate': 8.0,
     'ffn_norm_g': 4.198,
     'ffn_conv_b': 8.0,
     'g_norm1_2': 3.32,
     'g_norm2_2': 4.277,
     'na_rpb_2': 25.742,
     'da_lam_q1_2': 7.172,
     'da_lam_k1_2': 8.0,
     'da_lam_q2_2': 5.335,
     'da_lam_k2_2': 43.196,
     'da_subln_g_2': 25.078,
     'gm_ln_g_2': 5.86,
     'gm_ln_b_2': 8.0,
     'gm_b_s_2': 3.535}
    for name, (base, spread) in spreads.items():
        noise = np.random.default_rng([zlib.crc32(name.encode()), seed]).standard_normal(out[name].shape)
        drawn = base * np.exp(spread * noise) if base else spread * noise
        out[name] = jnp.asarray(drawn.astype(out[name].dtype))
    for name, factor in factors.items():
        out[name] = (out[name] * factor).astype(out[name].dtype)
    return out
```

```python
from contextlib import ExitStack, contextmanager

import numpy as np

import concourse.bass as bass
from concourse import mybir

F32 = mybir.dt.float32
ACT = mybir.ActivationFunctionType
ALU = mybir.AluOpType
AX = mybir.AxisListType

P = 128
D = 1024
DC = D // P
T = 256
TT = T // P
HD = 64
HEADS = D // HD
FF = 2816
FC = FF // P
LAYERS = 2
BW = 512
BC = BW // P
NA_HEADS = BW // HD
EXPERTS = 16
CAP = 2 * T // EXPERTS
MODC = 6 * DC
GRID = 64
EPS = 1e-6
NEG = -1e30
LRU_C = 8.0

R = 4
WORDS = 4096
CREDIT = 4

CONSTS = {}
_at = 0
for _name, _n in (("ident", P), ("tri", P), ("ones", P), ("swap", P), ("causal", 2 * T),
                  ("sb_add", 2 * T), ("sb_neg", 2 * T), ("cos", T), ("sin", T), ("before", 2 * T),
                  ("slots", CAP), ("head_sum", DC * 16), ("row_sum", 4 * 16)):
    CONSTS[_name] = (_at, _at + _n)
    _at += _n
N_CONST = _at

PAR1 = {}
_at = 0
for _name, _n in (("attn_g", DC), ("mem_g", DC), ("ffn_g", DC), ("fox_q_g", 1), ("fox_k_g", 1),
                  ("mem_q_g", 2), ("mem_k_g", 2), ("conv_w", 4 * DC), ("conv_b", DC), ("b_a", DC),
                  ("b_x", DC), ("lam", DC), ("b_gate", 4 * DC), ("ffn_w", 3 * FC), ("ffn_b", FC),
                  ("b_forget", 1), ("w_forget", DC * 16)):
    PAR1[_name] = (_at, _at + _n)
    _at += _n
N_PAR1 = _at

PAR2 = {}
_at = 0
for _name, _n in (("b_ada", MODC), ("g1", DC), ("g2", DC), ("subln", 1), ("b_s", 4), ("lam_q", 2),
                  ("lam_k", 2), ("w_router", DC * 16), ("g_final", DC), ("c", DC * 2)):
    PAR2[_name] = (_at, _at + _n)
    _at += _n
N_PAR2 = _at
N_PAR = max(N_PAR1, N_PAR2)

STREAM = [("first", 6 + 4 + 6 + 6 + 16 + 2 + 11, [WORDS] * R), ("down", 8, [FC * P] * R)]
for _l in range(LAYERS):
    STREAM += [("ada+proj", 12 + 8, [WORDS] * R), ("merge", 12, [WORDS, BC * 512] * (R // 2)),
               ("out+experts", 2 + 96, [WORDS] * R)]
N_TILES = sum(n for _, n, _ in STREAM)


class Cursor:

    def __init__(self):
        self.t = 0
        self.g = 0
        self.i = None
        self.slots_per = 0
        self.banks_per = 0
        self.rounds = {}
        self.stage = 0

    def base(self, kind):
        return self.rounds.get(kind, 0)

    def add(self, kind, n):
        self.rounds[kind] = self.base(kind) + n

    def slot(self):
        return self.t % R

    def slot_use(self, k=0, unit=1):
        v = unit * (self.t // R + k)
        return v if self.i is None else v + self.i * (unit * self.slots_per)

    def bank(self):
        return self.g % 4

    def bank_use(self, k=0):
        v = self.g // 4 + k
        return v if self.i is None else v + self.i * self.banks_per


def one(i):
    return slice(i, i + 1) if isinstance(i, int) else bass.ds(i, 1)


def span(i, n):
    return slice(i * n, i * n + n) if isinstance(i, int) else bass.ds(i * n, n)


def build(nc, a, out):
    ctx = ExitStack()
    with ctx:
        sb = lambda name, shape: ctx.enter_context(nc.sbuf_tensor(name, shape, F32))
        sem = lambda name: ctx.enter_context(nc.semaphore(name))

        ring = sb("ring", [P, R, WORDS])
        XT = sb("XT", [P, DC, 2 * T])
        HT = sb("HT", [P, DC, 2 * T])
        const = sb("const", [P, N_CONST])
        sel = sb("sel", [16, 16, P])
        head_sel = sb("head_sel", [16, DC, P])
        par = sb("par", [P, N_PAR])
        MOD = sb("MOD", [P, MODC, 2])
        gmod = sb("gmod", [P, DC, 2])
        small = sb("small", [P, 64])
        rowst = sb("rowst", [16, 2 * T])
        WK = sb("WK", [P, 20992])
        ps = ctx.enter_context(nc.psum_tensor("ps", [P, 8, 512], F32))

        def cst(name):
            lo, hi = CONSTS[name]
            return const[:, lo:hi]

        def p1(name, c=0, n=1):
            lo = PAR1[name][0] + c
            return par[:, lo:lo + n]

        def p2(name, c=0, n=1):
            lo = PAR2[name][0] + c
            return par[:, lo:lo + n]

        ident = cst("ident")
        ones = cst("ones")

        def wk(at, *shape):
            n = int(np.prod(shape))
            v = WK[:, at:at + n]
            if len(shape) == 1:
                return v
            names = "abcd"[:len(shape)]
            return v.rearrange(f"p ({' '.join(names)}) -> p {' '.join(names)}",
                               **{x: s for x, s in zip(names[1:], shape[1:])})

        landed = [sem(f"landed{s}") for s in range(R)]
        slot_free = [sem(f"slot_free{s}") for s in range(R)]
        bank_full = [sem(f"bank_full{b}") for b in range(4)]
        bank_free = [sem(f"bank_free{b}") for b in range(4)]
        stage_done = sem("stage_done")
        loads = sem("loads")
        stored = sem("stored")
        act_step = sem("act_step")
        dve_step = sem("dve_step")
        pool_step = sem("pool_step")
        att_staged = sem("att_staged")
        att_v_staged = sem("att_v_staged")
        att_scores = sem("att_scores")
        att_nmax = sem("att_nmax")
        att_exp = sem("att_exp")
        att_probs = sem("att_probs")
        att_turned = sem("att_turned")
        att_copied = sem("att_copied")
        att_y = sem("att_y")
        att_saved = sem("att_saved")
        sb_staged = sem("sb_staged")
        sb_v_staged = sem("sb_v_staged")
        sb_y = sem("sb_y")
        sb_saved = sem("sb_saved")
        sb_z = sem("sb_z")
        sb_abs = sem("sb_abs")
        sb_ln = sem("sb_ln")
        sb_l = sem("sb_l")
        sb_incl = sem("sb_incl")
        sb_logw = sem("sb_logw")
        sb_w = sem("sb_w")
        norm_sq = sem("norm_sq")
        norm_sum = sem("norm_sum")
        norm_var = sem("norm_var")
        norm_sd = sem("norm_sd")
        norm_r = sem("norm_r")
        moe_staged = sem("moe_staged")
        moe_h = sem("moe_h")
        moe_silu = sem("moe_silu")
        moe_hid = sem("moe_hid")
        moe_turned = sem("moe_turned")
        moe_copied = sem("moe_copied")
        moe_y = sem("moe_y")
        moe_saved = [sem(f"moe_saved{h}") for h in range(2)]
        lam_prod = sem("lam_prod")
        lru_xc = sem("lru_xc")
        lru_ri = sem("lru_ri")
        lru_gates = sem("lru_gates")
        lru_a = sem("lru_a")
        lru_om = sem("lru_om")
        lru_root = sem("lru_root")
        fox_z = sem("fox_z")
        fox_e = sem("fox_e")
        fox_cum = sem("fox_cum")
        rope_r = sem("rope_r")
        raw_gates = sem("raw_gates")
        silu_c = sem("silu_c")
        normed = sem("normed")
        ln_var = sem("ln_var")
        ln_sd = sem("ln_sd")
        ln_done = sem("ln_done")
        aff_logits = sem("aff_logits")
        aff_exp = sem("aff_exp")
        affinities = sem("affinities")
        onehot = sem("onehot")
        conv_done = sem("conv_done")
        silu_done = sem("silu_done")
        gate_used = sem("gate_used")
        looped = [att_staged, att_v_staged, att_scores, att_nmax, att_exp, att_probs, att_turned, att_copied,
                  att_y, att_saved, sb_staged, sb_v_staged, sb_y, sb_saved, sb_z, sb_abs, sb_ln, sb_l,
                  sb_incl, sb_logw, sb_w, moe_staged, moe_h, moe_silu, moe_hid, moe_turned, moe_copied,
                  moe_y, *moe_saved]

        class Steps:

            def __init__(self, eng, sem):
                self.eng, self.sem, self.n, self.i, self.per = eng, sem, 0, None, 0

            def __call__(self, ins):
                ins.then_inc(self.sem, 1)
                self.n += 1
                self.eng.wait_ge(self.sem, self.n if self.i is None else self.n + self.i * self.per)

        @contextmanager
        def loop(eng, cur, n, tiles=0, banks=0, steps=None, steps_per=0):
            assert tiles % R == 0 and banks % 4 == 0
            t0, g0 = cur.t, cur.g
            with eng.Fori(0, n) as i:
                cur.i, cur.slots_per, cur.banks_per = i, tiles // R, banks // 4
                if steps:
                    steps.i, steps.per, s0 = i, steps_per, steps.n
                yield i
            assert cur.t - t0 == tiles and cur.g - g0 == banks, (cur.t - t0, cur.g - g0)
            if steps:
                assert steps.n - s0 == steps_per, steps.n - s0
                steps.n += steps_per * (n - 1)
                steps.i = None
            cur.t += tiles * (n - 1)
            cur.g += banks * (n - 1)
            cur.i = None

        def barrier(eng, cur):
            eng.drain().then_inc(stage_done, 1)
            cur.stage += 1
            eng.wait_ge(stage_done, 4 * cur.stage)

        def tile_of(pe, cur):
            pe.wait_ge(landed[cur.slot()], cur.slot_use(1, 16))
            return ring[:, cur.slot(), :]

        def bank_parts(pe, cur, parts, turn=False):
            b = cur.bank()
            if cur.g >= 4:
                pe.wait_ge(bank_free[b], cur.bank_use())
            for rows, at, n, pairs in parts:
                for k, (l, r) in enumerate(pairs):
                    if turn:
                        last = nc.tensor.transpose(ps[0:rows, b, at:at + n], l, r)
                    else:
                        last = nc.tensor.matmul(ps[0:rows, b, at:at + n], l, r,
                                                start=(k == 0), stop=(k == len(pairs) - 1))
            last.then_inc(bank_full[b], 1)
            cur.g += 1

        def read_bank(eng, cur, mine, op, last_of_tile=False):
            b = cur.bank()
            if mine:
                eng.wait_ge(bank_full[b], cur.bank_use(1))
                if last_of_tile:
                    eng.sem_inc(slot_free[cur.slot()], 1)
                op(ps[:, b, :]).then_inc(bank_free[b], 1)
            cur.g += 1
            if last_of_tile:
                cur.t += 1

        def fm_tile(pe, cur, moving, n, kc=DC, cols=512):
            w = tile_of(pe, cur)[:, 0:kc * cols].rearrange("p (k c) -> p k c", k=kc)
            for c in range(cols // P):
                bank_parts(pe, cur, [(P, 0, n, [(w[:, k, c * P:(c + 1) * P], moving(k)) for k in range(kc)])])
            cur.t += 1

        def tm_tile(pe, cur, t0, tt):
            w = tile_of(pe, cur).rearrange("p (k c) -> p k c", k=DC)
            for m in range(tt):
                tok = slice(t0 + m * P, t0 + (m + 1) * P)
                bank_parts(pe, cur, [(P, 0, 512, [(HT[:, k, tok], w[:, k, :]) for k in range(DC)])])
            cur.t += 1

        def copies(eng, who, cur, dst, banks, n, scale=1.0, func=None):
            for j in range(banks):
                def op(bank, j=j):
                    if who == "act":
                        return nc.scalar.activation(dst(j), bank[:, 0:n], func or ACT.Copy, scale=scale)
                    return nc.vector.tensor_scalar(dst(j), bank[:, 0:n], scale, None, ALU.mult)
                mine = who == "act" if func or j % 2 == 0 else who == "dve"
                read_bank(eng, cur, mine, op, last_of_tile=(j == banks - 1))

        def norm_pe(pe, cur, sq, chunks, n, sums, spread):
            pe.wait_ge(norm_sq, cur.base("norm") + 1)
            for c in range(chunks):
                last = nc.tensor.matmul(ps[0:16, 7, 0:n], sums(c), sq[:, c, 0:n], start=(c == 0),
                                        stop=(c == chunks - 1))
            last.then_inc(norm_sum, 1)
            pe.wait_ge(norm_r, cur.base("norm") + 1)
            for s in spread:
                bank_parts(pe, cur, [(P, 0, n, [(s, rowst[:, 0:n])])])
            cur.add("norm", 1)

        def norm_act(act, cur, steps, x, sq, n):
            nc.scalar.activation(sq, x, ACT.Square).then_inc(norm_sq, 1)
            act.wait_ge(norm_var, cur.base("norm") + 1)
            nc.scalar.activation(rowst[:, 0:n], rowst[:, 0:n], ACT.Sqrt).then_inc(norm_sd, 1)
            cur.add("norm", 1)

        def norm_dve(dve, cur, steps, n, width, post, spread, apply):
            dve.wait_ge(norm_sum, cur.base("norm") + 1)
            nc.vector.tensor_scalar(rowst[:, 0:n], ps[0:16, 7, 0:n], 1.0 / width, EPS, ALU.mult, ALU.add)\
                .then_inc(norm_var, 1)
            dve.wait_ge(norm_sd, cur.base("norm") + 1)
            ins = nc.vector.reciprocal(rowst[:, 0:n], rowst[:, 0:n])
            if post != 1.0:
                steps(ins)
                ins = nc.vector.tensor_scalar(rowst[:, 0:n], rowst[:, 0:n], post, None, ALU.mult)
            ins.then_inc(norm_r, 1)
            for j in range(spread):
                read_bank(dve, cur, True, lambda bank, j=j: apply(j, bank))
            cur.add("norm", 1)

        def skip_banks(cur, n):
            cur.g += n

        ATT_T, ATT_PT, ATT_Q, ATT_K, ATT_V = 0, 2048, 4096, 4352, 5376
        ATT_END = 6400
        t_all = wk(ATT_T, 2, 2, 512)
        pt_all = wk(ATT_PT, 2, 4, 256)
        q_st = wk(ATT_Q, 1, 256)
        k_st = wk(ATT_K, 2, 512)
        v_st = wk(ATT_V, 4, 2, 128)
        nmax = small[:, 0:4].rearrange("p (a b) -> p a b", a=2)
        sums_ = small[:, 4:8].rearrange("p (a b) -> p a b", a=2)
        rcp = small[:, 8:12].rearrange("p (a b) -> p a b", a=2)
        nlam = small[:, 12:13]

        def att_chunks(at):
            if at["diff"]:
                return [[0]]
            return [[0, 1]] if at["nk"] == 256 else [[0], [1]]

        def att_rounds(eng, cur, at, body, before=None, after=None, steps=None, per=0):
            n = at["n"]
            if at["loop"]:
                with loop(eng, cur, n - 1, steps=steps, steps_per=per) as i:
                    body(i, True)
            else:
                for r in range(n - 1):
                    body(r, True)
            body(n - 1, False)

        def att_pe(pe, cur, at):
            nk, n = at["nk"], at["n"]
            kc = nk // P
            base, cbase = cur.base("att"), cur.base("att_c")
            chunks = att_chunks(at)

            def scores(r):
                pe.wait_ge(att_staged, CREDIT + base + r + 1)
                pe.wait_ge(att_exp, CREDIT + base + r)
                for a in range(2):
                    for qt in range(2):
                        for j, (l, m) in enumerate(at["qk"](r, a, qt)):
                            last = nc.tensor.matmul(ps[:, 2 * a + qt, 0:nk], l, m, start=(j == 0),
                                                    stop=(j == len(at["qk"](r, a, qt)) - 1))
                last.then_inc(att_scores, 1)

            def rest(r):
                pe.wait_ge(att_probs, CREDIT + base + r + 1)
                for j, heads in enumerate(chunks):
                    pe.wait_ge(att_copied, CREDIT + cbase + r * len(chunks) + j)
                    col = 0
                    for a in heads:
                        for k in range(kc):
                            for qt in range(2):
                                b = 4 + col // 512
                                last = nc.tensor.transpose(ps[:, b, col % 512:col % 512 + P],
                                                           t_all[:, a, qt, k * P:(k + 1) * P], ident)
                                col += P
                    last.then_inc(att_turned, 1)
                pe.wait_ge(att_copied, CREDIT + cbase + (r + 1) * len(chunks))
                pe.wait_ge(att_v_staged, CREDIT + base + r + 1)
                pe.wait_ge(att_saved, CREDIT + base + r)
                for col, pairs in at["pv"](r):
                    for j, (l, m) in enumerate(pairs):
                        last = nc.tensor.matmul(ps[:, 6 + col // 512, col % 512:col % 512 + T], l, m,
                                                start=(j == 0), stop=(j == len(pairs) - 1))
                last.then_inc(att_y, 1)

            scores(0)

            def body(r, more):
                if more:
                    scores(r + 1)
                rest(r)
            att_rounds(pe, cur, at, body)
            cur.add("att", n)
            cur.add("att_c", n * len(chunks))

        def att_act(act, cur, steps, at):
            nk, n = at["nk"], at["n"]
            kc = nk // P
            base, cbase = cur.base("att"), cur.base("att_c")
            chunks = att_chunks(at)

            def exps(r):
                act.wait_ge(att_nmax, CREDIT + base + r + 1)
                if not at["bias"]:
                    act.wait_ge(att_turned, CREDIT + cbase + r * len(chunks))
                for a in range(2):
                    for qt in range(2):
                        src = t_all[:, a, qt, 0:nk] if at["bias"] else ps[:, 2 * a + qt, 0:nk]
                        last = nc.scalar.activation(t_all[:, a, qt, 0:nk], src, ACT.Exp,
                                                    bias=nmax[:, a, qt:qt + 1],
                                                    accum_out=sums_[:, a, qt:qt + 1])
                last.then_inc(att_exp, 1)

            def copy(r):
                for j, heads in enumerate(chunks):
                    act.wait_ge(att_turned, CREDIT + cbase + r * len(chunks) + j + 1)
                    act.wait_ge(att_y, CREDIT + base + r)
                    words = len(heads) * kc * T
                    if words == 1024 and kc == 4:
                        dst, src = pt_all[:, heads[0], :, :], ps[:, 4:6, :]
                        dst = dst.rearrange("p (b k) q -> p b (k q)", b=2)
                    elif words == 1024:
                        dst, src = pt_all[:, 0:2, 0:2, :].rearrange("p a k q -> p a (k q)"), ps[:, 4:6, :]
                    else:
                        dst, src = pt_all[:, 0, 0:2, :].rearrange("p k q -> p (k q)"), ps[:, 4, :]
                    nc.scalar.activation(dst, src, ACT.Copy).then_inc(att_copied, 1)

            def save(r):
                act.wait_ge(att_y, CREDIT + base + r + 1)
                dst, src = at["save"](r)
                nc.scalar.activation(dst, src, ACT.Copy).then_inc(att_saved, 1)

            exps(0)

            def body(r, more):
                copy(r)
                if more:
                    exps(r + 1)
                save(r)
            att_rounds(act, cur, at, body)
            cur.add("att", n)
            cur.add("att_c", n * len(chunks))

        def att_dve(dve, cur, steps, at):
            nk, n = at["nk"], at["n"]
            base, cbase = cur.base("att"), cur.base("att_c")
            nch = len(att_chunks(at))
            s4 = ps[:, 0:4, :].rearrange("p (a b) k -> p a b k", a=2)

            def maxima(r):
                dve.wait_ge(att_scores, CREDIT + base + r + 1)
                dve.wait_ge(att_exp, CREDIT + base + r)
                src = s4[:, :, :, 0:nk]
                if at["bias"]:
                    dve.wait_ge(att_turned, CREDIT + cbase + r * nch)
                    at["bias"](r, s4, steps)
                    src = t_all[:, :, :, 0:nk]
                nc.vector.tensor_reduce(nmax, src, AX.X, ALU.max, negate=True).then_inc(att_nmax, 1)

            def probs(r):
                dve.wait_ge(att_exp, CREDIT + base + r + 1)
                steps(nc.vector.reciprocal(rcp, sums_))
                if at["diff"]:
                    steps(nc.vector.tensor_scalar(rcp[:, 1, :], rcp[:, 1, :], nlam, None, ALU.mult))
                t = t_all[:, :, :, 0:nk]
                ins = nc.vector.tensor_tensor(t, t, rcp.unsqueeze(3).to_broadcast([P, 2, 2, nk]), ALU.mult)
                if at["diff"]:
                    steps(ins)
                    ins = nc.vector.tensor_tensor(t[:, 0], t[:, 0], t[:, 1], ALU.add)
                ins.then_inc(att_probs, 1)

            def body(r, more):
                maxima(r)
                probs(r)
            att_rounds(dve, cur, at, body, steps=steps,
                       per=at["bias_steps"] + (3 if at["diff"] else 1))
            cur.add("att", n)
            cur.add("att_c", n * nch)

        def att_pool(pool, cur, steps, at):
            n = at["n"]
            base = cur.base("att")
            if at["stage"]:
                steps(nc.gpsimd.memset(k_st, 0.0))
                steps(nc.gpsimd.memset(v_st, 0.0))

            def body(r, more):
                if at["stage"]:
                    pool.wait_ge(att_scores, CREDIT + base + r)
                    at["stage"](r, steps)
                    pool.sem_inc(att_staged, 1)
                    pool.wait_ge(att_y, CREDIT + base + r)
                    at["stage_v"](r).then_inc(att_v_staged, 1)
            if at["stage"]:
                att_rounds(pool, cur, at, body, steps=steps, per=3)
            else:
                pool.sem_inc(att_staged, n)
                pool.sem_inc(att_v_staged, n)
            cur.add("att", n)
            cur.add("att_c", n * len(att_chunks(at)))

        def pair_att(n, nk, q, q0, k, k0, v, v0, y, y0, bias=None, bias_steps=0, diff=False, width=None):
            kc = nk // P

            def stage(r, steps):
                steps(nc.gpsimd.tensor_copy(q_st, q[:, one(r), q0:q0 + T]))
                for a in range(2):
                    h = slice(64 * a, 64 * a + 64)
                    steps(nc.gpsimd.tensor_copy(k_st[h, a:a + 1, 0:nk], k[h, one(r), k0:k0 + nk]))

            def stage_v(r):
                if diff:
                    return nc.gpsimd.tensor_copy(v_st[:, 0:kc, 0, :], v[:, v0:v0 + kc, span(r, P)])
                for a in range(2):
                    ins = nc.gpsimd.tensor_copy(v_st[:, 0:kc, a, 64 * a:64 * a + 64],
                                                v[:, v0:v0 + kc, at_half(r, a)])
                return ins

            def at_half(r, a):
                return slice(r * P + 64 * a, r * P + 64 * a + 64) if isinstance(r, int) else bass.ds(r * P + 64 * a, 64)

            def qk(r, a, qt):
                return [(q_st[:, 0, qt * P:(qt + 1) * P], k_st[:, a, 0:nk])]

            def pv(r):
                if diff:
                    return [(0, [(v_st[:, k_, 0, :], pt_of(0, k_)) for k_ in range(kc)])]
                return [(0, [(v_st[:, k_, a, :], pt_of(a, k_)) for a in range(2) for k_ in range(kc)])]

            def pt_of(a, k_):
                return pt_all[:, a, k_, :]

            def save(r):
                return y[:, one(r), y0:y0 + T], ps[:, 6:7, 0:T]

            return dict(n=n, nk=nk, loop=True, diff=diff, bias=bias, bias_steps=bias_steps, qk=qk, pv=pv,
                        save=save, stage=stage, stage_v=stage_v)

        YT = wk(6400 + 6144, 4, DC, T)
        QT, KT, VT = wk(6400, DC, T), wk(6400 + 2048, DC, T), wk(6400 + 4096, TT, D)
        CUM = wk(6400 + 6144 + 4096, 16, T)
        Q2, K2, V2 = wk(6400, BC, 2 * T), wk(6400 + 2048, BC, 2 * T), wk(6400 + 4096, 4, BW)
        Y2 = wk(6400 + 6144, 3, BC, 2 * T)
        NAB = wk(6400 + 6144 + 2048, 4, 2, 2, T)
        MIXT = wk(0, DC, 2 * T)
        GATE = wk(4096, 4, 2 * T)

        XIN_TM = wk(0, 4, D)

        def turn_in_pe(pe, cur, tiles, col0):
            for c in range(DC):
                bank_parts(pe, cur, [(P, m * P, P, [(XIN_TM[:, tt, c * P:(c + 1) * P], ident)])
                                     for m, tt in enumerate(tiles)], turn=True)

        def turn_in_read(eng, who, cur, tiles, col0):
            n = len(tiles) * P
            for c in range(DC):
                def op(bank, c=c):
                    dst = XT[:, c, col0:col0 + n]
                    if who == "act":
                        return nc.scalar.activation(dst, bank[:, 0:n], ACT.Copy)
                    return nc.vector.tensor_copy(dst, bank[:, 0:n])
                read_bank(eng, cur, (who == "act") == (c % 2 == 0), op)

        def main_norm_pe(pe, cur, n):
            norm_pe(pe, cur, HT, DC, n, lambda c: cst("row_sum")[:, 0:16], [sel[:, 0, :]])

        def main_norm_act(act, cur, steps, n, shift=None):
            norm_act(act, cur, steps, XT[:, :, 0:n], HT[:, :, 0:n], n)
            skip_banks(cur, 1)
            if shift:
                for st in range(n // T):
                    for c in range(DC):
                        act.wait_ge(normed, cur.base("shift") + 1)
                        h = HT[:, c, st * T:(st + 1) * T]
                        nc.scalar.activation(h, h, ACT.Identity, bias=shift(c, st))
                        cur.add("shift", 1)

        def main_norm_dve(dve, cur, steps, n, gain, signal=False):
            def apply(_, bank):
                for st in range(n // T):
                    for c in range(DC):
                        tok = slice(st * T, (st + 1) * T)
                        ins = nc.vector.scalar_tensor_tensor(HT[:, c, tok], XT[:, c, tok], gain(c, st),
                                                             bank[:, tok], ALU.mult, ALU.mult)
                        if signal:
                            ins.then_inc(normed, 1)
                            cur.add("shift", 1)
                if signal:
                    return nc.vector.memset(small[0:1, 60:61], 0.0)
                return ins
            norm_dve(dve, cur, steps, n, D, 1.0, 1, apply)

        def head_norm(x, sq, chunks, n, width, gain, sums, spread, post=1.0, n0=0):
            return dict(x=x, sq=sq, chunks=chunks, n=n, width=width, gain=gain, sums=sums,
                        spread=spread, post=post, n0=n0)

        def head_norm_pe(pe, cur, h):
            norm_pe(pe, cur, h["sq"], h["chunks"], h["n"], h["sums"], [h["spread"](c) for c in range(h["chunks"])])

        def head_norm_act(act, cur, steps, h):
            s = slice(h["n0"], h["n0"] + h["n"])
            norm_act(act, cur, steps, h["x"][:, 0:h["chunks"], s], h["sq"][:, 0:h["chunks"], 0:h["n"]], h["n"])
            skip_banks(cur, h["chunks"])

        def head_norm_dve(dve, cur, steps, h):
            def apply(c, bank):
                x = h["x"][:, c, h["n0"]:h["n0"] + h["n"]]
                return nc.vector.scalar_tensor_tensor(x, x, h["gain"](c), bank[:, 0:h["n"]], ALU.mult, ALU.mult)
            norm_dve(dve, cur, steps, h["n"], h["width"], h["post"], h["chunks"], apply)

        SQ = wk(0, DC, T)
        row_sum = lambda j: cst("row_sum")[:, 16 * j:16 * j + 16]
        fox_sum = lambda c: cst("head_sum")[:, 16 * c:16 * c + 16]
        fox_q_norm = head_norm(QT, SQ, DC, T, HD, lambda c: p1("fox_q_g"), fox_sum, lambda c: head_sel[:, c, :],
                               post=HD ** -0.5)
        fox_k_norm = head_norm(KT, SQ, DC, T, HD, lambda c: p1("fox_k_g"), fox_sum, lambda c: head_sel[:, c, :])
        mem_q_norm = head_norm(QT, SQ, DC, T, 256, lambda c: p1("mem_q_g", c % 2), lambda c: row_sum(c // 2),
                               lambda c: sel[:, c // 2, :], post=256 ** -0.5)
        mem_k_norm = head_norm(KT, SQ, DC, T, 256, lambda c: p1("mem_k_g", c % 2), lambda c: row_sum(c // 2),
                               lambda c: sel[:, c // 2, :])

        def qkv_pe(pe, cur, kq=0, kk=0, kv=0):
            for _ in range(2):
                fm_tile(pe, cur, lambda k: HT[:, k, kq:kq + T], T)
            for _ in range(2):
                fm_tile(pe, cur, lambda k: HT[:, k, kk:kk + T], T)
            for _ in range(2):
                tm_tile(pe, cur, kv, TT)

        def qkv_read(eng, who, cur, q_scale=1.0):
            for dst, scale in ((QT, q_scale), (KT, 1.0)):
                for h in range(2):
                    copies(eng, who, cur, lambda j, h=h, dst=dst: dst[:, 4 * h + j, :], 4, T, scale)
            for h in range(2):
                copies(eng, who, cur, lambda j, h=h: VT[:, j, h * 512:(h + 1) * 512], TT, 512)

        FG = wk(ATT_T, 4, T)

        def forget_pe(pe, cur):
            wf = p1("w_forget", 0, DC * 16).rearrange("p (k h) -> p k h", k=DC)
            bank_parts(pe, cur, [(16, 0, T, [(wf[:, k, :], HT[:, k, 0:T]) for k in range(DC)])])

        def forget_act(act, cur, steps):
            skip_banks(cur, 1)
            act.wait_ge(fox_z, 1)
            steps(nc.scalar.activation(FG[0:16, 1, :], FG[0:16, 0, :], ACT.Abs))
            steps(nc.scalar.activation(FG[0:16, 1, :], FG[0:16, 1, :], ACT.Exp, scale=-1.0))
            nc.scalar.activation(FG[0:16, 1, :], FG[0:16, 1, :], ACT.Ln, bias=1.0).then_inc(fox_e, 1)

        def forget_dve(dve, cur, steps):
            read_bank(dve, cur, True, lambda bank: nc.vector.tensor_scalar(
                FG[0:16, 0, :], bank[0:16, 0:T], p1("b_forget")[0:16], None, ALU.add))
            steps(nc.vector.memset(FG[0:16, 3, :], 1.0))
            dve.wait_ge(bank_free[(cur.g - 1) % 4], (cur.g - 1) // 4 + 1)
            dve.drain().then_inc(fox_z, 1)
            dve.wait_ge(fox_e, 1)
            steps(nc.vector.scalar_tensor_tensor(FG[0:16, 2, :], FG[0:16, 0, :], 0.0, FG[0:16, 1, :],
                                                 ALU.min, ALU.subtract))
            nc.vector.tensor_tensor_scan(FG[0:16, 0, :], FG[0:16, 3, :], FG[0:16, 2, :], 0.0, ALU.mult, ALU.add)\
                .then_inc(fox_cum, 1)

        def forget_pool(pool, cur):
            pool.wait_ge(fox_cum, 1)
            pool.dma_start(a["cum_scratch"], FG[0:16, 0, :]).then_inc(loads, 16)
            pool.wait_ge(loads, 16 * LOADS["cum_out"])
            src = a["cum_scratch"].rearrange("h t -> (h t)").partition_broadcast(P)
            pool.dma_start(CUM.rearrange("p h t -> p (h t)"), src).then_inc(loads, 16)
            pool.wait_ge(loads, 16 * LOADS["cum_in"])

        def fox_bias(r, s4, steps):
            mask = cst("causal").rearrange("p (a b k) -> p a b k", a=1, b=2).to_broadcast([P, 2, 2, T])
            steps(nc.vector.tensor_tensor(t_all[:, :, :, 0:T], s4[:, :, :, 0:T], mask, ALU.add))
            cum = CUM[:, span(r, 2), :].unsqueeze(2).to_broadcast([P, 2, 2, T])
            t = t_all[:, :, :, 0:T]
            steps(nc.vector.tensor_tensor(t, t, cum, ALU.subtract))

        fox = pair_att(HEADS // 2, T, QT, 0, KT, 0, VT, 0, YT[:, 0], 0, bias=fox_bias, bias_steps=2)

        def mem_qk(r, a_, qt):
            c = 4 * r + 2 * a_
            return [(QT[:, c + j, qt * P:(qt + 1) * P], KT[:, c + j, :]) for j in range(2)]

        def mem_pv(r):
            return [((2 * a_ + d) * T, [(VT[:, k, (4 * r + 2 * a_ + d) * P:(4 * r + 2 * a_ + d + 1) * P],
                                         pt_all[:, a_, k, :]) for k in range(2)])
                    for a_ in range(2) for d in range(2)]

        def mem_save(r):
            return (YT[:, 3, 4 * r:4 * r + 4, :].rearrange("p (b c) t -> p b (c t)", b=2), ps[:, 6:8, :])

        mem_att = dict(n=2, nk=T, loop=False, diff=False, bias=None, bias_steps=0, qk=mem_qk, pv=mem_pv,
                       save=mem_save, stage=None, stage_v=None)

        SB_Z, SB_L, SB_LN = wk(0, 2, 2, T), wk(1024, 2, 2, T), wk(2048, 2, 2, T)
        SB_W, sb_q, sb_k = wk(3072, 2, 2, T), wk(4096, 2, T), wk(4608, 1, T)
        sb_v = wk(5376, 2, 2, P)
        z_ps = ps[:, 0:2, :].rearrange("p a (k t) -> p a k t", k=2)
        incl_ps = ps[:, 2:4, :].rearrange("p a (k t) -> p a k t", k=2)

        def sb_pe(pe, cur):
            def scores(r):
                pe.wait_ge(sb_staged, CREDIT + r + 1)
                pe.wait_ge(sb_l, CREDIT + r)
                for a_ in range(2):
                    for kt in range(2):
                        last = nc.tensor.matmul(z_ps[:, a_, kt, :], sb_k[:, 0, kt * P:(kt + 1) * P], sb_q[:, a_, :],
                                                start=True, stop=True)
                last.then_inc(sb_z, 1)

            def rest(r):
                pe.wait_ge(sb_l, CREDIT + r + 1)
                pe.wait_ge(sb_logw, CREDIT + r)
                for a_ in range(2):
                    nc.tensor.matmul(incl_ps[:, a_, 0, :], cst("tri"), SB_L[:, a_, 0, :], start=True, stop=False)
                    nc.tensor.matmul(incl_ps[:, a_, 0, :], ones, SB_L[:, a_, 1, :], start=False, stop=True)
                    last = nc.tensor.matmul(incl_ps[:, a_, 1, :], cst("tri"), SB_L[:, a_, 1, :], start=True, stop=True)
                last.then_inc(sb_incl, 1)
                pe.wait_ge(sb_w, CREDIT + r + 1)
                pe.wait_ge(sb_v_staged, CREDIT + r + 1)
                pe.wait_ge(sb_saved, CREDIT + r)
                for j in range(4):
                    last = nc.tensor.matmul(ps[:, 6, 0:T], sb_v[:, j % 2, j // 2, :], SB_W[:, j // 2, j % 2, :],
                                            start=(j == 0), stop=(j == 3))
                last.then_inc(sb_y, 1)

            scores(0)

            def body(r, more):
                if more:
                    scores(r + 1)
                rest(r)
            att_rounds(pe, cur, SB, body)

        def sb_act(act, cur, steps):
            def body(r, more):
                act.wait_ge(sb_z, CREDIT + r + 1)
                act.wait_ge(sb_l, CREDIT + r)
                nc.scalar.activation(SB_LN, z_ps, ACT.Abs).then_inc(sb_abs, 1)
                act.wait_ge(sb_abs, CREDIT + r + 1)
                steps(nc.scalar.activation(SB_LN, SB_LN, ACT.Exp, scale=-1.0))
                nc.scalar.activation(SB_LN, SB_LN, ACT.Ln, bias=1.0).then_inc(sb_ln, 1)
                act.wait_ge(sb_logw, CREDIT + r + 1)
                act.wait_ge(sb_y, CREDIT + r)
                nc.scalar.activation(SB_W, SB_Z, ACT.Exp).then_inc(sb_w, 1)
                act.wait_ge(sb_y, CREDIT + r + 1)
                nc.scalar.activation(YT[:, 2, one(r), :], ps[:, 6:7, 0:T], ACT.Copy).then_inc(sb_saved, 1)
            att_rounds(act, cur, SB, body, steps=steps, per=1)

        def sb_dve(dve, cur, steps):
            add = cst("sb_add").rearrange("p (a k t) -> p a k t", a=1, k=2).to_broadcast([P, 2, 2, T])
            neg = cst("sb_neg").rearrange("p (a k t) -> p a k t", a=1, k=2).to_broadcast([P, 2, 2, T])

            def body(r, more):
                dve.wait_ge(sb_z, CREDIT + r + 1)
                dve.wait_ge(sb_w, CREDIT + r)
                dve.wait_ge(sb_abs, CREDIT + r + 1)
                steps(nc.vector.tensor_tensor(SB_Z, z_ps, add, ALU.add))
                dve.wait_ge(sb_ln, CREDIT + r + 1)
                dve.wait_ge(sb_incl, CREDIT + r)
                flat = lambda x: x.rearrange("p a k t -> p (a k t)")
                steps(nc.vector.scalar_tensor_tensor(flat(SB_L), flat(z_ps), 0.0, flat(SB_LN), ALU.max, ALU.add))
                nc.vector.tensor_tensor(SB_L, SB_L, neg, ALU.mult).then_inc(sb_l, 1)
                dve.wait_ge(sb_incl, CREDIT + r + 1)
                nc.vector.tensor_tensor(SB_Z, SB_Z, incl_ps, ALU.add).then_inc(sb_logw, 1)
            att_rounds(dve, cur, SB, body, steps=steps, per=2)

        def sb_pool(pool, cur, steps):
            steps(nc.gpsimd.memset(sb_q, 0.0))
            steps(nc.gpsimd.memset(sb_v, 0.0))

            def body(r, more):
                pool.wait_ge(sb_z, CREDIT + r)
                steps(nc.gpsimd.tensor_copy(sb_k, KT[:, one(r), :]))
                for a_ in range(2):
                    h = slice(64 * a_, 64 * a_ + 64)
                    steps(nc.gpsimd.tensor_copy(sb_q[h, a_:a_ + 1, :], QT[h, one(r), :]))
                pool.sem_inc(sb_staged, 1)
                pool.wait_ge(sb_y, CREDIT + r)
                for a_ in range(2):
                    lo = slice(r * P + 64 * a_, r * P + 64 * a_ + 64) if isinstance(r, int) else bass.ds(r * P + 64 * a_, 64)
                    last = nc.gpsimd.tensor_copy(sb_v[:, :, a_, 64 * a_:64 * a_ + 64], VT[:, :, lo])
                last.then_inc(sb_v_staged, 1)
            att_rounds(pool, cur, SB, body, steps=steps, per=3)

        SB = dict(n=HEADS // 2, loop=True)

        LX, LG, LXC, LR, LI, LA = (wk(2048 * j, DC, T) for j in range(6))
        LW = wk(18688, 2, DC, P)
        LY = YT[:, 1]
        sp8 = small[:, 16:24]

        def lru_pe(pe, cur):
            pe.wait_ge(loads, 16 * LOADS["lru_w"])
            for c in range(DC):
                pe.wait_ge(lru_xc, c + 1)
                bank_parts(pe, cur, [(P, g * T, T, [(LW[:, g, c, :], LXC[:, c, :])]) for g in range(2)])

        def lru_act(act, cur, steps):
            tmp = small[:, 24:32]
            steps(nc.scalar.activation(tmp, p1("lam", 0, DC), ACT.Abs))
            steps(nc.scalar.activation(tmp, tmp, ACT.Exp, scale=-1.0))
            nc.scalar.activation(tmp, tmp, ACT.Ln, bias=1.0).then_inc(lru_ri, 1)
            for c in range(DC):
                def op(bank, c=c):
                    nc.scalar.activation(LR[:, c, :], bank[:, 0:T], ACT.Sigmoid, bias=p1("b_a", c))
                    return nc.scalar.activation(LI[:, c, :], bank[:, T:2 * T], ACT.Sigmoid, bias=p1("b_x", c))
                read_bank(act, cur, True, op)
            act.drain().then_inc(lru_gates, 1)
            act.wait_ge(lru_om, 1)
            nc.scalar.activation(LA[:, :, :], LR[:, :, :], ACT.Exp).then_inc(lru_a, 1)
            steps(nc.scalar.activation(LR[:, :, :], LR[:, :, :], ACT.Tanh, scale=-1.0))
            act.drain().then_inc(lru_a, 1)
            act.wait_ge(lru_om, 2)
            nc.scalar.activation(LR[:, :, :], LR[:, :, :], ACT.Sqrt).then_inc(lru_root, 1)

        def lru_dve(dve, cur, steps):
            nlm = small[:, 32:40]
            steps(nc.vector.tensor_scalar(nlm, p1("lam", 0, DC), -1.0, 0.0, ALU.mult, ALU.max))
            dve.wait_ge(lru_ri, 1)
            steps(nc.vector.tensor_tensor(sp8, nlm, small[:, 24:32], ALU.add))
            steps(nc.vector.tensor_scalar(sp8, sp8, -LRU_C, None, ALU.mult))
            for c in range(DC):
                steps(nc.vector.tensor_scalar(LXC[:, c, :], LX[:, c, :], p1("conv_w", 3 * DC + c),
                                              p1("conv_b", c), ALU.mult, ALU.add))
                for j in range(1, 4):
                    ins = nc.vector.scalar_tensor_tensor(
                        LXC[:, c, j:T], LX[:, c, 0:T - j], p1("conv_w", (3 - j) * DC + c), LXC[:, c, j:T],
                        ALU.mult, ALU.add)
                    if j < 3:
                        steps(ins)
                ins.then_inc(lru_xc, 1)
            skip_banks(cur, DC)
            dve.wait_ge(lru_gates, 1)
            for c in range(DC):
                ins = nc.vector.tensor_scalar(LR[:, c, :], LR[:, c, :], sp8[:, c:c + 1], None, ALU.mult)
            ins.then_inc(lru_om, 1)
            dve.wait_ge(lru_xc, DC)
            steps(nc.vector.tensor_tensor(LI[:, :, :], LI[:, :, :], LXC[:, :, :], ALU.mult))
            dve.wait_ge(lru_a, 2)
            steps(nc.vector.tensor_tensor(LXC[:, :, :], LA[:, :, :], LA[:, :, :], ALU.mult))
            flat = lambda x: x.rearrange("p a t -> p (a t)")
            nc.vector.scalar_tensor_tensor(flat(LR), flat(LXC), 1.0, flat(LR), ALU.add, ALU.mult)\
                .then_inc(lru_om, 1)
            dve.wait_ge(lru_root, 1)
            steps(nc.vector.tensor_tensor(LI[:, :, :], LI[:, :, :], LR[:, :, :], ALU.mult))
            for c in range(DC):
                ins = nc.vector.tensor_tensor_scan(LXC[:, c, :], LA[:, c, :], LI[:, c, :], 0.0, ALU.mult, ALU.add)
            steps(ins)
            steps(nc.vector.tensor_tensor(LY, LXC[:, :, :], LG[:, :, :], ALU.mult))

        def merge_pe(pe, cur, branches, kc, n, y, q0=0):
            with loop(pe, cur, branches, tiles=4, banks=16) as i:
                for h in range(2):
                    fm_tile(pe, cur, lambda k: HT[:, k, 0:n], n)
                    fm_tile(pe, cur, lambda k: y[:, one(i), k, 0:n].squeeze(1), n, kc)

        def merge_act(act, cur, branches, n, bias):
            with loop(act, cur, branches, tiles=4, banks=16) as i:
                for h in range(2):
                    for j in range(4):
                        def op(bank, j=j):
                            b = {} if bias is None else {"bias": bias(i, 4 * h + j)}
                            return nc.scalar.activation(GATE[:, j, 0:n], bank[:, 0:n], ACT.Sigmoid, **b)
                        if j == 0:
                            act.wait_ge(gate_used, cur.base("merge") + 1 + h + i * 2)
                        read_bank(act, cur, True, op, last_of_tile=(j == 3))
                    skip_banks(cur, 4)
                    cur.t += 1
            cur.add("merge", 2 * branches + 1)

        def merge_dve(dve, cur, steps, branches, n):
            steps(nc.vector.memset(MIXT[:, :, 0:n], 0.0))
            dve.drain().then_inc(gate_used, 1)
            cur.add("merge", 1)
            with loop(dve, cur, branches, tiles=4, banks=16, steps=steps, steps_per=8) as i:
                for h in range(2):
                    dve.wait_ge(bank_free[(cur.g + 3) % 4], cur.bank_use(1))
                    skip_banks(cur, 4)
                    cur.t += 1
                    for j in range(4):
                        def op(bank, j=j):
                            steps(nc.vector.tensor_tensor(GATE[:, j, 0:n], GATE[:, j, 0:n], bank[:, 0:n], ALU.mult))
                            m = MIXT[:, 4 * h + j, 0:n]
                            return nc.vector.tensor_tensor(m, m, GATE[:, j, 0:n], ALU.add)
                        read_bank(dve, cur, True, op, last_of_tile=(j == 3))
                    dve.drain().then_inc(gate_used, 1)
            cur.add("merge", 2 * branches)

        def out_pe(pe, cur, src, n):
            for _ in range(2):
                fm_tile(pe, cur, lambda k: src[:, k, 0:n], n)

        def out_act(act, cur, n):
            skip_banks(cur, 8)
            cur.t += 2

        def out_dve(dve, cur, n, gain=None):
            for h in range(2):
                for j in range(4):
                    c = 4 * h + j
                    def op(bank, c=c):
                        if gain is None:
                            return nc.vector.tensor_tensor(XT[:, c, 0:n], XT[:, c, 0:n], bank[:, 0:n], ALU.add)
                        for st in range(n // T):
                            tok = slice(st * T, (st + 1) * T)
                            ins = nc.vector.scalar_tensor_tensor(XT[:, c, tok], bank[:, tok], gain(c, st),
                                                                 XT[:, c, tok], ALU.mult, ALU.add)
                        return ins
                    read_bank(dve, cur, True, op, last_of_tile=(j == 3))

        FG_RAW = wk(0, 2, T)
        FH = wk(512, FC, T)
        UPS = FC // 2

        def up_pe(pe, cur):
            def tile_(_):
                fm_tile(pe, cur, lambda k: HT[:, k, 0:T], T)
            up_loop(pe, cur, tile_)

        def up_loop(eng, cur, tile_, steps=None, per=0):
            with loop(eng, cur, 2, tiles=4, banks=16, steps=steps, steps_per=4 * per) as i:
                for j in range(4):
                    tile_(i * 4 + j)
            for j in range(8, UPS):
                tile_(j)

        def up_act(act, cur, steps):
            def tile_(n):
                for j in range(2):
                    act.wait_ge(conv_done, 2 * n + j + 1)
                    f = FH[:, one(2 * n + j), :]
                    nc.scalar.activation(f, f, ACT.Silu).then_inc(silu_done, 1)
                skip_banks(cur, 4)
                cur.t += 1
            up_loop(act, cur, tile_)

        def up_dve(dve, cur, steps):
            def par1(name, i):
                lo = PAR1[name][0] + i
                return par[:, lo:lo + 1] if isinstance(lo, int) else par[:, bass.ds(lo, 1)]

            def tile_(n):
                for j in range(2):
                    f = FH[:, one(2 * n + j), :].squeeze(1)
                    def op(bank, j=j):
                        return nc.vector.tensor_copy(FG_RAW[:, j, :], bank[:, 0:T])
                    read_bank(dve, cur, True, op)
                for j in range(2):
                    f = FH[:, one(2 * n + j), :].squeeze(1)
                    if j == 0:
                        dve.drain().then_inc(raw_gates, 1)
                        dve.wait_ge(raw_gates, n + 1)
                    steps(nc.vector.tensor_scalar(f, FG_RAW[:, j, :], par1("ffn_w", 2 * FC + 2 * n + j),
                                                  par1("ffn_b", 2 * n + j), ALU.mult, ALU.add))
                    steps(nc.vector.scalar_tensor_tensor(f[:, 1:T], FG_RAW[:, j, 0:T - 1], par1("ffn_w", FC + 2 * n + j),
                                                         f[:, 1:T], ALU.mult, ALU.add))
                    nc.vector.scalar_tensor_tensor(f[:, 2:T], FG_RAW[:, j, 0:T - 2], par1("ffn_w", 2 * n + j),
                                                   f[:, 2:T], ALU.mult, ALU.add).then_inc(conv_done, 1)
                for j in range(2):
                    f = FH[:, one(2 * n + j), :].squeeze(1)
                    def op(bank, f=f):
                        return nc.vector.tensor_tensor(f, f, bank[:, 0:T], ALU.mult)
                    dve.wait_ge(silu_done, 2 * n + j + 1)
                    read_bank(dve, cur, True, op, last_of_tile=(j == 1))
            up_loop(dve, cur, tile_, steps=steps, per=4)

        def down_pe(pe, cur):
            with loop(pe, cur, 2, tiles=4, banks=4):
                for _ in range(4):
                    fm_tile(pe, cur, lambda k: FH[:, k, :], T, FC, P)

        def down_act(act, cur):
            skip_banks(cur, DC)
            cur.t += DC

        def down_dve(dve, cur):
            with loop(dve, cur, 2, tiles=4, banks=4) as i:
                for j in range(4):
                    def op(bank, j=j):
                        x = XT[:, one(i * 4 + j), 0:T].squeeze(1)
                        return nc.vector.tensor_tensor(x, x, bank[:, 0:T], ALU.add)
                    read_bank(dve, cur, True, op, last_of_tile=True)

        cs = small[:, 40:56].rearrange("p (k s) -> p k s", k=DC)

        def ada_pe(pe, cur):
            pe.wait_ge(silu_c, cur.base("ada") + 1)
            with loop(pe, cur, 3, tiles=4, banks=4):
                for _ in range(4):
                    w = tile_of(pe, cur).rearrange("p (k c) -> p k c", k=DC)
                    bank_parts(pe, cur, [(P, 2 * c, 2, [(w[:, k, c * P:(c + 1) * P], cs[:, k, :]) for k in range(DC)])
                                         for c in range(4)])
                    cur.t += 1
            cur.add("ada", 1)

        def ada_act(act, cur, layer):
            act.wait_ge(loads, 16 * LOADS["par"][layer])
            nc.scalar.activation(cs, p2("c", 0, 2 * DC).rearrange("p (k s) -> p k s", k=DC), ACT.Silu)\
                .then_inc(silu_c, 1)
            skip_banks(cur, 12)
            cur.t += 12

        def ada_dve(dve, cur, steps, layer):
            dve.wait_ge(loads, 16 * LOADS["par"][layer])
            with loop(dve, cur, 3, tiles=4, banks=4) as i:
                for j in range(4):
                    def op(bank, j=j):
                        lo = i * 16 + 4 * j
                        b = par[:, bass.ds(lo + PAR2["b_ada"][0], 4)].unsqueeze(2).to_broadcast([P, 4, 2])
                        return nc.vector.tensor_tensor(MOD[:, bass.ds(lo, 4), :],
                                                       bank[:, 0:8].rearrange("p (c s) -> p c s", c=4), b, ALU.add)
                    read_bank(dve, cur, True, op, last_of_tile=True)

        def gmod_dve(dve, steps, g, which):
            gb = p2(g, 0, DC).unsqueeze(2).to_broadcast([P, DC, 2])
            steps(nc.vector.tensor_scalar(gmod[:, :, :], MOD[:, which * DC:(which + 1) * DC, :], 1.0, None, ALU.add))
            steps(nc.vector.tensor_tensor(gmod[:, :, :], gmod[:, :, :], gb, ALU.mult))

        def proj2_pe(pe, cur, nq):
            fm_tile(pe, cur, lambda k: HT[:, k, 0:nq], nq)
            fm_tile(pe, cur, lambda k: HT[:, k, :], 2 * T)
            tm_tile(pe, cur, 0, 4)

        def proj2_read(eng, who, cur, nq):
            copies(eng, who, cur, lambda j: Q2[:, j, 0:nq], 4, nq, HD ** -0.5)
            copies(eng, who, cur, lambda j: K2[:, j, :], 4, 2 * T)
            copies(eng, who, cur, lambda j: V2[:, j, :], 4, BW)

        def na_bias(r, s4, steps):
            steps(nc.vector.tensor_tensor(t_all[:, :, :, 0:T], s4[:, :, :, 0:T], NAB[:, one(r)].squeeze(1), ALU.add))
            steps(nc.vector.tensor_copy(t_all[:, :, :, T:2 * T], s4[:, :, :, T:2 * T]))

        na_x = pair_att(4, 2 * T, Q2, 0, K2, 0, V2, 0, Y2[:, 0], 0, bias=na_bias, bias_steps=2)
        na_ctx = pair_att(4, T, Q2, T, K2, T, V2, 2, Y2[:, 0], T)
        da_x = pair_att(4, 2 * T, Q2, 0, K2, 0, V2, 0, Y2[:, 1], 0, diff=True)
        da_ctx = pair_att(4, T, Q2, T, K2, T, V2, 2, Y2[:, 1], T, diff=True)

        ROT = wk(0, BC, T)

        def rope_pe(pe, cur):
            for x in (Q2, K2):
                for c in range(BC):
                    bank_parts(pe, cur, [(P, 0, T, [(cst("swap"), x[:, c, 0:T])])])

        def rope_dve(dve, cur, steps):
            for x in (Q2, K2):
                for c in range(BC):
                    def op(bank, c=c):
                        return nc.vector.tensor_tensor(ROT[:, c, :], bank[:, 0:T], cst("sin"), ALU.mult)
                    read_bank(dve, cur, True, op)
                dve.drain().then_inc(rope_r, 1)
                cur.add("rope", 1)
                dve.wait_ge(rope_r, cur.base("rope"))
                cos = cst("cos").unsqueeze(1).to_broadcast([P, BC, T])
                steps(nc.vector.tensor_tensor(x[:, :, 0:T], x[:, :, 0:T], cos, ALU.mult))
                steps(nc.vector.tensor_tensor(x[:, :, 0:T], x[:, :, 0:T], ROT, ALU.add))

        lamp = small[:, 56:58]

        def lam_pe(pe, cur):
            pe.wait_ge(lam_prod, cur.base("lam") * 2 + 1)
            bank_parts(pe, cur, [(P, 0, 2, [(ones, lamp)])])
            cur.add("lam", 1)

        def lam_act(act, cur):
            read_bank(act, cur, True, lambda bank: nc.scalar.activation(small[:, 58:60], bank[:, 0:2], ACT.Exp))

        def lam_dve(dve, cur, steps, lam_init):
            nc.vector.tensor_tensor(lamp, p2("lam_q", 0, 2), p2("lam_k", 0, 2), ALU.mult).then_inc(lam_prod, 1)
            cur.g += 1
            b = (cur.g - 1) % 4
            dve.wait_ge(bank_free[b], (cur.g - 1) // 4 + 1)
            steps(nc.vector.tensor_tensor(nlam, small[:, 59:60], small[:, 58:59], ALU.subtract))
            steps(nc.vector.tensor_scalar(nlam, nlam, -lam_init, None, ALU.add))
            dve.drain().then_inc(lam_prod, 1)

        SQ2 = wk(0, BC, 2 * T)

        def da_norm(n, lam_init):
            return head_norm(Y2[:, 1], SQ2, BC, n, P, lambda c: p2("subln"), lambda c: row_sum(c),
                             lambda c: sel[:, c, :], post=1.0 - lam_init)

        GU, GV = wk(0, 4, BW), wk(2048, 4, BW)
        GWS = wk(6400, 4, P)
        GLN = wk(6400 + 512, 2, BW)
        GST = wk(6400 + 1536, 4, 8)

        def gmlp_proj_pe(pe, cur, tt):
            tm_tile(pe, cur, 0, tt)
            tm_tile(pe, cur, 0, tt)

        def gmlp_proj_read(eng, who, cur, tt):
            copies(eng, who, cur, lambda j: GU[:, j, :], tt, BW, func=ACT.Gelu_apprx_tanh)
            copies(eng, who, cur, lambda j: GV[:, j, :], tt, BW, func=ACT.Gelu_apprx_tanh)

        def gmlp_ln_dve(dve, cur, steps, tt, layer):
            for m in range(tt):
                steps(nc.vector.bn_stats(GST[:, m, 0:6], GV[:, m, :]))
                steps(nc.vector.bn_aggr(GST[:, m, 6:8], GST[:, m, 0:6]))
            var = GST[:, 0:tt, 7:8]
            nc.vector.tensor_scalar(var, var, EPS, None, ALU.add).then_inc(ln_var, 1)
            dve.wait_ge(ln_sd, layer + 1)
            steps(nc.vector.reciprocal(var, var))
            dve.wait_ge(loads, 16 * LOADS["ln"][layer])
            for m in range(tt):
                v = GV[:, m, :]
                steps(nc.vector.tensor_scalar(v, v, GST[:, m, 6:7], GST[:, m, 7:8], ALU.subtract, ALU.mult))
                steps(nc.vector.tensor_tensor(v, v, GLN[:, 0, :], ALU.mult))
                ins = nc.vector.tensor_tensor(v, v, GLN[:, 1, :], ALU.add)
            ins.then_inc(ln_done, 1)

        def gmlp_ln_act(act, tt, layer):
            act.wait_ge(ln_var, layer + 1)
            var = GST[:, 0:tt, 7:8]
            nc.scalar.activation(var, var, ACT.Sqrt).then_inc(ln_sd, 1)

        def gmlp_mix_pe(pe, cur, tt, layer):
            pe.wait_ge(loads, 16 * LOADS["ln"][layer])
            pe.wait_ge(ln_done, layer + 1)
            for m in range(tt):
                bank_parts(pe, cur, [(P, g * P, P, [(GWS[:, g, :], GV[:, m, g * P:(g + 1) * P])]) for g in range(4)])
            for m in range(tt):
                g = cur.g - tt
                pe.wait_ge(bank_free[g % 4], g // 4 + 1)
                bank_parts(pe, cur, [(P, c * P, P, [(GU[:, m, c * P:(c + 1) * P], ident)]) for c in range(BC)], turn=True)

        def gmlp_mix_dve(dve, cur, steps, tt):
            for m in range(tt):
                def op(bank, m=m):
                    for g in range(4):
                        u = GU[:, m, g * P:(g + 1) * P]
                        ins = nc.vector.scalar_tensor_tensor(u, bank[:, g * P:(g + 1) * P], p2("b_s", g), u,
                                                             ALU.add, ALU.mult)
                    return ins
                read_bank(dve, cur, True, op)
            skip_banks(cur, tt)

        def gmlp_mix_act(act, cur, tt):
            skip_banks(cur, tt)
            for m in range(tt):
                read_bank(act, cur, True, lambda bank, m=m: nc.scalar.activation(
                    Y2[:, 2, :, m * P:(m + 1) * P], bank.rearrange("p (c t) -> p c t", c=BC), ACT.Copy))

        XIN = wk(0, DC, 2, EXPERTS * CAP)
        YE = wk(8192, 2, 4, D)
        H2 = wk(8192, 4, D)
        GT = wk(16384, 2, 4, T)
        PH = wk(18432, 4, EXPERTS * CAP)
        AFF = small[:, 0:64].rearrange("p (m e) -> p m e", m=4)
        XS = HT[:, 0:2, :].rearrange("p a (k s) -> p a k s", k=DC)
        SG = HT[:, 2:4, :]
        HID = HT[:, 4:6, :]
        HIDT = HT[:, 6, :].rearrange("p (k s) -> p k s", k=DC)
        CMP, RANKS, AUX = wk(0, 2, 8, T), wk(4096, 2, 4, EXPERTS), wk(4224, 8)
        AFFT = rowst

        def route_pe(pe, cur, st):
            tt = 2 * st
            wr = p2("w_router", 0, DC * 16).rearrange("p (k e) -> p k e", k=DC)
            bank_parts(pe, cur, [(P, m * 16, 16, [(HT[:, k, m * P:(m + 1) * P], wr[:, k, :]) for k in range(DC)])
                                 for m in range(tt)])
            for m in range(tt):
                for h in range(2):
                    bank_parts(pe, cur, [(P, c * P, P, [(HT[:, 4 * h + c, m * P:(m + 1) * P], ident)])
                                         for c in range(4)], turn=True)
            pe.wait_ge(affinities, cur.base("route") + 1)
            bank_parts(pe, cur, [(16, m * P, P, [(AFF[:, m, :], ident)]) for m in range(tt)], turn=True)
            g = cur.g - 1
            pe.wait_ge(bank_free[g % 4], g // 4 + 1)
            for e in range(EXPERTS):
                bank_parts(pe, cur, [(P, 0, st * T, [(sel[:, e, :], AFFT[:, 0:st * T])])])
            pe.wait_ge(onehot, 2 * cur.base("route") + 1)
            for s in range(st):
                for c in range(DC):
                    bank_parts(pe, cur, [(P, 0, 512, [(H2[:, 2 * s + m, c * P:(c + 1) * P], PH[:, 2 * s + m, :])
                                                      for m in range(2)])])
            pe.wait_ge(onehot, 2 * cur.base("route") + 2)
            for s in range(st):
                for half in range(2):
                    bank_parts(pe, cur, [(P, g_ * T + m * P, P, [(PH[:, 2 * s + m, (2 * half + g_) * P:(2 * half + g_ + 1) * P], ident)])
                                         for g_ in range(2) for m in range(2)], turn=True)
            cur.add("route", 1)

        def route_act(act, cur, steps, st):
            tt = 2 * st
            act.wait_ge(aff_logits, cur.base("route") + 1)
            skip_banks(cur, 1)
            nc.scalar.activation(AFF[:, 0:tt, :], AFF[:, 0:tt, :], ACT.Exp).then_inc(aff_exp, 1)
            for m in range(tt):
                for h in range(2):
                    read_bank(act, cur, True, lambda bank, m=m, h=h: nc.scalar.activation(
                        H2[:, m, h * 512:(h + 1) * 512], bank, ACT.Copy))
            read_bank(act, cur, True, lambda bank: nc.scalar.activation(AFFT[:, 0:st * T], bank[0:16, 0:st * T], ACT.Copy))
            skip_banks(cur, EXPERTS)
            for s in range(st):
                for c in range(DC):
                    read_bank(act, cur, c % 2 == 0, lambda bank, s=s, c=c: nc.scalar.activation(XIN[:, c, s, :], bank, ACT.Copy))
            for s in range(st):
                for half in range(2):
                    read_bank(act, cur, True, lambda bank, s=s, half=half: nc.scalar.activation(
                        GT[:, s, 2 * half:2 * half + 2, :], bank.rearrange("p (g t) -> p g t", g=2), ACT.Copy))
            cur.add("route", 1)

        def route_dve(dve, cur, steps, st):
            tt = 2 * st
            aff = AFF[:, 0:tt, :]
            aux = AUX[:, 0:tt]
            wide = lambda x: x.unsqueeze(2).to_broadcast([P, tt, 16])
            g = cur.g
            dve.wait_ge(bank_full[g % 4], g // 4 + 1)
            lg = ps[:, g % 4, 0:16 * tt].rearrange("p (m e) -> p m e", m=tt)
            steps(nc.vector.tensor_reduce(aux, lg, AX.X, ALU.max))
            read_bank(dve, cur, True, lambda bank: nc.vector.tensor_tensor(aff, lg, wide(aux), ALU.subtract))
            dve.drain().then_inc(aff_logits, 1)
            dve.wait_ge(aff_exp, cur.base("route") + 1)
            steps(nc.vector.tensor_reduce(aux, aff, AX.X, ALU.add))
            steps(nc.vector.reciprocal(aux, aux))
            nc.vector.tensor_tensor(aff, aff, wide(aux), ALU.mult).then_inc(affinities, 1)
            dve.wait_ge(affinities, cur.base("route") + 1)
            skip_banks(cur, 2 * tt + 1)
            before = cst("before").rearrange("p (m t) -> p m t", m=2)
            for e in range(EXPERTS):
                if e >= 2:
                    dve.wait_ge(bank_free[(cur.g - 2) % 4], (cur.g - 2) // 4 + 1)

                def op(bank, e=e):
                    for s in range(st):
                        for m in range(2):
                            row, av = bank[:, s * T:(s + 1) * T], AFF[:, 2 * s + m, e:e + 1]
                            nc.vector.tensor_scalar(CMP[:, e % 2, 4 * s + 2 * m, :], row, av, 0.0, ALU.is_gt, ALU.add,
                                                    accum_out=RANKS[:, 0, 2 * s + m, e:e + 1])
                            ins = nc.vector.scalar_tensor_tensor(CMP[:, e % 2, 4 * s + 2 * m + 1, :], row, av, before[:, m, :],
                                                                 ALU.is_equal, ALU.mult,
                                                                 accum_out=RANKS[:, 1, 2 * s + m, e:e + 1])
                    return ins
                read_bank(dve, cur, True, op)
            dve.wait_ge(bank_free[(cur.g - 1) % 4], (cur.g - 1) // 4 + 1)
            steps(nc.vector.tensor_tensor(RANKS[:, 0, 0:tt], RANKS[:, 0, 0:tt], RANKS[:, 1, 0:tt], ALU.add))
            slots = cst("slots").unsqueeze(1).to_broadcast([P, EXPERTS, CAP])
            ph = PH.rearrange("p m (e s) -> p m e s", e=EXPERTS)
            for m in range(tt):
                ins = nc.vector.tensor_tensor(ph[:, m], slots, RANKS[:, 0, m, :].unsqueeze(2).to_broadcast([P, EXPERTS, CAP]),
                                              ALU.is_equal)
            ins.then_inc(onehot, 1)
            for s in range(st):
                for c in range(DC):
                    read_bank(dve, cur, c % 2 == 1, lambda bank, s=s, c=c: nc.vector.tensor_copy(XIN[:, c, s, :], bank))
            for b in range(4):
                last = cur.g - 1 - (cur.g - 1 - b) % 4
                dve.wait_ge(bank_full[b], last // 4 + 1)
            for m in range(tt):
                ins = nc.vector.tensor_tensor(ph[:, m], ph[:, m], AFF[:, m, :].unsqueeze(2).to_broadcast([P, EXPERTS, CAP]),
                                              ALU.mult)
            ins.then_inc(onehot, 1)
            skip_banks(cur, 2 * st)
            cur.add("route", 1)

        HB = [0, 2]
        def experts(eng, cur, one_expert, steps=None, per=0):
            with loop(eng, cur, EXPERTS // 4, tiles=24, steps=steps, steps_per=per) as i:
                for j in range(4):
                    one_expert(i, j, cur.base("moe") + j + i * 4)
            cur.add("moe", EXPERTS)

        def experts_pe(pe, cur, st):
            rows = CAP * st

            def up(xs, bank):
                w = tile_of(pe, cur).rearrange("p (k c) -> p k c", k=DC)
                for k in range(DC):
                    last = nc.tensor.matmul(ps[0:rows, bank, :], xs[:, k, 0:rows], w[:, k, :],
                                            start=(k == 0), stop=(k == DC - 1))
                cur.t += 1
                return last

            def turn(e, h):
                pe.wait_ge(moe_hid, CREDIT + 2 * e + h + 1)
                pe.wait_ge(moe_copied, CREDIT + 2 * e + h - 1)
                for c in range(4):
                    last = nc.tensor.matmul(ps[:, 4 + h, c * rows:(c + 1) * rows],
                                            HID[0:rows, h, c * P:(c + 1) * P], ident[0:rows, 0:rows],
                                            start=True, stop=True)
                last.then_inc(moe_turned, 1)

            def down(e, n, w, ks, last_part):
                if ks[0] == 0:
                    pe.wait_ge(moe_saved[n], CREDIT + e)
                pe.wait_ge(moe_copied, CREDIT + 2 * e + (1 if ks[0] == 0 else 2))
                for k in ks:
                    last = nc.tensor.matmul(ps[0:rows, 6 + n, :], HIDT[:, k, 0:rows], w[:, k, :],
                                            start=(k == 0), stop=(k == DC - 1))
                if last_part:
                    last.then_inc(moe_y, 1)

            def one_expert(i, j, e):
                xs = XS[:, j % 2]
                pe.wait_ge(moe_staged, CREDIT + e + 1)
                for h in range(2):
                    pe.wait_ge(moe_hid, CREDIT + 2 * e + h - 1)
                    up(xs, HB[h])
                    if h == 1:
                        turn(e, 0)
                    up(xs, HB[h] + 1).then_inc(moe_h, 1)
                w = tile_of(pe, cur).rearrange("p (k c) -> p k c", k=DC)
                down(e, 0, w, [0, 1, 2, 3], False)
                turn(e, 1)
                down(e, 0, w, [4, 5, 6, 7], True)
                cur.t += 1
                w = tile_of(pe, cur).rearrange("p (k c) -> p k c", k=DC)
                down(e, 1, w, [0, 1, 2, 3], False)
                down(e, 1, w, [4, 5, 6, 7], True)
                cur.t += 1
            experts(pe, cur, one_expert)

        def experts_act(act, cur, st):
            rows = CAP * st

            def one_expert(i, j, e):
                for h in range(2):
                    act.wait_ge(moe_h, CREDIT + 2 * e + h + 1)
                    for _ in range(2):
                        act.sem_inc(slot_free[cur.slot()], 1)
                        cur.t += 1
                    act.wait_ge(moe_hid, CREDIT + 2 * e + h - 1)
                    nc.scalar.activation(SG[0:rows, h, :], ps[0:rows, HB[h], :], ACT.Silu).then_inc(moe_silu, 1)
                for h in range(2):
                    act.wait_ge(moe_turned, CREDIT + 2 * e + h + 1)
                    act.wait_ge(moe_y, CREDIT + 2 * e)
                    nc.scalar.activation(HIDT[:, 4 * h:4 * h + 4, 0:rows],
                                         ps[:, 4 + h, 0:4 * rows].rearrange("p (c s) -> p c s", c=4), ACT.Copy)\
                        .then_inc(moe_copied, 1)
                cur.t += 1
                act.wait_ge(moe_y, CREDIT + 2 * e + 2)
                act.sem_inc(slot_free[cur.slot()], 1)
                cur.t += 1
                save(nc.scalar.activation, i, j, 1, moe_saved[1], ACT.Copy)

            def save(f, i, j, n, sig, *args):
                for s in range(st):
                    ins = f(YE[CAP * j:CAP * (j + 1), s, one(i), n * 512:(n + 1) * 512],
                            ps[CAP * s:CAP * (s + 1), 6 + n:7 + n, :], *args)
                ins.then_inc(sig, 1)
            experts(act, cur, one_expert)

        def experts_dve(dve, cur, st):
            rows = CAP * st

            def one_expert(i, j, e):
                for h in range(2):
                    dve.wait_ge(moe_silu, CREDIT + 2 * e + h + 1)
                    dve.wait_ge(moe_turned, CREDIT + 2 * e + h - 1)
                    nc.vector.tensor_tensor(HID[0:rows, h, :], SG[0:rows, h, :], ps[0:rows, HB[h] + 1, :], ALU.mult)\
                        .then_inc(moe_hid, 1)
                cur.t += 4
                dve.wait_ge(moe_y, CREDIT + 2 * e + 1)
                dve.sem_inc(slot_free[cur.slot()], 1)
                for s in range(st):
                    ins = nc.vector.tensor_copy(YE[CAP * j:CAP * (j + 1), s, one(i), 0:512],
                                                ps[CAP * s:CAP * (s + 1), 6:7, :])
                ins.then_inc(moe_saved[0], 1)
                cur.t += 2
            experts(dve, cur, one_expert)

        def experts_pool(pool, cur, st):
            def one_expert(i, j, e):
                pool.wait_ge(moe_h, CREDIT + 2 * e - 2)
                for s in range(st):
                    lo = bass.ds(i * (4 * CAP) + j * CAP, CAP)
                    ins = nc.gpsimd.tensor_copy(XS[:, j % 2, :, CAP * s:CAP * (s + 1)], XIN[:, :, s, lo])
                ins.then_inc(moe_staged, 1)
                cur.t += 6
            experts(pool, cur, one_expert)

        def scatter_pe(pe, cur, st):
            for c in range(DC):
                bank_parts(pe, cur, [(P, s * T, T, [(YE[:, s, g, c * P:(c + 1) * P], GT[:, s, g, :]) for g in range(4)])
                                     for s in range(st)])

        def scatter_dve(dve, cur, st):
            for c in range(DC):
                def op(bank, c=c):
                    for s in range(st):
                        tok = slice(s * T, (s + 1) * T)
                        ins = nc.vector.scalar_tensor_tensor(XT[:, c, tok], bank[:, tok], MOD[:, 5 * DC + c, s:s + 1],
                                                             XT[:, c, tok], ALU.mult, ALU.add)
                    return ins
                read_bank(dve, cur, True, op)

        OUT = wk(0, TT, D)

        def turn_out_pe(pe, cur):
            for m in range(TT):
                for h in range(2):
                    bank_parts(pe, cur, [(P, c * P, P, [(HT[:, 4 * h + c, m * P:(m + 1) * P], ident)])
                                         for c in range(4)], turn=True)

        def turn_out_act(act, cur):
            for m in range(TT):
                for h in range(2):
                    read_bank(act, cur, True, lambda bank, m=m, h=h: nc.scalar.activation(
                        OUT[:, m, h * 512:(h + 1) * 512], bank, ACT.Copy))

        LOADS = {"start": 6, "cum_out": 7, "cum_in": 8, "lru_w": 9}
        LOADS["par"] = [11 + 5 * l for l in range(LAYERS)]
        LOADS["nab"] = [LOADS["par"][l] + 1 for l in range(LAYERS)]
        LOADS["ln"] = [LOADS["par"][l] + 4 for l in range(LAYERS)]

        block = ctx.enter_context(nc.Block())
        ended = []

        @block.sync
        def _(sp):
            cur = Cursor()

            def load(t, words):
                sp.dma_start(ring[:, cur.slot(), 0:words], a["stream"][t, :, 0:words])\
                    .then_inc(landed[cur.slot()], 16)

            for n, words in [(n, w) for _, n, w in STREAM]:
                done = 0
                while cur.t < R:
                    load(cur.t, words[0])
                    cur.t += 1
                    done += 1
                t0 = cur.t
                turns = (n - done) // R
                if turns > 1:
                    with loop(sp, cur, turns, tiles=R) as i:
                        for j in range(R):
                            sp.wait_ge(slot_free[cur.slot()], cur.slot_use())
                            sp.dma_start(ring[:, cur.slot(), 0:words[j]],
                                         a["stream"][bass.ds(i * R + (t0 + j), 1), :, 0:words[j]]
                                         .rearrange("a p w -> (a p) w")).then_inc(landed[cur.slot()], 16)
                            cur.t += 1
                    done += turns * R
                for j in range(n - done):
                    sp.wait_ge(slot_free[cur.slot()], cur.slot_use())
                    load(cur.t, words[j % R])
                    cur.t += 1
            assert cur.t == N_TILES

        @block.tensor
        def _(pe):
            cur = Cursor()
            pe.wait_ge(loads, 16 * LOADS["start"])
            turn_in_pe(pe, cur, range(4), 0)
            barrier(pe, cur)
            main_norm_pe(pe, cur, 2 * T)
            barrier(pe, cur)
            qkv_pe(pe, cur)
            forget_pe(pe, cur)
            barrier(pe, cur)
            head_norm_pe(pe, cur, fox_q_norm)
            barrier(pe, cur)
            head_norm_pe(pe, cur, fox_k_norm)
            barrier(pe, cur)
            att_pe(pe, cur, fox)
            barrier(pe, cur)
            for _ in range(4):
                fm_tile(pe, cur, lambda k: HT[:, k, 0:T], T)
            barrier(pe, cur)
            lru_pe(pe, cur)
            barrier(pe, cur)
            qkv_pe(pe, cur)
            barrier(pe, cur)
            sb_pe(pe, cur)
            barrier(pe, cur)
            qkv_pe(pe, cur, 0, T, T)
            barrier(pe, cur)
            head_norm_pe(pe, cur, mem_q_norm)
            barrier(pe, cur)
            head_norm_pe(pe, cur, mem_k_norm)
            barrier(pe, cur)
            att_pe(pe, cur, mem_att)
            barrier(pe, cur)
            merge_pe(pe, cur, 4, DC, T, YT)
            barrier(pe, cur)
            out_pe(pe, cur, MIXT, T)
            barrier(pe, cur)
            main_norm_pe(pe, cur, T)
            barrier(pe, cur)
            up_pe(pe, cur)
            barrier(pe, cur)
            down_pe(pe, cur)
            barrier(pe, cur)
            pe.wait_ge(loads, 16 * LOADS["par"][0])
            turn_in_pe(pe, cur, range(2), T)
            barrier(pe, cur)
            for layer in range(LAYERS):
                n = T if layer == LAYERS - 1 else 2 * T
                ada_pe(pe, cur)
                barrier(pe, cur)
                main_norm_pe(pe, cur, 2 * T)
                barrier(pe, cur)
                proj2_pe(pe, cur, n)
                barrier(pe, cur)
                att_pe(pe, cur, na_x)
                barrier(pe, cur)
                if n > T:
                    att_pe(pe, cur, na_ctx)
                    barrier(pe, cur)
                proj2_pe(pe, cur, n)
                barrier(pe, cur)
                rope_pe(pe, cur)
                lam_pe(pe, cur)
                barrier(pe, cur)
                att_pe(pe, cur, da_x)
                barrier(pe, cur)
                if n > T:
                    att_pe(pe, cur, da_ctx)
                    barrier(pe, cur)
                head_norm_pe(pe, cur, da_norm(n, 0.0))
                barrier(pe, cur)
                gmlp_proj_pe(pe, cur, n // P)
                barrier(pe, cur)
                gmlp_mix_pe(pe, cur, n // P, layer)
                barrier(pe, cur)
                merge_pe(pe, cur, 3, BC, n, Y2)
                barrier(pe, cur)
                out_pe(pe, cur, MIXT, n)
                barrier(pe, cur)
                main_norm_pe(pe, cur, n)
                barrier(pe, cur)
                route_pe(pe, cur, n // T)
                barrier(pe, cur)
                experts_pe(pe, cur, n // T)
                barrier(pe, cur)
                scatter_pe(pe, cur, n // T)
                barrier(pe, cur)
            main_norm_pe(pe, cur, T)
            barrier(pe, cur)
            turn_out_pe(pe, cur)
            barrier(pe, cur)
            ended.append((cur.stage, cur.t, cur.g))

        @block.scalar
        def _(act):
            cur = Cursor()
            steps = Steps(act, act_step)
            turn_in_read(act, "act", cur, range(4), 0)
            barrier(act, cur)
            main_norm_act(act, cur, steps, 2 * T)
            barrier(act, cur)
            qkv_read(act, "act", cur)
            forget_act(act, cur, steps)
            barrier(act, cur)
            head_norm_act(act, cur, steps, fox_q_norm)
            barrier(act, cur)
            head_norm_act(act, cur, steps, fox_k_norm)
            barrier(act, cur)
            att_act(act, cur, steps, fox)
            barrier(act, cur)
            for h in range(2):
                copies(act, "act", cur, lambda j, h=h: LX[:, 4 * h + j, :], 4, T)
            for h in range(2):
                copies(act, "act", cur, lambda j, h=h: LG[:, 4 * h + j, :], 4, T, func=ACT.Gelu_apprx_tanh)
            barrier(act, cur)
            lru_act(act, cur, steps)
            barrier(act, cur)
            qkv_read(act, "act", cur, HD ** -0.5)
            barrier(act, cur)
            sb_act(act, cur, steps)
            barrier(act, cur)
            qkv_read(act, "act", cur)
            barrier(act, cur)
            head_norm_act(act, cur, steps, mem_q_norm)
            barrier(act, cur)
            head_norm_act(act, cur, steps, mem_k_norm)
            barrier(act, cur)
            att_act(act, cur, steps, mem_att)
            barrier(act, cur)
            merge_act(act, cur, 4, T, lambda i, c: par[:, bass.ds(i * DC + (PAR1["b_gate"][0] + c), 1)])
            barrier(act, cur)
            out_act(act, cur, T)
            barrier(act, cur)
            main_norm_act(act, cur, steps, T)
            barrier(act, cur)
            up_act(act, cur, steps)
            barrier(act, cur)
            down_act(act, cur)
            barrier(act, cur)
            turn_in_read(act, "act", cur, range(2), T)
            barrier(act, cur)
            for layer in range(LAYERS):
                n = T if layer == LAYERS - 1 else 2 * T
                ada_act(act, cur, layer)
                barrier(act, cur)
                main_norm_act(act, cur, steps, 2 * T, shift=lambda c, s: MOD[:, c, s:s + 1])
                barrier(act, cur)
                proj2_read(act, "act", cur, n)
                barrier(act, cur)
                att_act(act, cur, steps, na_x)
                barrier(act, cur)
                if n > T:
                    att_act(act, cur, steps, na_ctx)
                    barrier(act, cur)
                proj2_read(act, "act", cur, n)
                barrier(act, cur)
                skip_banks(cur, 8)
                lam_act(act, cur)
                barrier(act, cur)
                att_act(act, cur, steps, da_x)
                barrier(act, cur)
                if n > T:
                    att_act(act, cur, steps, da_ctx)
                    barrier(act, cur)
                head_norm_act(act, cur, steps, da_norm(n, 0.0))
                barrier(act, cur)
                gmlp_proj_read(act, "act", cur, n // P)
                barrier(act, cur)
                gmlp_ln_act(act, n // P, layer)
                gmlp_mix_act(act, cur, n // P)
                barrier(act, cur)
                merge_act(act, cur, 3, n, None)
                barrier(act, cur)
                out_act(act, cur, n)
                barrier(act, cur)
                main_norm_act(act, cur, steps, n, shift=lambda c, s: MOD[:, 3 * DC + c, s:s + 1])
                barrier(act, cur)
                route_act(act, cur, steps, n // T)
                barrier(act, cur)
                experts_act(act, cur, n // T)
                barrier(act, cur)
                skip_banks(cur, DC)
                barrier(act, cur)
            main_norm_act(act, cur, steps, T)
            barrier(act, cur)
            turn_out_act(act, cur)
            barrier(act, cur)
            ended.append((cur.stage, cur.t, cur.g))
            act.dma_start(out.rearrange("a (m p) d -> p (a m) d", p=P), OUT).then_inc(stored, 16)
            act.wait_ge(stored, 16)

        @block.vector
        def _(dve):
            cur = Cursor()
            steps = Steps(dve, dve_step)
            turn_in_read(dve, "dve", cur, range(4), 0)
            barrier(dve, cur)
            main_norm_dve(dve, cur, steps, 2 * T, lambda c, s: p1("attn_g" if s == 0 else "mem_g", c))
            barrier(dve, cur)
            qkv_read(dve, "dve", cur)
            forget_dve(dve, cur, steps)
            barrier(dve, cur)
            head_norm_dve(dve, cur, steps, fox_q_norm)
            barrier(dve, cur)
            head_norm_dve(dve, cur, steps, fox_k_norm)
            barrier(dve, cur)
            att_dve(dve, cur, steps, fox)
            barrier(dve, cur)
            for h in range(2):
                copies(dve, "dve", cur, lambda j, h=h: LX[:, 4 * h + j, :], 4, T)
            skip_banks(cur, 8)
            cur.t += 2
            barrier(dve, cur)
            lru_dve(dve, cur, steps)
            barrier(dve, cur)
            qkv_read(dve, "dve", cur, HD ** -0.5)
            barrier(dve, cur)
            sb_dve(dve, cur, steps)
            barrier(dve, cur)
            qkv_read(dve, "dve", cur)
            barrier(dve, cur)
            head_norm_dve(dve, cur, steps, mem_q_norm)
            barrier(dve, cur)
            head_norm_dve(dve, cur, steps, mem_k_norm)
            barrier(dve, cur)
            att_dve(dve, cur, steps, mem_att)
            barrier(dve, cur)
            merge_dve(dve, cur, steps, 4, T)
            barrier(dve, cur)
            out_dve(dve, cur, T)
            barrier(dve, cur)
            main_norm_dve(dve, cur, steps, T, lambda c, s: p1("ffn_g", c))
            barrier(dve, cur)
            up_dve(dve, cur, steps)
            barrier(dve, cur)
            down_dve(dve, cur)
            barrier(dve, cur)
            turn_in_read(dve, "dve", cur, range(2), T)
            barrier(dve, cur)
            for layer in range(LAYERS):
                n = T if layer == LAYERS - 1 else 2 * T
                lam_init = 0.8 - 0.6 * float(np.exp(-0.3 * layer))
                ada_dve(dve, cur, steps, layer)
                dve.drain().then_inc(dve_step, 1)
                steps.n += 1
                dve.wait_ge(dve_step, steps.n)
                gmod_dve(dve, steps, "g1", 1)
                barrier(dve, cur)
                main_norm_dve(dve, cur, steps, 2 * T, lambda c, s: gmod[:, c, s:s + 1], signal=True)
                barrier(dve, cur)
                proj2_read(dve, "dve", cur, n)
                barrier(dve, cur)
                dve.wait_ge(loads, 16 * LOADS["nab"][layer])
                att_dve(dve, cur, steps, na_x)
                barrier(dve, cur)
                if n > T:
                    att_dve(dve, cur, steps, na_ctx)
                    barrier(dve, cur)
                proj2_read(dve, "dve", cur, n)
                barrier(dve, cur)
                rope_dve(dve, cur, steps)
                lam_dve(dve, cur, steps, lam_init)
                barrier(dve, cur)
                att_dve(dve, cur, steps, da_x)
                barrier(dve, cur)
                if n > T:
                    att_dve(dve, cur, steps, da_ctx)
                    barrier(dve, cur)
                head_norm_dve(dve, cur, steps, da_norm(n, lam_init))
                barrier(dve, cur)
                gmlp_proj_read(dve, "dve", cur, n // P)
                barrier(dve, cur)
                gmlp_ln_dve(dve, cur, steps, n // P, layer)
                gmlp_mix_dve(dve, cur, steps, n // P)
                barrier(dve, cur)
                merge_dve(dve, cur, steps, 3, n)
                barrier(dve, cur)
                out_dve(dve, cur, n, gain=lambda c, s: MOD[:, 2 * DC + c, s:s + 1])
                gmod_dve(dve, steps, "g2", 4)
                barrier(dve, cur)
                main_norm_dve(dve, cur, steps, n, lambda c, s: gmod[:, c, s:s + 1], signal=True)
                barrier(dve, cur)
                route_dve(dve, cur, steps, n // T)
                barrier(dve, cur)
                experts_dve(dve, cur, n // T)
                barrier(dve, cur)
                scatter_dve(dve, cur, n // T)
                barrier(dve, cur)
            main_norm_dve(dve, cur, steps, T, lambda c, s: p2("g_final", c))
            barrier(dve, cur)
            skip_banks(cur, 4)
            barrier(dve, cur)
            ended.append((cur.stage, cur.t, cur.g))
            assert len(set(ended)) == 1, ended

        @block.gpsimd
        def _(pool):
            cur = Cursor()
            steps = Steps(pool, pool_step)
            for signal in looped:
                pool.sem_inc(signal, CREDIT)
            pool.dma_start(XIN_TM[:, 0:2, :], a["x"].rearrange("a (m p) d -> p (a m) d", p=P)).then_inc(loads, 16)
            pool.dma_start(XIN_TM[:, 2:4, :], a["mem"].rearrange("a (m p) d -> p (a m) d", p=P)).then_inc(loads, 16)
            pool.dma_start(const[:, :], a["const"]).then_inc(loads, 16)
            pool.dma_start(sel[:, :, :], a["sel"]).then_inc(loads, 16)
            pool.dma_start(head_sel[:, :, :], a["head_sel"]).then_inc(loads, 16)
            pool.dma_start(par[:, 0:N_PAR1], a["par1"]).then_inc(loads, 16)
            pool.wait_ge(loads, 16 * LOADS["start"])
            steps(nc.gpsimd.memset(small[:, :], 0.0))
            barrier(pool, cur)
            barrier(pool, cur)
            forget_pool(pool, cur)
            barrier(pool, cur)
            barrier(pool, cur)
            barrier(pool, cur)
            att_pool(pool, cur, steps, fox)
            barrier(pool, cur)
            pool.dma_start(LW, a["lru_w"]).then_inc(loads, 16)
            pool.wait_ge(loads, 16 * LOADS["lru_w"])
            barrier(pool, cur)
            barrier(pool, cur)
            barrier(pool, cur)
            sb_pool(pool, cur, steps)
            barrier(pool, cur)
            for _ in range(3):
                barrier(pool, cur)
            att_pool(pool, cur, steps, mem_att)
            barrier(pool, cur)
            for _ in range(5):
                barrier(pool, cur)
            pool.dma_start(XIN_TM[:, 0:2, :], a["ctx"].rearrange("a (m p) d -> p (a m) d", p=P)).then_inc(loads, 16)
            pool.dma_start(par[:, 0:N_PAR2], a["par2"][0]).then_inc(loads, 16)
            pool.wait_ge(loads, 16 * 11)
            barrier(pool, cur)
            n_loads = 11
            for layer in range(LAYERS):
                n = T if layer == LAYERS - 1 else 2 * T
                assert n_loads == LOADS["par"][layer], (n_loads, layer)
                pool.dma_start(NAB.rearrange("p a b c t -> p (a b c t)"), a["na_bias"][layer]).then_inc(loads, 16)
                barrier(pool, cur)
                barrier(pool, cur)
                barrier(pool, cur)
                pool.wait_ge(loads, 16 * (n_loads + 1))
                att_pool(pool, cur, steps, na_x)
                barrier(pool, cur)
                if n > T:
                    att_pool(pool, cur, steps, na_ctx)
                    barrier(pool, cur)
                barrier(pool, cur)
                barrier(pool, cur)
                att_pool(pool, cur, steps, da_x)
                barrier(pool, cur)
                if n > T:
                    att_pool(pool, cur, steps, da_ctx)
                    barrier(pool, cur)
                barrier(pool, cur)
                pool.dma_start(GWS, a["w_s"][layer]).then_inc(loads, 16)
                pool.dma_start(GLN[:, 0, :], a["ln_g"][layer].partition_broadcast(P)).then_inc(loads, 16)
                pool.dma_start(GLN[:, 1, :], a["ln_b"][layer].partition_broadcast(P)).then_inc(loads, 16)
                pool.wait_ge(loads, 16 * (n_loads + 4))
                barrier(pool, cur)
                barrier(pool, cur)
                barrier(pool, cur)
                barrier(pool, cur)
                barrier(pool, cur)
                barrier(pool, cur)
                experts_pool(pool, cur, n // T)
                barrier(pool, cur)
                barrier(pool, cur)
                n_loads += 4
                if layer < LAYERS - 1:
                    pool.dma_start(par[:, 0:N_PAR2], a["par2"][layer + 1]).then_inc(loads, 16)
                    n_loads += 1
                    pool.wait_ge(loads, 16 * n_loads)
            barrier(pool, cur)
            barrier(pool, cur)
            assert cur.stage == ended[0][0], (cur.stage, ended)


def _chunks(v):
    return v.reshape(-1, P).T


def _rows(w):
    return w.reshape(-1, P, w.shape[1]).transpose(1, 0, 2)


def _stream(x):
    tiles = []

    def put(w):
        t = np.zeros((P, WORDS), np.float32)
        w = w.reshape(P, -1)
        t[:, :w.shape[1]] = w
        tiles.append(t)

    def cols(w, lo, hi):
        w = _rows(w)
        for c in range(lo, hi, 512):
            put(w[:, :, c:c + 512])

    w_in = x["w_in"][0]
    f0 = 3 * D + HEADS
    cols(w_in, 0, 3 * D)
    cols(w_in, f0, f0 + 5 * D)
    cols(w_in, f0 + 5 * D, f0 + 6 * D)
    cols(x["w_mem_kv"][0], 0, 2 * D)
    for n in range(4):
        for h in range(2):
            lo = f0 + 6 * D + n * D + h * 512
            cols(w_in, lo, lo + 512)
            cols(x["w_branch"][0, n], h * 512, h * 512 + 512)
    cols(x["w_out"][0], 0, D)
    up = _rows(x["w_up"][0])
    for j in range(FC // 2):
        put(np.concatenate([up[:, :, j * 256:(j + 1) * 256], up[:, :, FF + j * 256:FF + (j + 1) * 256]], axis=2))
    down = _rows(x["w_down"][0])
    for c in range(DC):
        put(down[:, :, c * P:(c + 1) * P])
    for l in range(LAYERS):
        cols(x["w_ada_2"][l], 0, 6 * D)
        w = x["w_in_2"][l]
        for at in (4, 0, 1, 5, 2, 3, 6, 7):
            cols(w, at * BW, (at + 1) * BW)
        for n in range(3):
            for h in range(2):
                lo = 8 * BW + n * D + h * 512
                cols(w, lo, lo + 512)
                cols(x["w_branch_2"][l, n], h * 512, h * 512 + 512)
        cols(x["w_out_2"][l], 0, D)
        for e in range(EXPERTS):
            for h in range(2):
                cols(x["w_e1_2"][l, e], h * 512, h * 512 + 512)
                cols(x["w_e3_2"][l, e], h * 512, h * 512 + 512)
            cols(x["w_e2_2"][l, e], 0, D)
    assert len(tiles) == N_TILES, (len(tiles), N_TILES)
    return np.stack(tiles)


def _constants():
    i = np.arange(P)
    t = np.arange(T)
    c = {}
    c["ident"] = np.eye(P)
    c["tri"] = (i[:, None] >= i[None, :])
    c["ones"] = np.ones((P, P))
    row = (i[:, None] + P * np.arange(2)[None, :])
    c["causal"] = np.where(t[None, None, :] <= row[:, :, None], 0.0, NEG)
    valid = row[:, :, None] < t[None, None, :]
    c["sb_add"] = np.where(valid, 0.0, NEG)
    c["sb_neg"] = np.where(valid, -1.0, 0.0)
    c["before"] = t[None, None, :] < row[:, :, None]
    f = i % 64
    inv = (np.float32(10000.0) ** (-np.arange(0, 32, 2, dtype=np.float32) / np.float32(32))).astype(np.float32)
    place = np.where((f < 32)[:, None], (t // GRID)[None, :], (t % GRID)[None, :]).astype(np.float32)
    ang = place * inv[f % 16][:, None]
    c["cos"], c["sin"] = np.cos(ang), np.sin(ang)
    swap = np.zeros((P, P))
    for p in range(P):
        first = p % 32 < 16
        swap[p + 16 if first else p - 16, p] = -1.0 if first else 1.0
    c["swap"] = swap
    c["slots"] = np.broadcast_to(np.arange(CAP), (P, CAP))
    hs = np.zeros((P, DC, 16))
    for k in range(DC):
        hs[i, k, 2 * k + i // 64] = 1.0
    c["head_sum"] = hs
    rs = np.zeros((P, 4, 16))
    for k in range(4):
        rs[:, k, k] = 1.0
    c["row_sum"] = rs
    const = np.zeros((P, N_CONST), np.float32)
    for name, (lo, hi) in CONSTS.items():
        const[:, lo:hi] = np.asarray(c[name], np.float32).reshape(P, -1)
    sel = np.zeros((16, 16, P), np.float32)
    sel[np.arange(16), np.arange(16), :] = 1.0
    return const, sel, np.ascontiguousarray(hs.transpose(2, 1, 0)).astype(np.float32)


def _params(table, values, n):
    par = np.zeros((P, n), np.float32)
    for name, (lo, hi) in table.items():
        v = values[name]
        par[:v.shape[0], lo:hi] = v.reshape(v.shape[0], -1)
    return par


def _layout(x):
    const, sel, head_sel = _constants()
    pair = lambda v: np.concatenate([v, v]).reshape(P, 1)
    chunk_rows = lambda w: np.concatenate([_chunks(r) for r in w], axis=1)
    w_in = x["w_in"][0]
    par1 = dict(attn_g=_chunks(x["attn_norm_g"][0]), mem_g=_chunks(x["mem_norm_g"][0]),
                ffn_g=_chunks(x["ffn_norm_g"][0]), fox_q_g=pair(x["fox_q_norm_g"][0]),
                fox_k_g=pair(x["fox_k_norm_g"][0]), mem_q_g=_chunks(x["mem_q_norm_g"][0]),
                mem_k_g=_chunks(x["mem_k_norm_g"][0]), conv_w=chunk_rows(x["lru_conv_w"][0]),
                conv_b=_chunks(x["lru_conv_b"][0]), b_a=_chunks(x["lru_b_a"][0]), b_x=_chunks(x["lru_b_x"][0]),
                lam=_chunks(x["lru_lambda"][0]), b_gate=chunk_rows(x["b_gate"][0]),
                ffn_w=chunk_rows(x["ffn_conv_w"][0]), ffn_b=_chunks(x["ffn_conv_b"][0]),
                b_forget=x["b_forget"][0].reshape(16, 1), w_forget=_rows(w_in[:, 3 * D:3 * D + HEADS]))
    lru_w = np.zeros((P, 2, DC, P), np.float32)
    for g, name in enumerate(("lru_w_a", "lru_w_x")):
        for b in range(16):
            o = 64 * (b % 2)
            lru_w[o:o + 64, g, b // 2, o:o + 64] = x[name][0, b]
    both = np.stack([_chunks(x["c_2"][0]), _chunks(x["c_ctx_2"])], axis=2)
    par2 = []
    q = np.arange(T)
    qr, qc, kr, kcol = q[:, None] // GRID, q[:, None] % GRID, q[None, :] // GRID, q[None, :] % GRID
    start = np.clip(qc - 8, 0, GRID - 16)
    inside = (kcol >= start) & (kcol < start + 16)
    dr, dc = kr - qr + 7, np.where(inside, kcol - qc + 15, 0)
    na = np.full((LAYERS, P, 8, 2, T), NEG, np.float32)
    for l in range(LAYERS):
        par2.append(_params(PAR2, dict(
            b_ada=_chunks(x["b_ada_2"][l]), g1=_chunks(x["g_norm1_2"][l]), g2=_chunks(x["g_norm2_2"][l]),
            subln=x["da_subln_g_2"][l].reshape(P, 1), b_s=x["gm_b_s_2"][l].T,
            lam_q=np.stack([x["da_lam_q1_2"][l], x["da_lam_q2_2"][l]], axis=1),
            lam_k=np.stack([x["da_lam_k1_2"][l], x["da_lam_k2_2"][l]], axis=1),
            w_router=_rows(x["w_router_2"][l]), g_final=_chunks(x["g_final_2"]), c=both), N_PAR2))
        b = np.where(inside[None], x["na_rpb_2"][l][:, dr, dc], np.float32(NEG))
        na[l] = b.reshape(8, 2, P, T).transpose(2, 0, 1, 3)
    return {
        "stream": _stream(x), "x": x["x"], "mem": x["mem"], "ctx": x["ctx_2"], "const": const, "sel": sel,
        "head_sel": head_sel, "par1": _params(PAR1, par1, N_PAR1), "par2": np.stack(par2), "lru_w": lru_w,
        "na_bias": na.reshape(LAYERS, P, -1), "w_s": np.ascontiguousarray(x["gm_w_s_2"].transpose(0, 3, 1, 2)),
        "ln_g": x["gm_ln_g_2"], "ln_b": x["gm_ln_b_2"],
    }


def kernel(**inputs):
    import concourse.bacc as _bacc
    from concourse.bass_utils import run_bass_kernel_spmd as _run

    nc = _bacc.Bacc("TRN2", target_bir_lowering=False, num_devices=1)
    arrays, aps = {}, {}
    for name, v in _layout({k: np.asarray(v) for k, v in inputs.items()}).items():
        v = np.ascontiguousarray(v)
        arrays[f"in_{name}"] = v
        aps[name] = nc.dram_tensor(f"in_{name}", v.shape, mybir.dt.from_np(v.dtype), kind="ExternalInput").ap()
    aps["cum_scratch"] = nc.dram_tensor("cum_scratch", (HEADS, T), F32).ap()
    out = nc.dram_tensor("out_0", (1, T, D), F32, kind="ExternalOutput").ap()
    build(nc, aps, out)
    r = _run(nc, [arrays], core_ids=[0])
    return r.results[0]["out_0"]
```

```python
from contextlib import ExitStack, contextmanager

import numpy as np

import concourse.bass as bass
from concourse import mybir

F32 = mybir.dt.float32
F32R = mybir.dt.float32r
ACT = mybir.ActivationFunctionType
ALU = mybir.AluOpType
AX = mybir.AxisListType

P = 128
D = 1024
DC = D // P
T = 256
TT = T // P
HD = 64
HEADS = D // HD
FF = 2816
FC = FF // P
LAYERS = 2
BW = 512
BC = BW // P
NA_HEADS = BW // HD
EXPERTS = 16
CAP = 2 * T // EXPERTS
MODC = 6 * DC
GRID = 64
EPS = 1e-6
NEG = -1e30
LRU_C = 8.0

R = 4
PIECE = 1024
WORDS = 2 * PIECE
AHEAD = 3
CREDIT = 4
WK_WORDS = 20736
XS_CHUNK = 3 * 64
XS_WORDS = DC * XS_CHUNK

CONSTS = {}
_at = 0
for _name, _n in (("ident", P), ("tri", P), ("ones", P), ("swap", P), ("causal", 2 * T),
                  ("sb_add", 2 * T), ("sb_neg", 2 * T), ("cos", T), ("sin", T), ("before", 2 * T),
                  ("slots", CAP), ("pair_ones", P)):
    CONSTS[_name] = (_at, _at + _n)
    _at += _n
N_CONST = _at

PAR1 = {}
_at = 0
for _name, _n in (("attn_g", DC), ("mem_g", DC), ("ffn_g", DC), ("fox_q_g", 1), ("fox_k_g", 1),
                  ("mem_q_g", 2), ("mem_k_g", 2), ("conv_w", 4 * DC), ("conv_b", DC), ("b_a", DC),
                  ("b_x", DC), ("lam", DC), ("b_gate", 4 * DC), ("ffn_w", 3 * FC), ("ffn_b", FC),
                  ("b_forget", 1), ("w_forget", DC * 16)):
    PAR1[_name] = (_at, _at + _n)
    _at += _n
N_PAR1 = _at

PAR2 = {}
_at = 0
for _name, _n in (("b_ada", MODC), ("g1", DC), ("g2", DC), ("subln", 1), ("b_s", 4), ("lam_q", 2),
                  ("lam_k", 2), ("w_router", DC * 16), ("g_final", DC), ("c", DC * 2)):
    PAR2[_name] = (_at, _at + _n)
    _at += _n
N_PAR2 = _at
N_PAR = max(N_PAR1, N_PAR2)

TILE = DC * 512
STREAM_WORDS = (6 + 4 + 6 + 6 + 16 + 2 + FC // 2) * TILE + FC * D \
    + LAYERS * ((12 + 8) * TILE + 3 * 2 * (TILE + BC * 512) + (2 + 6 * EXPERTS) * TILE)
N_SLOTS = STREAM_WORDS // WORDS + 2
assert STREAM_WORDS % WORDS == 0


class Cursor:

    def __init__(self, who):
        self.who = who
        self.p = 0
        self.s = 0
        self.g = 0
        self.i = None
        self.pieces_per = 0
        self.banks_per = 0
        self.rounds = {}
        self.stage = 0

    def base(self, kind):
        return self.rounds.get(kind, 0)

    def add(self, kind, n):
        self.rounds[kind] = self.base(kind) + n

    def piece_use(self, piece, k=0, unit=1, period=4):
        v = unit * (piece // period + k)
        return v if self.i is None else v + self.i * (unit * (self.pieces_per // period))

    def bank(self):
        return self.g % 4

    def bank_use(self, k=0):
        v = self.g // 4 + k
        return v if self.i is None else v + self.i * self.banks_per


def one(i):
    return slice(i, i + 1) if isinstance(i, int) else bass.ds(i, 1)


def span(i, n):
    return slice(i * n, i * n + n) if isinstance(i, int) else bass.ds(i * n, n)


def build(nc, a, out):
    ctx = ExitStack()
    with ctx:
        sb = lambda name, shape: ctx.enter_context(nc.sbuf_tensor(name, shape, F32))
        sem = lambda name: ctx.enter_context(nc.semaphore(name))

        with ExitStack() as place:
            ring = place.enter_context(nc.sbuf_tensor("ring", [P, R, WORDS], F32))
            WK = place.enter_context(nc.sbuf_tensor("WK", [P, WK_WORDS], F32))
        ring_lo = ctx.enter_context(nc.sbuf_tensor("ring_lo", [P, R, WORDS], F32R))
        WKR = ctx.enter_context(nc.sbuf_tensor("WKR", [P, WK_WORDS], F32R))
        piece_hi = ctx.enter_context(nc.sbuf_tensor("piece_hi", [P, 4, PIECE], F32R))
        A = ctx.enter_context(nc.sbuf_tensor("A", [P, 2, DC, 2 * T], F32R))
        AH, AL = A[:, 0], A[:, 1]
        XT = sb("XT", [P, DC, 2 * T])
        const = sb("const", [P, N_CONST])
        sel = sb("sel", [16, 16, P])
        par = sb("par", [P, N_PAR])
        MOD = sb("MOD", [P, MODC, 2])
        gmod = sb("gmod", [P, DC, 2])
        small = sb("small", [P, 64])
        rowst = sb("rowst", [16, 2 * T])
        ps = ctx.enter_context(nc.psum_tensor("ps", [P, 8, 512], F32))

        def cst(name):
            lo, hi = CONSTS[name]
            return const[:, lo:hi]

        def p1(name, c=0, n=1):
            lo = PAR1[name][0] + c
            return par[:, lo:lo + n]

        def p2(name, c=0, n=1):
            lo = PAR2[name][0] + c
            return par[:, lo:lo + n]

        ident = cst("ident")
        ones = cst("ones")

        def wk(at, *shape):
            n = int(np.prod(shape))
            v = WK[:, at:at + n]
            if len(shape) == 1:
                return v
            names = "abcd"[:len(shape)]
            return v.rearrange(f"p ({' '.join(names)}) -> p {' '.join(names)}",
                               **{x: s for x, s in zip(names[1:], shape[1:])})

        def f32(x):
            return x.bitcast(F32)

        landed = [sem(f"landed{s}") for s in range(R)]
        hi_done = [sem(f"hi_done{j}") for j in range(4)]
        lo_done = [sem(f"lo_done{j}") for j in range(4)]
        piece_used = [sem(f"piece_used{j}") for j in range(4)]
        bank_full = [sem(f"bank_full{b}") for b in range(4)]
        bank_free = [sem(f"bank_free{b}") for b in range(4)]
        stage_done = sem("stage_done")
        loads = sem("loads")
        stored = sem("stored")
        act_step = sem("act_step")
        dve_step = sem("dve_step")
        pool_step = sem("pool_step")
        att_scores = sem("att_scores")
        att_nmax = sem("att_nmax")
        att_exp = sem("att_exp")
        att_probs = sem("att_probs")
        att_turned = sem("att_turned")
        att_copied = sem("att_copied")
        att_y = sem("att_y")
        att_saved = sem("att_saved")
        sb_y = sem("sb_y")
        sb_saved = sem("sb_saved")
        sb_z = sem("sb_z")
        sb_abs = sem("sb_abs")
        sb_ln = sem("sb_ln")
        sb_l = sem("sb_l")
        sb_incl = sem("sb_incl")
        sb_logw = sem("sb_logw")
        sb_w = sem("sb_w")
        norm_sq = sem("norm_sq")
        norm_sd = sem("norm_sd")
        x_hi = sem("x_hi")
        x_lo = sem("x_lo")
        y_hi = sem("y_hi")
        y_lo = sem("y_lo")
        moe_staged = sem("moe_staged")
        moe_h = sem("moe_h")
        moe_silu = sem("moe_silu")
        moe_hid = sem("moe_hid")
        moe_turned = sem("moe_turned")
        moe_copied = sem("moe_copied")
        moe_split = sem("moe_split")
        moe_y = sem("moe_y")
        moe_saved = [sem(f"moe_saved{h}") for h in range(2)]
        lam_prod = sem("lam_prod")
        lru_xc = sem("lru_xc")
        lru_ri = sem("lru_ri")
        lru_gates = sem("lru_gates")
        lru_a = sem("lru_a")
        lru_om = sem("lru_om")
        lru_root = sem("lru_root")
        fox_z = sem("fox_z")
        fox_e = sem("fox_e")
        fox_cum = sem("fox_cum")
        rope_r = sem("rope_r")
        raw_gates = sem("raw_gates")
        silu_c = sem("silu_c")
        split_c = sem("split_c")
        normed = sem("normed")
        ln_var = sem("ln_var")
        ln_sd = sem("ln_sd")
        ln_done = sem("ln_done")
        aff_logits = sem("aff_logits")
        aff_exp = sem("aff_exp")
        affinities = sem("affinities")
        onehot = sem("onehot")
        conv_done = sem("conv_done")
        silu_done = sem("silu_done")
        gate_used = sem("gate_used")
        looped = [att_scores, att_nmax, att_exp, att_probs, att_turned, att_copied,
                  att_y, att_saved, sb_y, sb_saved, sb_z, sb_abs, sb_ln, sb_l,
                  sb_incl, sb_logw, sb_w, moe_staged, moe_h, moe_silu, moe_hid, moe_turned, moe_copied,
                  moe_split, moe_y, *moe_saved]

        class Steps:

            def __init__(self, eng, sem):
                self.eng, self.sem, self.n, self.i, self.per = eng, sem, 0, None, 0

            def __call__(self, ins):
                ins.then_inc(self.sem, 1)
                self.n += 1
                self.eng.wait_ge(self.sem, self.n if self.i is None else self.n + self.i * self.per)

        @contextmanager
        def loop(eng, cur, n, pieces=0, banks=0, steps=None, steps_per=0):
            assert pieces % (2 * R) == 0 and banks % 4 == 0
            p0, g0, ahead = cur.p, cur.g, cur.s - cur.p
            with eng.Fori(0, n) as i:
                cur.i, cur.pieces_per, cur.banks_per = i, pieces, banks // 4
                if steps:
                    steps.i, steps.per, s0 = i, steps_per, steps.n
                yield i
            assert cur.p - p0 == pieces and cur.g - g0 == banks, (cur.p - p0, cur.g - g0)
            if steps:
                assert steps.n - s0 == steps_per, steps.n - s0
                steps.n += steps_per * (n - 1)
                steps.i = None
            cur.p += pieces * (n - 1)
            cur.s = cur.p + ahead
            cur.g += banks * (n - 1)
            cur.i = None

        def barrier(eng, cur):
            eng.drain().then_inc(stage_done, 1)
            cur.stage += 1
            eng.wait_ge(stage_done, 4 * cur.stage)

        def split_hi(act, cur):
            j, slot, at = cur.s % 4, cur.s // 2 % R, cur.s % 2 * PIECE
            act.wait_ge(landed[slot], cur.piece_use(cur.s, 1, 16, 2 * R))
            if cur.s >= 4:
                act.wait_ge(piece_used[j], cur.piece_use(cur.s))
            nc.scalar.activation(piece_hi[:, j, :], ring[:, slot, at:at + PIECE], ACT.Copy).then_inc(hi_done[j], 1)
            cur.s += 1

        def split_lo(dve, cur):
            j, slot, at = cur.s % 4, cur.s // 2 % R, cur.s % 2 * PIECE
            dve.wait_ge(hi_done[j], cur.piece_use(cur.s, 1))
            nc.vector.tensor_tensor(ring_lo[:, slot, at:at + PIECE], ring[:, slot, at:at + PIECE],
                                    f32(piece_hi[:, j, :]), ALU.subtract).then_inc(lo_done[j], 1)
            cur.s += 1

        def next_piece(eng, cur, n=1):
            for _ in range(n):
                cur.p += 1
                if cur.who == "act":
                    split_hi(eng, cur)
                if cur.who == "dve":
                    split_lo(eng, cur)

        def piece_of(pe, cur):
            j, slot, at = cur.p % 4, cur.p // 2 % R, cur.p % 2 * PIECE
            pe.wait_ge(lo_done[j], cur.piece_use(cur.p, 1))
            cur.p += 1
            return piece_hi[:, j, :], ring_lo[:, slot, at:at + PIECE]

        def three(out_, l, r, first, last):
            nc.tensor.matmul(out_, l[0], r[0], start=first, stop=False)
            nc.tensor.matmul(out_, l[0], r[1], start=False, stop=False)
            return nc.tensor.matmul(out_, l[1], r[0], start=False, stop=last)

        def bank_parts(pe, cur, parts, turn=False):
            b = cur.bank()
            if cur.g >= 4:
                pe.wait_ge(bank_free[b], cur.bank_use())
            for rows, at, n, pairs in parts:
                for k, (l, r) in enumerate(pairs):
                    if turn:
                        last = nc.tensor.transpose(ps[0:rows, b, at:at + n], l, r)
                    else:
                        last = nc.tensor.matmul(ps[0:rows, b, at:at + n], l, r,
                                                start=(k == 0), stop=(k == len(pairs) - 1))
            last.then_inc(bank_full[b], 1)
            cur.g += 1

        def read_bank(eng, cur, mine, op, piece=False):
            b = cur.bank()
            if mine:
                eng.wait_ge(bank_full[b], cur.bank_use(1))
                if piece:
                    eng.sem_inc(piece_used[cur.p % 4], 1)
                op(ps[:, b, :]).then_inc(bank_free[b], 1)
            cur.g += 1
            if piece:
                next_piece(eng, cur)

        def skip_fm(eng, cur, banks, kc=DC):
            for j in range(banks):
                read_bank(eng, cur, False, None, piece=(kc == DC or j % 2 == 1))

        def fm_banks(pe, cur, moving, n, banks, kc=DC, ready=None):
            for c in range(banks):
                b = cur.bank()
                if cur.g >= 4:
                    pe.wait_ge(bank_free[b], cur.bank_use())
                for k in range(kc):
                    block = c * kc + k
                    if block % 8 == 0:
                        hi, lo = piece_of(pe, cur)
                    if ready and c == 0:
                        ready(k)
                    at = slice(block % 8 * P, (block % 8 + 1) * P)
                    last = three(ps[:, b, 0:n], (hi[:, at], lo[:, at]), moving(k), k == 0, k == kc - 1)
                    if block % 8 == 7 and k < kc - 1:
                        last.then_inc(piece_used[(cur.p - 1) % 4], 1)
                last.then_inc(bank_full[b], 1)
                cur.g += 1

        def in_a(c0=0):
            return lambda n: lambda k: (AH[:, k, c0:c0 + n], AL[:, k, c0:c0 + n])

        def tm_tile(pe, cur, t0, tt):
            banks = [(cur.g + m) % 4 for m in range(tt)]
            for j in range(4):
                hi, lo = piece_of(pe, cur)
                for m in range(tt):
                    if j == 0 and cur.g + m >= 4:
                        pe.wait_ge(bank_free[banks[m]], (cur.g + m) // 4)
                    tok = slice(t0 + m * P, t0 + (m + 1) * P)
                    for q in range(2):
                        k, w = 2 * j + q, slice(q * 512, q * 512 + 512)
                        last = three(ps[:, banks[m], :], (AH[:, k, tok], AL[:, k, tok]), (hi[:, w], lo[:, w]),
                                     k == 0, k == DC - 1)
                    if j == 3:
                        last.then_inc(bank_full[banks[m]], 1)
                if j < 3:
                    last.then_inc(piece_used[(cur.p - 1) % 4], 1)
            cur.g += tt

        def copies(eng, who, cur, dst, banks, n, scale=1.0, func=None, tm=False):
            if tm:
                next_piece(eng, cur, 3)
            for j in range(banks):
                def op(bank, j=j):
                    if who == "act":
                        return nc.scalar.activation(dst(j), bank[:, 0:n], func or ACT.Copy, scale=scale)
                    return nc.vector.tensor_scalar(dst(j), bank[:, 0:n], scale, None, ALU.mult)
                mine = who == "act" if func or j % 2 == 0 else who == "dve"
                read_bank(eng, cur, mine, op, piece=not tm or j == banks - 1)

        def split_x_act(act, cur, groups):
            for src_, hi in groups:
                nc.scalar.activation(hi, src_, ACT.Copy).then_inc(x_hi, 1)
            cur.add("x", len(groups))

        def split_x_dve(dve, cur, groups):
            for n, (src_, hi, lo) in enumerate(groups):
                dve.wait_ge(x_hi, cur.base("x") + n + 1)
                nc.vector.tensor_tensor(lo, src_, f32(hi), ALU.subtract).then_inc(x_lo, 1)
            cur.add("x", len(groups))

        SQ = wk(0, DC, 2 * T)
        RB = wk(4096, 2048)
        HF = SQ
        FG = wk(4608, 4, T)

        def skip_banks(cur, n):
            cur.g += n

        ATT_PT = 2048
        ATT_END = 6400
        SPARE = WK_WORDS - 2048
        pt_all = wk(ATT_PT, 2, 4, 256)

        def t_of(r, nk):
            if nk == T:
                return wk(1024 * (r % 2), 2, 2, T)
            return wk(0 if r % 2 == 0 else SPARE, 2, 2, 2 * T)

        nmax = small[:, 0:4].rearrange("p (a b) -> p a b", a=2)
        sums_ = small[:, 4:8].rearrange("p (a b) -> p a b", a=2)
        rcp = small[:, 8:12].rearrange("p (a b) -> p a b", a=2)
        nlam = small[:, 12:13]

        def att_chunks(at):
            if at["diff"]:
                return [[0]]
            return [[0, 1]] if at["nk"] == 256 else [[0], [1]]

        def att_pe(pe, cur, at):
            nk, n = at["nk"], at["n"]
            kc = nk // P
            base, cbase = cur.base("att"), cur.base("att_c")
            chunks = att_chunks(at)

            def scores(r):
                pe.wait_ge(att_nmax if at["bias"] else att_exp, CREDIT + base + r)
                for a in range(2):
                    for qt in range(2):
                        pairs = at["qk"](r, a, qt)
                        for j, (l, m) in enumerate(pairs):
                            last = nc.tensor.matmul(ps[:, 2 * a + qt, 0:nk], l, m, start=(j == 0),
                                                    stop=(j == len(pairs) - 1))
                last.then_inc(att_scores, 1)

            def rest(r):
                t = t_of(r, nk)
                pe.wait_ge(att_probs, CREDIT + base + r + 1)
                for j, heads in enumerate(chunks):
                    pe.wait_ge(att_copied, CREDIT + cbase + r * len(chunks) + j)
                    col = 0
                    for a in heads:
                        for k in range(kc):
                            for qt in range(2):
                                b = 4 + col // 512
                                last = nc.tensor.transpose(ps[:, b, col % 512:col % 512 + P],
                                                           t[:, a, qt, k * P:(k + 1) * P], ident)
                                col += P
                    last.then_inc(att_turned, 1)
                pe.wait_ge(att_saved, CREDIT + base + r)
                for a, rows, col, pairs in at["pv"](r):
                    if a < len(chunks):
                        pe.wait_ge(att_copied, CREDIT + cbase + r * len(chunks) + a + 1)
                    for j, (l, m) in enumerate(pairs):
                        last = nc.tensor.matmul(ps[rows, 6 + col // 512, col % 512:col % 512 + T], l, m,
                                                start=(j == 0), stop=(j == len(pairs) - 1))
                last.then_inc(att_y, 1)

            scores(0)
            for r in range(n):
                if r < n - 1:
                    scores(r + 1)
                rest(r)
            cur.add("att", n)
            cur.add("att_c", n * len(chunks))

        def att_act(act, cur, steps, at):
            nk, n = at["nk"], at["n"]
            kc = nk // P
            base, cbase = cur.base("att"), cur.base("att_c")
            chunks = att_chunks(at)

            def exps(r):
                act.wait_ge(att_nmax, CREDIT + base + r + 1)
                t = t_of(r, nk)
                if not at["bias"]:
                    act.wait_ge(att_turned, CREDIT + cbase + (r - 1) * len(chunks))
                for a in range(2):
                    for qt in range(2):
                        src = t[:, a, qt, :] if at["bias"] else ps[:, 2 * a + qt, 0:nk]
                        last = nc.scalar.activation(t[:, a, qt, :], src, ACT.Exp,
                                                    bias=nmax[:, a, qt:qt + 1],
                                                    accum_out=sums_[:, a, qt:qt + 1])
                last.then_inc(att_exp, 1)

            def copy(r):
                for j, heads in enumerate(chunks):
                    act.wait_ge(att_turned, CREDIT + cbase + r * len(chunks) + j + 1)
                    act.wait_ge(att_y, CREDIT + base + r)
                    words = len(heads) * kc * T
                    if words == 1024 and kc == 4:
                        dst, src = pt_all[:, heads[0], :, :], ps[:, 4:6, :]
                        dst = dst.rearrange("p (b k) q -> p b (k q)", b=2)
                    elif words == 1024:
                        dst, src = pt_all[:, 0:2, 0:2, :].rearrange("p a k q -> p a (k q)"), ps[:, 4:6, :]
                    else:
                        dst, src = pt_all[:, 0, 0:2, :].rearrange("p k q -> p (k q)"), ps[:, 4, :]
                    nc.scalar.activation(dst, src, ACT.Copy).then_inc(att_copied, 1)

            def save(r):
                act.wait_ge(att_y, CREDIT + base + r + 1)
                dst, src = at["save"](r)
                nc.scalar.activation(dst, src, ACT.Copy).then_inc(att_saved, 1)

            exps(0)
            for r in range(n):
                copy(r)
                if r < n - 1:
                    exps(r + 1)
                save(r)
            cur.add("att", n)
            cur.add("att_c", n * len(chunks))

        def att_dve(dve, cur, steps, at):
            nk, n = at["nk"], at["n"]
            base, cbase = cur.base("att"), cur.base("att_c")
            nch = len(att_chunks(at))
            s4 = ps[:, 0:4, :].rearrange("p (a b) k -> p a b k", a=2)

            def maxima(r):
                dve.wait_ge(att_scores, CREDIT + base + r + 1)
                dve.wait_ge(att_exp, CREDIT + base + r)
                src = s4[:, :, :, 0:nk]
                if at["bias"]:
                    dve.wait_ge(att_turned, CREDIT + cbase + (r - 1) * nch)
                    at["bias"](r, s4, steps, t_of(r, nk))
                    src = t_of(r, nk)
                nc.vector.tensor_reduce(nmax, src, AX.X, ALU.max, negate=True).then_inc(att_nmax, 1)

            def probs(r):
                dve.wait_ge(att_exp, CREDIT + base + r + 1)
                steps(nc.vector.reciprocal(rcp, sums_))
                if at["diff"]:
                    steps(nc.vector.tensor_scalar(rcp[:, 1, :], rcp[:, 1, :], nlam, None, ALU.mult))
                t = t_of(r, nk)
                ins = nc.vector.tensor_tensor(t, t, rcp.unsqueeze(3).to_broadcast([P, 2, 2, nk]), ALU.mult)
                if at["diff"]:
                    steps(ins)
                    ins = nc.vector.tensor_tensor(t[:, 0], t[:, 0], t[:, 1], ALU.add)
                ins.then_inc(att_probs, 1)

            for r in range(n):
                maxima(r)
                probs(r)
            cur.add("att", n)
            cur.add("att_c", n * nch)

        def pair_att(n, nk, q, q0, k, k0, v, v0, y, y0, bias=None, diff=False):
            kc = nk // P

            def qk(r, a, qt):
                h = slice(64 * a, 64 * a + 64)
                return [(q[h, r, q0 + qt * P:q0 + (qt + 1) * P], k[h, r, k0:k0 + nk])]

            def pv(r):
                if diff:
                    return [(0, slice(0, P), 0, [(v[:, v0 + k_, r * P:(r + 1) * P], pt_all[:, 0, k_, :])
                                                 for k_ in range(kc)])]
                return [(a, slice(64 * a, 64 * a + 64), 0,
                         [(v[:, v0 + k_, r * P + 64 * a:r * P + 64 * a + 64], pt_all[:, a, k_, :])
                          for k_ in range(kc)]) for a in range(2)]

            def save(r):
                return y[:, r, y0:y0 + T], ps[:, 6, 0:T]

            return dict(n=n, nk=nk, diff=diff, bias=bias, qk=qk, pv=pv, save=save)

        YT = wk(6400 + 6144, 4, DC, T)
        QT, KT, VT = wk(6400, DC, T), wk(6400 + 2048, DC, T), wk(6400 + 4096, TT, D)
        CUM = wk(6400 + 6144 + 4096, 16, T)
        Q2, K2, V2 = wk(6400, BC, 2 * T), wk(6400 + 2048, BC, 2 * T), wk(6400 + 4096, 4, BW)
        Y2 = wk(6400 + 6144, 3, BC, 2 * T)
        NAB = wk(6400 + 6144 + 2048, 4, 2, 2, T)
        MIXT = wk(0, DC, 2 * T)
        GATE = wk(4096, 4, 2 * T)

        XIN_TM = wk(0, 4, D)

        def turn_in_pe(pe, cur, tiles, col0):
            for c in range(DC):
                bank_parts(pe, cur, [(P, m * P, P, [(XIN_TM[:, tt, c * P:(c + 1) * P], ident)])
                                     for m, tt in enumerate(tiles)], turn=True)

        def turn_in_read(eng, who, cur, tiles, col0):
            n = len(tiles) * P
            for c in range(DC):
                def op(bank, c=c):
                    dst = XT[:, c, col0:col0 + n]
                    if who == "act":
                        return nc.scalar.activation(dst, bank[:, 0:n], ACT.Copy)
                    return nc.vector.tensor_copy(dst, bank[:, 0:n])
                read_bank(eng, cur, (who == "act") == (c % 2 == 0), op)

        def main_norm_pe(pe, cur, n, split=True):
            b = cur.bank()
            if cur.g >= 4:
                pe.wait_ge(bank_free[b], cur.bank_use())
            for c in range(DC):
                if c % 4 == 0:
                    pe.wait_ge(norm_sq, cur.base("sq") + c // 4 + 1)
                last = nc.tensor.matmul(ps[:, b, 0:n], ones, SQ[:, c, 0:n], start=(c == 0), stop=(c == DC - 1))
            last.then_inc(bank_full[b], 1)
            cur.g += 1
            cur.add("sq", 2)
            cur.add("x", DC * n // T if split else 0)

        def main_norm_act(act, cur, steps, n, shift=None, split=True):
            for h in range(2):
                c = slice(4 * h, 4 * h + 4)
                nc.scalar.activation(SQ[:, c, 0:n], XT[:, c, 0:n], ACT.Square).then_inc(norm_sq, 1)
            g = cur.g
            act.wait_ge(bank_free[g % 4], g // 4 + 1)
            nc.scalar.activation(RB[:, 0:n], RB[:, 0:n], ACT.Sqrt).then_inc(norm_sd, 1)
            skip_banks(cur, 1)
            for st in range(n // T):
                for c in range(DC):
                    tok = slice(st * T, (st + 1) * T)
                    if split or shift:
                        act.wait_ge(normed, cur.base("normed") + 1)
                    if split and shift:
                        nc.scalar.activation(AH[:, c, tok], HF[:, c, tok], ACT.Identity, bias=shift(c, st))\
                            .then_inc(x_hi, 1)
                    elif split:
                        nc.scalar.activation(AH[:, c, tok], HF[:, c, tok], ACT.Copy).then_inc(x_hi, 1)
                    elif shift:
                        nc.scalar.activation(HF[:, c, tok], HF[:, c, tok], ACT.Identity, bias=shift(c, st))
                    cur.add("normed", 1)
            cur.add("x", DC * n // T if split else 0)

        def main_norm_dve(dve, cur, steps, n, gain, shift=None, split=True):
            read_bank(dve, cur, True, lambda bank: nc.vector.tensor_scalar(
                RB[:, 0:n], bank[:, 0:n], 1.0 / D, EPS, ALU.mult, ALU.add))
            dve.wait_ge(norm_sd, cur.base("sd") + 1)
            steps(nc.vector.reciprocal(RB[:, 0:n], RB[:, 0:n]))
            chunks = [(st, c, slice(st * T, (st + 1) * T)) for st in range(n // T) for c in range(DC)]
            for st, c, tok in chunks:
                nc.vector.scalar_tensor_tensor(HF[:, c, tok], XT[:, c, tok], gain(c, st), RB[:, tok],
                                               ALU.mult, ALU.mult).then_inc(normed, 1)
            if split:
                for st, c, tok in chunks:
                    dve.wait_ge(x_hi, cur.base("x") + 1)
                    if shift:
                        nc.vector.scalar_tensor_tensor(AL[:, c, tok], HF[:, c, tok], shift(c, st), f32(AH[:, c, tok]),
                                                       ALU.add, ALU.subtract).then_inc(x_lo, 1)
                    else:
                        nc.vector.tensor_tensor(AL[:, c, tok], HF[:, c, tok], f32(AH[:, c, tok]), ALU.subtract)\
                            .then_inc(x_lo, 1)
                    cur.add("x", 1)
            cur.add("sd", 1)

        def head_norm(x, groups, n, width, gain, stationary, post=1.0):
            chunks = sum(len(g) for g in groups)
            return dict(x=x[:, :, 0:n], sq=wk(0, chunks, n), rb=RB[:, 0:len(groups) * n], groups=groups, n=n,
                        width=width, gain=gain, stationary=stationary, post=post)

        def head_norm_pe(pe, cur, h):
            pe.wait_ge(norm_sq, cur.base("sq") + 1)
            for g in h["groups"]:
                bank_parts(pe, cur, [(P, 0, h["n"], [(h["stationary"], h["sq"][:, c, :]) for c in g])])
            cur.add("sq", 1)

        def head_norm_act(act, cur, steps, h):
            nc.scalar.activation(h["sq"], h["x"], ACT.Square).then_inc(norm_sq, 1)
            skip_banks(cur, len(h["groups"]))
            act.wait_ge(bank_free[(cur.g - 1) % 4], (cur.g - 1) // 4 + 1)
            nc.scalar.activation(h["rb"], h["rb"], ACT.Sqrt).then_inc(norm_sd, 1)

        def head_norm_dve(dve, cur, steps, h):
            n, post = h["n"], h["post"]
            for j in range(len(h["groups"])):
                read_bank(dve, cur, True, lambda bank, j=j: nc.vector.tensor_scalar(
                    h["rb"][:, j * n:(j + 1) * n], bank[:, 0:n], 1.0 / (h["width"] * post * post), EPS / (post * post),
                    ALU.mult, ALU.add))
            dve.wait_ge(norm_sd, cur.base("sd") + 1)
            steps(nc.vector.reciprocal(h["rb"], h["rb"]))
            for j, group in enumerate(h["groups"]):
                for c in group:
                    x = h["x"][:, c, :]
                    nc.vector.scalar_tensor_tensor(x, x, h["gain"](c), h["rb"][:, j * n:(j + 1) * n],
                                                   ALU.mult, ALU.mult)
            cur.add("sd", 1)

        each = [[c] for c in range(DC)]
        pairs = [[2 * j, 2 * j + 1] for j in range(DC // 2)]
        fox_q_norm = head_norm(QT, each, T, HD, lambda c: p1("fox_q_g"), cst("pair_ones"), post=HD ** -0.5)
        fox_k_norm = head_norm(KT, each, T, HD, lambda c: p1("fox_k_g"), cst("pair_ones"))
        mem_q_norm = head_norm(QT, pairs, T, 256, lambda c: p1("mem_q_g", c % 2), ones, post=256 ** -0.5)
        mem_k_norm = head_norm(KT, pairs, T, 256, lambda c: p1("mem_k_g", c % 2), ones)

        def qkv_pe(pe, cur, kq=0, kk=0, kv=0):
            fm_banks(pe, cur, in_a(kq)(T), T, DC)
            fm_banks(pe, cur, in_a(kk)(T), T, DC)
            for _ in range(2):
                tm_tile(pe, cur, kv, TT)

        def qkv_read(eng, who, cur, q_scale=1.0):
            for dst, scale in ((QT, q_scale), (KT, 1.0)):
                for h in range(2):
                    copies(eng, who, cur, lambda j, h=h, dst=dst: dst[:, 4 * h + j, :], 4, T, scale)
            for h in range(2):
                copies(eng, who, cur, lambda j, h=h: VT[:, j, h * 512:(h + 1) * 512], TT, 512, tm=True)


        def forget_pe(pe, cur):
            wf = p1("w_forget", 0, DC * 16).rearrange("p (k h) -> p k h", k=DC)
            bank_parts(pe, cur, [(16, 0, T, [(wf[:, k, :], HF[:, k, 0:T]) for k in range(DC)])])

        def forget_act(act, cur, steps):
            skip_banks(cur, 1)
            act.wait_ge(fox_z, 1)
            steps(nc.scalar.activation(FG[0:16, 1, :], FG[0:16, 0, :], ACT.Abs))
            steps(nc.scalar.activation(FG[0:16, 1, :], FG[0:16, 1, :], ACT.Exp, scale=-1.0))
            nc.scalar.activation(FG[0:16, 1, :], FG[0:16, 1, :], ACT.Ln, bias=1.0).then_inc(fox_e, 1)

        def forget_dve(dve, cur, steps):
            read_bank(dve, cur, True, lambda bank: nc.vector.tensor_scalar(
                FG[0:16, 0, :], bank[0:16, 0:T], p1("b_forget")[0:16], None, ALU.add))
            steps(nc.vector.memset(FG[0:16, 3, :], 1.0))
            dve.wait_ge(bank_free[(cur.g - 1) % 4], (cur.g - 1) // 4 + 1)
            dve.drain().then_inc(fox_z, 1)
            dve.wait_ge(fox_e, 1)
            steps(nc.vector.scalar_tensor_tensor(FG[0:16, 2, :], FG[0:16, 0, :], 0.0, FG[0:16, 1, :],
                                                 ALU.min, ALU.subtract))
            nc.vector.tensor_tensor_scan(FG[0:16, 0, :], FG[0:16, 3, :], FG[0:16, 2, :], 0.0, ALU.mult, ALU.add)\
                .then_inc(fox_cum, 1)

        def forget_pool(pool, cur):
            pool.wait_ge(fox_cum, 1)
            pool.dma_start(a["cum_scratch"], FG[0:16, 0, :]).then_inc(loads, 16)
            pool.wait_ge(loads, 16 * LOADS["cum_out"])
            src = a["cum_scratch"].rearrange("h t -> (h t)").partition_broadcast(P)
            pool.dma_start(CUM.rearrange("p h t -> p (h t)"), src).then_inc(loads, 16)
            pool.wait_ge(loads, 16 * LOADS["cum_in"])

        def fox_bias(r, s4, steps, t):
            mask = cst("causal").rearrange("p (a b k) -> p a b k", a=1, b=2).to_broadcast([P, 2, 2, T])
            steps(nc.vector.tensor_tensor(t, s4[:, :, :, 0:T], mask, ALU.add))
            cum = CUM[:, 2 * r:2 * r + 2, :].unsqueeze(2).to_broadcast([P, 2, 2, T])
            steps(nc.vector.tensor_tensor(t, t, cum, ALU.subtract))

        fox = pair_att(HEADS // 2, T, QT, 0, KT, 0, VT, 0, YT[:, 0], 0, bias=fox_bias)

        def mem_qk(r, a_, qt):
            c = 4 * r + 2 * a_
            return [(QT[:, c + j, qt * P:(qt + 1) * P], KT[:, c + j, :]) for j in range(2)]

        def mem_pv(r):
            return [(a_ if d == 0 else 2, slice(0, P), (2 * a_ + d) * T, [(VT[:, k, (4 * r + 2 * a_ + d) * P:(4 * r + 2 * a_ + d + 1) * P],
                                         pt_all[:, a_, k, :]) for k in range(2)])
                    for a_ in range(2) for d in range(2)]

        def mem_save(r):
            return (YT[:, 3, 4 * r:4 * r + 4, :].rearrange("p (b c) t -> p b (c t)", b=2), ps[:, 6:8, :])

        mem_att = dict(n=2, nk=T, diff=False, bias=None, qk=mem_qk, pv=mem_pv, save=mem_save)

        SB_Z, SB_L, SB_LN, SB_W = ([wk(at, 2, 2, T), wk(at + 1024, 2, 2, T)] for at in (0, 2048, 4096, SPARE))
        z_ps = [ps[:, b:b + 2, :].rearrange("p a (k t) -> p a k t", k=2) for b in (0, 2)]
        incl_ps = ps[:, 4:6, :].rearrange("p a (k t) -> p a k t", k=2)
        SB_ROUNDS = HEADS // 2

        def sb_pe(pe, cur):
            def scores(r):
                pe.wait_ge(sb_l, CREDIT + r - 1)
                for a in range(2):
                    h = slice(64 * a, 64 * a + 64)
                    for kt in range(2):
                        last = nc.tensor.matmul(z_ps[r % 2][:, a, kt, :], KT[h, r, kt * P:(kt + 1) * P], QT[h, r, :],
                                                start=True, stop=True)
                last.then_inc(sb_z, 1)

            scores(0)
            scores(1)
            for r in range(SB_ROUNDS):
                L, W = SB_L[r % 2], SB_W[r % 2]
                pe.wait_ge(sb_l, CREDIT + r + 1)
                pe.wait_ge(sb_logw, CREDIT + r)
                for a in range(2):
                    nc.tensor.matmul(incl_ps[:, a, 0, :], cst("tri"), L[:, a, 0, :], start=True, stop=False)
                    nc.tensor.matmul(incl_ps[:, a, 0, :], ones, L[:, a, 1, :], start=False, stop=True)
                    last = nc.tensor.matmul(incl_ps[:, a, 1, :], cst("tri"), L[:, a, 1, :], start=True, stop=True)
                last.then_inc(sb_incl, 1)
                if r + 2 < SB_ROUNDS:
                    scores(r + 2)
                pe.wait_ge(sb_w, CREDIT + r + 1)
                pe.wait_ge(sb_saved, CREDIT + r - 1)
                for a in range(2):
                    for kt in range(2):
                        last = nc.tensor.matmul(ps[64 * a:64 * a + 64, 6 + r % 2, 0:T],
                                                VT[:, kt, r * P + 64 * a:r * P + 64 * a + 64], W[:, a, kt, :],
                                                start=(kt == 0), stop=(kt == 1))
                last.then_inc(sb_y, 1)

        def sb_act(act, cur, steps):
            def softplus(r):
                LN = SB_LN[r % 2]
                act.wait_ge(sb_z, CREDIT + r + 1)
                act.wait_ge(sb_l, CREDIT + r - 1)
                nc.scalar.activation(LN, z_ps[r % 2], ACT.Abs).then_inc(sb_abs, 1)
                act.wait_ge(sb_abs, CREDIT + r + 1)
                steps(nc.scalar.activation(LN, LN, ACT.Exp, scale=-1.0))
                nc.scalar.activation(LN, LN, ACT.Ln, bias=1.0).then_inc(sb_ln, 1)

            def save(r):
                act.wait_ge(sb_y, CREDIT + r + 1)
                nc.scalar.activation(YT[:, 2, r, :], ps[:, 6 + r % 2, 0:T], ACT.Copy).then_inc(sb_saved, 1)

            softplus(0)
            for r in range(SB_ROUNDS):
                if r + 1 < SB_ROUNDS:
                    softplus(r + 1)
                act.wait_ge(sb_logw, CREDIT + r + 1)
                act.wait_ge(sb_y, CREDIT + r - 1)
                nc.scalar.activation(SB_W[r % 2], SB_Z[r % 2], ACT.Exp).then_inc(sb_w, 1)
                if r > 0:
                    save(r - 1)
            save(SB_ROUNDS - 1)

        def sb_dve(dve, cur, steps):
            add = cst("sb_add").rearrange("p (a k t) -> p a k t", a=1, k=2).to_broadcast([P, 2, 2, T])
            neg = cst("sb_neg").rearrange("p (a k t) -> p a k t", a=1, k=2).to_broadcast([P, 2, 2, T])
            flat = lambda x: x.rearrange("p a k t -> p (a k t)")

            def logs(r):
                Z, L, z = SB_Z[r % 2], SB_L[r % 2], z_ps[r % 2]
                dve.wait_ge(sb_w, CREDIT + r - 1)
                dve.wait_ge(sb_abs, CREDIT + r + 1)
                steps(nc.vector.tensor_tensor(Z, z, add, ALU.add))
                dve.wait_ge(sb_ln, CREDIT + r + 1)
                dve.wait_ge(sb_incl, CREDIT + r - 1)
                steps(nc.vector.scalar_tensor_tensor(flat(L), flat(z), 0.0, flat(SB_LN[r % 2]), ALU.max, ALU.add))
                nc.vector.tensor_tensor(L, L, neg, ALU.mult).then_inc(sb_l, 1)

            logs(0)
            for r in range(SB_ROUNDS):
                if r + 1 < SB_ROUNDS:
                    logs(r + 1)
                Z = SB_Z[r % 2]
                dve.wait_ge(sb_incl, CREDIT + r + 1)
                nc.vector.tensor_tensor(Z, Z, incl_ps, ALU.add).then_inc(sb_logw, 1)

        LX, LG, LXC, LR, LI, LA = (wk(2048 * j, DC, T) for j in range(6))
        LW = wk(18688, 2, DC, P)
        LY = YT[:, 1]
        sp8 = small[:, 16:24]

        def lru_pe(pe, cur):
            pe.wait_ge(loads, 16 * LOADS["lru_w"])
            for c in range(DC):
                pe.wait_ge(lru_xc, c + 1)
                bank_parts(pe, cur, [(P, g * T, T, [(LW[:, g, c, :], LXC[:, c, :])]) for g in range(2)])

        def lru_act(act, cur, steps):
            tmp = small[:, 24:32]
            steps(nc.scalar.activation(tmp, p1("lam", 0, DC), ACT.Abs))
            steps(nc.scalar.activation(tmp, tmp, ACT.Exp, scale=-1.0))
            nc.scalar.activation(tmp, tmp, ACT.Ln, bias=1.0).then_inc(lru_ri, 1)
            for c in range(DC):
                def op(bank, c=c):
                    nc.scalar.activation(LR[:, c, :], bank[:, 0:T], ACT.Sigmoid, bias=p1("b_a", c))
                    return nc.scalar.activation(LI[:, c, :], bank[:, T:2 * T], ACT.Sigmoid, bias=p1("b_x", c))
                read_bank(act, cur, True, op)
            act.drain().then_inc(lru_gates, 1)
            act.wait_ge(lru_om, 1)
            nc.scalar.activation(LA[:, :, :], LR[:, :, :], ACT.Exp).then_inc(lru_a, 1)
            steps(nc.scalar.activation(LR[:, :, :], LR[:, :, :], ACT.Tanh, scale=-1.0))
            act.drain().then_inc(lru_a, 1)
            act.wait_ge(lru_om, 2)
            nc.scalar.activation(LR[:, :, :], LR[:, :, :], ACT.Sqrt).then_inc(lru_root, 1)

        def lru_dve(dve, cur, steps):
            nlm = small[:, 32:40]
            steps(nc.vector.tensor_scalar(nlm, p1("lam", 0, DC), -1.0, 0.0, ALU.mult, ALU.max))
            dve.wait_ge(lru_ri, 1)
            steps(nc.vector.tensor_tensor(sp8, nlm, small[:, 24:32], ALU.add))
            steps(nc.vector.tensor_scalar(sp8, sp8, -LRU_C, None, ALU.mult))
            for c in range(DC):
                steps(nc.vector.tensor_scalar(LXC[:, c, :], LX[:, c, :], p1("conv_w", 3 * DC + c),
                                              p1("conv_b", c), ALU.mult, ALU.add))
                for j in range(1, 4):
                    ins = nc.vector.scalar_tensor_tensor(
                        LXC[:, c, j:T], LX[:, c, 0:T - j], p1("conv_w", (3 - j) * DC + c), LXC[:, c, j:T],
                        ALU.mult, ALU.add)
                    if j < 3:
                        steps(ins)
                ins.then_inc(lru_xc, 1)
            skip_banks(cur, DC)
            dve.wait_ge(lru_gates, 1)
            for c in range(DC):
                ins = nc.vector.tensor_scalar(LR[:, c, :], LR[:, c, :], sp8[:, c:c + 1], None, ALU.mult)
            ins.then_inc(lru_om, 1)
            dve.wait_ge(lru_xc, DC)
            steps(nc.vector.tensor_tensor(LI[:, :, :], LI[:, :, :], LXC[:, :, :], ALU.mult))
            dve.wait_ge(lru_a, 2)
            steps(nc.vector.tensor_tensor(LXC[:, :, :], LA[:, :, :], LA[:, :, :], ALU.mult))
            flat = lambda x: x.rearrange("p a t -> p (a t)")
            nc.vector.scalar_tensor_tensor(flat(LR), flat(LXC), 1.0, flat(LR), ALU.add, ALU.mult)\
                .then_inc(lru_om, 1)
            dve.wait_ge(lru_root, 1)
            steps(nc.vector.tensor_tensor(LI[:, :, :], LI[:, :, :], LR[:, :, :], ALU.mult))
            for c in range(DC):
                ins = nc.vector.tensor_tensor_scan(LXC[:, c, :], LA[:, c, :], LI[:, c, :], 0.0, ALU.mult, ALU.add)
            steps(ins)
            steps(nc.vector.tensor_tensor(LY, LXC[:, :, :], LG[:, :, :], ALU.mult))

        def merge_loop(eng, cur, branches, kc, one_branch, steps=None, per=0):
            if 2 * (4 + kc // 2) % (2 * R) == 0:
                with loop(eng, cur, branches, pieces=2 * (4 + kc // 2), banks=16, steps=steps, steps_per=per) as i:
                    one_branch(i)
            else:
                for i in range(branches):
                    one_branch(i)

        def y_split(kc, n):
            v = WKR[:, 6400:6400 + 4096].rearrange("p (s k t) -> p s k t", s=2, k=kc)
            return v[:, 0, :, 0:n], v[:, 1, :, 0:n]

        def merge_pe(pe, cur, branches, kc, n):
            yh, yl = y_split(kc, n)

            def one_branch(i):
                for h in range(2):
                    fm_banks(pe, cur, in_a()(n), n, 4)
                    if h == 0:
                        pe.wait_ge(y_lo, cur.base("y") + 1 + i)
                    fm_banks(pe, cur, lambda k: (yh[:, k, :], yl[:, k, :]), n, 4, kc)
            merge_loop(pe, cur, branches, kc, one_branch)
            cur.add("y", branches)

        def merge_act(act, cur, branches, kc, n, y, bias):
            yh, _ = y_split(kc, n)

            def one_branch(i):
                for h in range(2):
                    act.wait_ge(gate_used, cur.base("merge") + 1 + h + i * 2)
                    if h == 0:
                        nc.scalar.activation(yh, y[:, one(i), :, 0:n].squeeze(1), ACT.Copy).then_inc(y_hi, 1)
                    for j in range(4):
                        def op(bank, j=j):
                            b = {} if bias is None else {"bias": bias(i, 4 * h + j)}
                            return nc.scalar.activation(GATE[:, j, 0:n], bank[:, 0:n], ACT.Sigmoid, **b)
                        read_bank(act, cur, True, op, piece=True)
                    skip_fm(act, cur, 4, kc)
            merge_loop(act, cur, branches, kc, one_branch)
            cur.add("merge", 2 * branches + 1)

        def merge_dve(dve, cur, steps, branches, kc, n, y):
            yh, yl = y_split(kc, n)
            steps(nc.vector.memset(MIXT[:, :, 0:n], 0.0))
            dve.drain().then_inc(gate_used, 1)
            cur.add("merge", 1)

            def one_branch(i):
                dve.wait_ge(y_hi, cur.base("y") + 1 + i)
                nc.vector.tensor_tensor(yl, y[:, one(i), :, 0:n].squeeze(1), f32(yh), ALU.subtract).then_inc(y_lo, 1)
                for h in range(2):
                    skip_fm(dve, cur, 4)
                    dve.wait_ge(bank_free[(cur.g + 3) % 4], cur.bank_use(-1 if cur.g % 4 == 0 else 0) + 1)
                    for j in range(4):
                        def op(bank, j=j):
                            steps(nc.vector.tensor_tensor(GATE[:, j, 0:n], GATE[:, j, 0:n], bank[:, 0:n], ALU.mult))
                            m = MIXT[:, 4 * h + j, 0:n]
                            return nc.vector.tensor_tensor(m, m, GATE[:, j, 0:n], ALU.add)
                        read_bank(dve, cur, True, op, piece=(kc == DC or j % 2 == 1))
                    dve.drain().then_inc(gate_used, 1)
            merge_loop(dve, cur, branches, kc, one_branch, steps=steps, per=8)
            cur.add("merge", 2 * branches)
            cur.add("y", branches)

        def out_pe(pe, cur, n):
            def ready(k):
                if k % 4 == 0:
                    pe.wait_ge(x_lo, cur.base("x") + k // 4 + 1)
            fm_banks(pe, cur, in_a()(n), n, DC, ready=ready)
            cur.add("x", 2)

        def out_act(act, cur, n):
            split_x_act(act, cur, [(MIXT[:, c:c + 4, 0:n], AH[:, c:c + 4, 0:n]) for c in (0, 4)])
            skip_fm(act, cur, DC)

        def out_dve(dve, cur, n, gain=None):
            split_x_dve(dve, cur, [(MIXT[:, c:c + 4, 0:n], AH[:, c:c + 4, 0:n], AL[:, c:c + 4, 0:n]) for c in (0, 4)])
            for h in range(2):
                for j in range(4):
                    c = 4 * h + j
                    def op(bank, c=c):
                        if gain is None:
                            return nc.vector.tensor_tensor(XT[:, c, 0:n], XT[:, c, 0:n], bank[:, 0:n], ALU.add)
                        for st in range(n // T):
                            tok = slice(st * T, (st + 1) * T)
                            ins = nc.vector.scalar_tensor_tensor(XT[:, c, tok], bank[:, tok], gain(c, st),
                                                                 XT[:, c, tok], ALU.mult, ALU.add)
                        return ins
                    read_bank(dve, cur, True, op, piece=True)

        FG_RAW = wk(0, 2, T)
        FH = wk(512, FC, T)
        UPS = FC // 2

        def up_pe(pe, cur):
            def tile_(_):
                fm_banks(pe, cur, in_a()(T), T, 4)
            up_loop(pe, cur, tile_)

        def up_loop(eng, cur, tile_, steps=None, per=0):
            with loop(eng, cur, 2, pieces=16, banks=16, steps=steps, steps_per=4 * per) as i:
                for j in range(4):
                    tile_(i * 4 + j)
            for j in range(8, UPS):
                tile_(j)

        def up_act(act, cur, steps):
            def tile_(n):
                skip_fm(act, cur, 2)
                for j in range(2):
                    act.wait_ge(conv_done, 2 * n + j + 1)
                    f = FH[:, one(2 * n + j), :]
                    nc.scalar.activation(f, f, ACT.Silu).then_inc(silu_done, 1)
                skip_fm(act, cur, 2)
            up_loop(act, cur, tile_)

        def up_dve(dve, cur, steps):
            def par1(name, i):
                lo = PAR1[name][0] + i
                return par[:, lo:lo + 1] if isinstance(lo, int) else par[:, bass.ds(lo, 1)]

            def tile_(n):
                for j in range(2):
                    f = FH[:, one(2 * n + j), :].squeeze(1)
                    def op(bank, j=j):
                        return nc.vector.tensor_copy(FG_RAW[:, j, :], bank[:, 0:T])
                    read_bank(dve, cur, True, op, piece=True)
                for j in range(2):
                    f = FH[:, one(2 * n + j), :].squeeze(1)
                    if j == 0:
                        dve.drain().then_inc(raw_gates, 1)
                        dve.wait_ge(raw_gates, n + 1)
                    steps(nc.vector.tensor_scalar(f, FG_RAW[:, j, :], par1("ffn_w", 2 * FC + 2 * n + j),
                                                  par1("ffn_b", 2 * n + j), ALU.mult, ALU.add))
                    steps(nc.vector.scalar_tensor_tensor(f[:, 1:T], FG_RAW[:, j, 0:T - 1], par1("ffn_w", FC + 2 * n + j),
                                                         f[:, 1:T], ALU.mult, ALU.add))
                    nc.vector.scalar_tensor_tensor(f[:, 2:T], FG_RAW[:, j, 0:T - 2], par1("ffn_w", 2 * n + j),
                                                   f[:, 2:T], ALU.mult, ALU.add).then_inc(conv_done, 1)
                for j in range(2):
                    f = FH[:, one(2 * n + j), :].squeeze(1)
                    def op(bank, f=f):
                        return nc.vector.tensor_tensor(f, f, bank[:, 0:T], ALU.mult)
                    dve.wait_ge(silu_done, 2 * n + j + 1)
                    read_bank(dve, cur, True, op, piece=True)
            up_loop(dve, cur, tile_, steps=steps, per=4)

        FHR = WKR[:, 6400:6400 + 2 * FC * T].rearrange("p (s k t) -> p s k t", s=2, k=FC)
        FGROUPS = [slice(0, 4), slice(4, 10), slice(10, 16), slice(16, FC)]

        def down_pe(pe, cur):
            def ready(k):
                for n, group in enumerate(FGROUPS):
                    if k == group.start:
                        pe.wait_ge(x_lo, cur.base("x") + n + 1)
            fm_banks(pe, cur, lambda k: (FHR[:, 0, k, :], FHR[:, 1, k, :]), T, DC, FC, ready=ready)
            cur.add("x", len(FGROUPS))

        def down_read(eng, cur, read):
            for piece in range(FC):
                c = (piece * 8 + 8) // FC - 1
                both = (piece * 8 + 8) % FC == 0
                if (piece * 8 + 8) // FC > piece * 8 // FC:
                    read_bank(eng, cur, read is not None, read and read(c), piece=both)
                if not both:
                    next_piece(eng, cur)

        def down_act(act, cur):
            split_x_act(act, cur, [(FH[:, s, :], FHR[:, 0, s, :]) for s in FGROUPS])
            down_read(act, cur, None)

        def down_dve(dve, cur):
            split_x_dve(dve, cur, [(FH[:, s, :], FHR[:, 0, s, :], FHR[:, 1, s, :]) for s in FGROUPS])

            def read(c):
                return lambda bank: nc.vector.tensor_tensor(XT[:, c, 0:T], XT[:, c, 0:T], bank[:, 0:T], ALU.add)
            down_read(dve, cur, read)

        cs = small[:, 40:56].rearrange("p (k s) -> p k s", k=DC)
        AF = A.rearrange("p a k t -> p (a k t)")
        ROWS = wk(0, 4, 512)

        def split_place(at):
            v = AF[:, at:at + XS_WORDS].rearrange("p (k c) -> p k c", k=DC)
            return v[:, :, 0:64], v[:, :, 64:128]

        def stationary(at, k):
            at = at + k * XS_CHUNK
            return AF[:, at:at + P], AF[:, at + 64:at + 64 + P]

        CS_HI, CS_LO = split_place(0)

        def rows_tile(pe, cur, xs, bank):
            for j in range(4):
                hi, lo = piece_of(pe, cur)
                for q in range(2):
                    k, w = 2 * j + q, slice(q * 512, q * 512 + 512)
                    last = three(ps[:, bank, :], xs(k), (hi[:, w], lo[:, w]), k == 0, k == DC - 1)
                if j < 3:
                    last.then_inc(piece_used[(cur.p - 1) % 4], 1)
            return last

        def ada_pe(pe, cur):
            pe.wait_ge(split_c, cur.base("ada") + 1)
            with loop(pe, cur, 3, pieces=16, banks=8):
                rows_in = {}

                def product(j):
                    b = cur.bank()
                    if cur.g >= 4:
                        pe.wait_ge(bank_free[b], cur.bank_use())
                    rows_tile(pe, cur, lambda k: stationary(0, k), b).then_inc(bank_full[b], 1)
                    rows_in[j] = b, cur.bank_use(1)
                    cur.g += 1

                def turn(j):
                    b, use = rows_in[j]
                    pe.wait_ge(bank_free[b], use)
                    bank_parts(pe, cur, [(P, 2 * c, 2, [(ROWS[0:2, j, c * P:(c + 1) * P], ident[0:2, 0:2])])
                                         for c in range(4)])
                product(0)
                for j in range(1, 4):
                    product(j)
                    turn(j - 1)
                turn(3)
            cur.add("ada", 1)

        def ada_act(act, cur, layer):
            act.wait_ge(loads, 16 * LOADS["par"][layer])
            nc.scalar.activation(cs, p2("c", 0, 2 * DC).rearrange("p (k s) -> p k s", k=DC), ACT.Silu)\
                .then_inc(silu_c, 1)
            act.wait_ge(silu_c, 2 * cur.base("ada") + 1)
            nc.scalar.activation(CS_HI[:, :, 0:2], cs, ACT.Copy).then_inc(silu_c, 1)
            with loop(act, cur, 3, pieces=16, banks=8):
                for _ in range(16):
                    next_piece(act, cur)
                skip_banks(cur, 8)
            cur.add("ada", 1)

        def ada_dve(dve, cur, steps, layer):
            dve.wait_ge(loads, 16 * LOADS["par"][layer])
            dve.wait_ge(silu_c, 2 * cur.base("ada") + 2)
            nc.vector.tensor_tensor(CS_LO[:, :, 0:2], cs, f32(CS_HI[:, :, 0:2]), ALU.subtract).then_inc(split_c, 1)
            with loop(dve, cur, 3, pieces=16, banks=8) as i:
                def rows(j):
                    next_piece(dve, cur, 3)
                    read_bank(dve, cur, True, lambda bank: nc.vector.tensor_copy(ROWS[0:2, j, :], bank[0:2, :]),
                              piece=True)

                def add_bias(j):
                    def op(bank):
                        lo = i * 16 + 4 * j
                        b = par[:, bass.ds(lo + PAR2["b_ada"][0], 4)].unsqueeze(2).to_broadcast([P, 4, 2])
                        return nc.vector.tensor_tensor(MOD[:, bass.ds(lo, 4), :],
                                                       bank[:, 0:8].rearrange("p (c s) -> p c s", c=4), b, ALU.add)
                    read_bank(dve, cur, True, op)
                rows(0)
                for j in range(1, 4):
                    rows(j)
                    add_bias(j - 1)
                add_bias(3)
            cur.add("ada", 1)

        def gmod_dve(dve, steps, g, which):
            gb = p2(g, 0, DC).unsqueeze(2).to_broadcast([P, DC, 2])
            steps(nc.vector.tensor_scalar(gmod[:, :, :], MOD[:, which * DC:(which + 1) * DC, :], 1.0, None, ALU.add))
            steps(nc.vector.tensor_tensor(gmod[:, :, :], gmod[:, :, :], gb, ALU.mult))

        def proj2_pe(pe, cur, nq):
            fm_banks(pe, cur, in_a()(nq), nq, BC)
            fm_banks(pe, cur, in_a()(2 * T), 2 * T, BC)
            tm_tile(pe, cur, 0, 4)

        def proj2_read(eng, who, cur, nq):
            copies(eng, who, cur, lambda j: Q2[:, j, 0:nq], 4, nq, HD ** -0.5)
            copies(eng, who, cur, lambda j: K2[:, j, :], 4, 2 * T)
            copies(eng, who, cur, lambda j: V2[:, j, :], 4, BW, tm=True)

        def na_bias(r, s4, steps, t):
            steps(nc.vector.tensor_tensor(t[:, :, :, 0:T], s4[:, :, :, 0:T], NAB[:, r], ALU.add))
            steps(nc.vector.tensor_copy(t[:, :, :, T:2 * T], s4[:, :, :, T:2 * T]))

        na_x = pair_att(4, 2 * T, Q2, 0, K2, 0, V2, 0, Y2[:, 0], 0, bias=na_bias)
        na_ctx = pair_att(4, T, Q2, T, K2, T, V2, 2, Y2[:, 0], T)
        da_x = pair_att(4, 2 * T, Q2, 0, K2, 0, V2, 0, Y2[:, 1], 0, diff=True)
        da_ctx = pair_att(4, T, Q2, T, K2, T, V2, 2, Y2[:, 1], T, diff=True)

        ROT = wk(0, BC, T)

        def rope_pe(pe, cur):
            for x in (Q2, K2):
                for c in range(BC):
                    bank_parts(pe, cur, [(P, 0, T, [(cst("swap"), x[:, c, 0:T])])])

        def rope_dve(dve, cur, steps):
            for x in (Q2, K2):
                for c in range(BC):
                    def op(bank, c=c):
                        return nc.vector.tensor_tensor(ROT[:, c, :], bank[:, 0:T], cst("sin"), ALU.mult)
                    read_bank(dve, cur, True, op)
                dve.drain().then_inc(rope_r, 1)
                cur.add("rope", 1)
                dve.wait_ge(rope_r, cur.base("rope"))
                cos = cst("cos").unsqueeze(1).to_broadcast([P, BC, T])
                steps(nc.vector.tensor_tensor(x[:, :, 0:T], x[:, :, 0:T], cos, ALU.mult))
                steps(nc.vector.tensor_tensor(x[:, :, 0:T], x[:, :, 0:T], ROT, ALU.add))

        lamp = small[:, 56:58]

        def lam_pe(pe, cur):
            pe.wait_ge(lam_prod, cur.base("lam") * 2 + 1)
            bank_parts(pe, cur, [(P, 0, 2, [(ones, lamp)])])
            cur.add("lam", 1)

        def lam_act(act, cur):
            read_bank(act, cur, True, lambda bank: nc.scalar.activation(small[:, 58:60], bank[:, 0:2], ACT.Exp))

        def lam_dve(dve, cur, steps, lam_init):
            nc.vector.tensor_tensor(lamp, p2("lam_q", 0, 2), p2("lam_k", 0, 2), ALU.mult).then_inc(lam_prod, 1)
            cur.g += 1
            b = (cur.g - 1) % 4
            dve.wait_ge(bank_free[b], (cur.g - 1) // 4 + 1)
            steps(nc.vector.tensor_tensor(nlam, small[:, 59:60], small[:, 58:59], ALU.subtract))
            steps(nc.vector.tensor_scalar(nlam, nlam, -lam_init, None, ALU.add))
            dve.drain().then_inc(lam_prod, 1)

        def da_norm(n, lam_init):
            return head_norm(Y2[:, 1], [[c] for c in range(BC)], n, P, lambda c: p2("subln"), ones, post=1.0 - lam_init)

        GU, GV = wk(0, 4, BW), wk(2048, 4, BW)
        GWS = wk(6400, 4, P)
        GLN = wk(6400 + 512, 2, BW)
        GST = wk(6400 + 1536, 4, 8)

        def gmlp_proj_pe(pe, cur, tt):
            tm_tile(pe, cur, 0, tt)
            tm_tile(pe, cur, 0, tt)

        def gmlp_proj_read(eng, who, cur, tt):
            copies(eng, who, cur, lambda j: GU[:, j, :], tt, BW, func=ACT.Gelu_apprx_tanh, tm=True)
            copies(eng, who, cur, lambda j: GV[:, j, :], tt, BW, func=ACT.Gelu_apprx_tanh, tm=True)

        def gmlp_ln_dve(dve, cur, steps, tt, layer):
            for m in range(tt):
                steps(nc.vector.bn_stats(GST[:, m, 0:6], GV[:, m, :]))
                steps(nc.vector.bn_aggr(GST[:, m, 6:8], GST[:, m, 0:6]))
            var = GST[:, 0:tt, 7:8]
            nc.vector.tensor_scalar(var, var, EPS, None, ALU.add).then_inc(ln_var, 1)
            dve.wait_ge(ln_sd, layer + 1)
            steps(nc.vector.reciprocal(var, var))
            dve.wait_ge(loads, 16 * LOADS["ln"][layer])
            for m in range(tt):
                v = GV[:, m, :]
                steps(nc.vector.tensor_scalar(v, v, GST[:, m, 6:7], GST[:, m, 7:8], ALU.subtract, ALU.mult))
                steps(nc.vector.tensor_tensor(v, v, GLN[:, 0, :], ALU.mult))
                ins = nc.vector.tensor_tensor(v, v, GLN[:, 1, :], ALU.add)
            ins.then_inc(ln_done, 1)

        def gmlp_ln_act(act, tt, layer):
            act.wait_ge(ln_var, layer + 1)
            var = GST[:, 0:tt, 7:8]
            nc.scalar.activation(var, var, ACT.Sqrt).then_inc(ln_sd, 1)

        def gmlp_mix_pe(pe, cur, tt, layer):
            pe.wait_ge(loads, 16 * LOADS["ln"][layer])
            pe.wait_ge(ln_done, layer + 1)
            for m in range(tt):
                bank_parts(pe, cur, [(P, g * P, P, [(GWS[:, g, :], GV[:, m, g * P:(g + 1) * P])]) for g in range(4)])
            for m in range(tt):
                g = cur.g - tt
                pe.wait_ge(bank_free[g % 4], g // 4 + 1)
                bank_parts(pe, cur, [(P, c * P, P, [(GU[:, m, c * P:(c + 1) * P], ident)]) for c in range(BC)], turn=True)

        def gmlp_mix_dve(dve, cur, steps, tt):
            for m in range(tt):
                def op(bank, m=m):
                    for g in range(4):
                        u = GU[:, m, g * P:(g + 1) * P]
                        ins = nc.vector.scalar_tensor_tensor(u, bank[:, g * P:(g + 1) * P], p2("b_s", g), u,
                                                             ALU.add, ALU.mult)
                    return ins
                read_bank(dve, cur, True, op)
            skip_banks(cur, tt)

        def gmlp_mix_act(act, cur, tt):
            skip_banks(cur, tt)
            for m in range(tt):
                read_bank(act, cur, True, lambda bank, m=m: nc.scalar.activation(
                    Y2[:, 2, :, m * P:(m + 1) * P], bank.rearrange("p (c t) -> p c t", c=BC), ACT.Copy))

        XIN = wk(0, DC, 2, EXPERTS * CAP)
        YE = wk(8192, 2, 4, D)
        H2 = wk(8192, 4, D)
        GT = wk(16384, 2, 4, T)
        PH = wk(18432, 4, EXPERTS * CAP)
        AFF = small[:, 0:64].rearrange("p (m e) -> p m e", m=4)
        XS_AT = [0, XS_WORDS]
        HIDT_AT = 2 * XS_WORDS
        HIDT_HI, HIDT_LO = split_place(HIDT_AT)
        SG, HID = wk(18432, 2, 512), wk(18432 + 1024, 2, 512)
        CMP, RANKS, AUX = wk(16384, 2, 8, T), wk(4096, 2, 4, EXPERTS), wk(4224, 8)
        AFFT = rowst

        def route_pe(pe, cur, st):
            tt = 2 * st
            wr = p2("w_router", 0, DC * 16).rearrange("p (k e) -> p k e", k=DC)
            bank_parts(pe, cur, [(P, m * 16, 16, [(HF[:, k, m * P:(m + 1) * P], wr[:, k, :]) for k in range(DC)])
                                 for m in range(tt)])
            for m in range(tt):
                for h in range(2):
                    bank_parts(pe, cur, [(P, c * P, P, [(HF[:, 4 * h + c, m * P:(m + 1) * P], ident)])
                                         for c in range(4)], turn=True)
            pe.wait_ge(affinities, cur.base("route") + 1)
            bank_parts(pe, cur, [(16, m * P, P, [(AFF[:, m, :], ident)]) for m in range(tt)], turn=True)
            g = cur.g - 1
            pe.wait_ge(bank_free[g % 4], g // 4 + 1)
            for e in range(EXPERTS):
                bank_parts(pe, cur, [(P, 0, st * T, [(sel[:, e, :], AFFT[:, 0:st * T])])])
            pe.wait_ge(onehot, 2 * cur.base("route") + 1)
            for s in range(st):
                for c in range(DC):
                    bank_parts(pe, cur, [(P, 0, 512, [(H2[:, 2 * s + m, c * P:(c + 1) * P], PH[:, 2 * s + m, :])
                                                      for m in range(2)])])
            pe.wait_ge(onehot, 2 * cur.base("route") + 2)
            for s in range(st):
                for half in range(2):
                    bank_parts(pe, cur, [(P, g_ * T + m * P, P, [(PH[:, 2 * s + m, (2 * half + g_) * P:(2 * half + g_ + 1) * P], ident)])
                                         for g_ in range(2) for m in range(2)], turn=True)
            cur.add("route", 1)

        def route_act(act, cur, steps, st):
            tt = 2 * st
            act.wait_ge(aff_logits, cur.base("route") + 1)
            skip_banks(cur, 1)
            nc.scalar.activation(AFF[:, 0:tt, :], AFF[:, 0:tt, :], ACT.Exp).then_inc(aff_exp, 1)
            for m in range(tt):
                for h in range(2):
                    read_bank(act, cur, True, lambda bank, m=m, h=h: nc.scalar.activation(
                        H2[:, m, h * 512:(h + 1) * 512], bank, ACT.Copy))
            read_bank(act, cur, True, lambda bank: nc.scalar.activation(AFFT[:, 0:st * T], bank[0:16, 0:st * T], ACT.Copy))
            skip_banks(cur, EXPERTS)
            for s in range(st):
                for c in range(DC):
                    read_bank(act, cur, c % 2 == 0, lambda bank, s=s, c=c: nc.scalar.activation(XIN[:, c, s, :], bank, ACT.Copy))
            for s in range(st):
                for half in range(2):
                    read_bank(act, cur, True, lambda bank, s=s, half=half: nc.scalar.activation(
                        GT[:, s, 2 * half:2 * half + 2, :], bank.rearrange("p (g t) -> p g t", g=2), ACT.Copy))
            cur.add("route", 1)

        def route_dve(dve, cur, steps, st):
            tt = 2 * st
            aff = AFF[:, 0:tt, :]
            aux = AUX[:, 0:tt]
            wide = lambda x: x.unsqueeze(2).to_broadcast([P, tt, 16])
            g = cur.g
            dve.wait_ge(bank_full[g % 4], g // 4 + 1)
            lg = ps[:, g % 4, 0:16 * tt].rearrange("p (m e) -> p m e", m=tt)
            steps(nc.vector.tensor_reduce(aux, lg, AX.X, ALU.max))
            read_bank(dve, cur, True, lambda bank: nc.vector.tensor_tensor(aff, lg, wide(aux), ALU.subtract))
            dve.drain().then_inc(aff_logits, 1)
            dve.wait_ge(aff_exp, cur.base("route") + 1)
            steps(nc.vector.tensor_reduce(aux, aff, AX.X, ALU.add))
            steps(nc.vector.reciprocal(aux, aux))
            nc.vector.tensor_tensor(aff, aff, wide(aux), ALU.mult).then_inc(affinities, 1)
            dve.wait_ge(affinities, cur.base("route") + 1)
            skip_banks(cur, 2 * tt + 1)
            before = cst("before").rearrange("p (m t) -> p m t", m=2)
            for e in range(EXPERTS):
                if e >= 2:
                    dve.wait_ge(bank_free[(cur.g - 2) % 4], (cur.g - 2) // 4 + 1)

                def op(bank, e=e):
                    for s in range(st):
                        for m in range(2):
                            row, av = bank[:, s * T:(s + 1) * T], AFF[:, 2 * s + m, e:e + 1]
                            nc.vector.tensor_scalar(CMP[:, e % 2, 4 * s + 2 * m, :], row, av, 0.0, ALU.is_gt, ALU.add,
                                                    accum_out=RANKS[:, 0, 2 * s + m, e:e + 1])
                            ins = nc.vector.scalar_tensor_tensor(CMP[:, e % 2, 4 * s + 2 * m + 1, :], row, av, before[:, m, :],
                                                                 ALU.is_equal, ALU.mult,
                                                                 accum_out=RANKS[:, 1, 2 * s + m, e:e + 1])
                    return ins
                read_bank(dve, cur, True, op)
            dve.wait_ge(bank_free[(cur.g - 1) % 4], (cur.g - 1) // 4 + 1)
            steps(nc.vector.tensor_tensor(RANKS[:, 0, 0:tt], RANKS[:, 0, 0:tt], RANKS[:, 1, 0:tt], ALU.add))
            slots = cst("slots").unsqueeze(1).to_broadcast([P, EXPERTS, CAP])
            ph = PH.rearrange("p m (e s) -> p m e s", e=EXPERTS)
            for m in range(tt):
                ins = nc.vector.tensor_tensor(ph[:, m], slots, RANKS[:, 0, m, :].unsqueeze(2).to_broadcast([P, EXPERTS, CAP]),
                                              ALU.is_equal)
            ins.then_inc(onehot, 1)
            for s in range(st):
                for c in range(DC):
                    read_bank(dve, cur, c % 2 == 1, lambda bank, s=s, c=c: nc.vector.tensor_copy(XIN[:, c, s, :], bank))
            for b in range(4):
                last = cur.g - 1 - (cur.g - 1 - b) % 4
                dve.wait_ge(bank_full[b], last // 4 + 1)
            for m in range(tt):
                ins = nc.vector.tensor_tensor(ph[:, m], ph[:, m], AFF[:, m, :].unsqueeze(2).to_broadcast([P, EXPERTS, CAP]),
                                              ALU.mult)
            ins.then_inc(onehot, 1)
            skip_banks(cur, 2 * st)
            cur.add("route", 1)

        HB = [0, 2]
        def experts(eng, cur, one_expert, steps=None, per=0):
            with loop(eng, cur, EXPERTS // 4, pieces=96, steps=steps, steps_per=per) as i:
                for j in range(4):
                    one_expert(i, j, cur.base("moe") + j + i * 4)
            cur.add("moe", EXPERTS)

        def experts_pe(pe, cur, st):
            rows = CAP * st

            def turn(e, h):
                pe.wait_ge(moe_hid, CREDIT + 2 * e + h + 1)
                pe.wait_ge(moe_split, CREDIT + 2 * e + h - 1)
                for c in range(4):
                    last = nc.tensor.matmul(ps[:, 4 + h, c * rows:(c + 1) * rows],
                                            HID[0:rows, h, c * P:(c + 1) * P], ident[0:rows, 0:rows],
                                            start=True, stop=True)
                last.then_inc(moe_turned, 1)

            def down(n, j):
                hi, lo = piece_of(pe, cur)
                for q in range(2):
                    k, w = 2 * j + q, slice(q * 512, q * 512 + 512)
                    last = three(ps[:, 6 + n, :], stationary(HIDT_AT, k), (hi[:, w], lo[:, w]), k == 0, k == DC - 1)
                if j < 3:
                    last.then_inc(piece_used[(cur.p - 1) % 4], 1)
                else:
                    last.then_inc(moe_y, 1)

            def one_expert(i, j, e):
                xs = lambda k: stationary(XS_AT[j % 2], k)
                pe.wait_ge(moe_staged, CREDIT + e + 1)
                for h in range(2):
                    pe.wait_ge(moe_hid, CREDIT + 2 * e + h - 1)
                    rows_tile(pe, cur, xs, HB[h]).then_inc(piece_used[(cur.p - 1) % 4], 1)
                    if h == 1:
                        turn(e, 0)
                    rows_tile(pe, cur, xs, HB[h] + 1).then_inc(moe_h, 1)
                pe.wait_ge(moe_split, CREDIT + 2 * e + 1)
                pe.wait_ge(moe_saved[0], CREDIT + e)
                down(0, 0)
                down(0, 1)
                turn(e, 1)
                pe.wait_ge(moe_saved[1], CREDIT + e)
                down(1, 0)
                down(1, 1)
                pe.wait_ge(moe_split, CREDIT + 2 * e + 2)
                down(0, 2)
                down(0, 3)
                down(1, 2)
                down(1, 3)
            experts(pe, cur, one_expert)

        def experts_act(act, cur, st):
            rows = CAP * st

            def silu(e, h):
                act.wait_ge(moe_h, CREDIT + 2 * e + h + 1)
                act.sem_inc(piece_used[(cur.p - 1) % 4], 1)
                act.wait_ge(moe_hid, CREDIT + 2 * e + h - 1)
                nc.scalar.activation(SG[0:rows, h, :], ps[0:rows, HB[h], :], ACT.Silu).then_inc(moe_silu, 1)

            def copy_turned(e, h):
                act.wait_ge(moe_turned, CREDIT + 2 * e + h + 1)
                act.wait_ge(moe_y, CREDIT + 2 * e)
                nc.scalar.activation(HIDT_HI[:, 4 * h:4 * h + 4, 0:rows],
                                     ps[:, 4 + h, 0:4 * rows].rearrange("p (c s) -> p c s", c=4), ACT.Copy)\
                    .then_inc(moe_copied, 1)

            def one_expert(i, j, e):
                next_piece(act, cur, 7)
                cur.p += 1
                silu(e, 0)
                split_hi(act, cur)
                next_piece(act, cur, 5)
                copy_turned(e, 0)
                next_piece(act, cur, 2)
                cur.p += 1
                silu(e, 1)
                split_hi(act, cur)
                next_piece(act, cur, 1)
                copy_turned(e, 1)
                next_piece(act, cur, 6)
                cur.p += 1
                act.wait_ge(moe_y, CREDIT + 2 * e + 2)
                act.sem_inc(piece_used[(cur.p - 1) % 4], 1)
                for s in range(st):
                    ins = nc.scalar.activation(YE[CAP * j:CAP * (j + 1), s, one(i), 512:1024],
                                               ps[CAP * s:CAP * (s + 1), 7:8, :], ACT.Copy)
                ins.then_inc(moe_saved[1], 1)
                split_hi(act, cur)
            experts(act, cur, one_expert)

        def experts_dve(dve, cur, st):
            rows = CAP * st

            def gate(e, h):
                dve.wait_ge(moe_silu, CREDIT + 2 * e + h + 1)
                dve.wait_ge(moe_turned, CREDIT + 2 * e + h - 1)
                nc.vector.tensor_tensor(HID[0:rows, h, :], SG[0:rows, h, :], ps[0:rows, HB[h] + 1, :], ALU.mult)\
                    .then_inc(moe_hid, 1)

            def split_turned(e, h):
                dve.wait_ge(moe_copied, CREDIT + 2 * e + h + 1)
                k = slice(4 * h, 4 * h + 4)
                nc.vector.tensor_tensor(HIDT_LO[:, k, 0:rows],
                                        ps[:, 4 + h, 0:4 * rows].rearrange("p (c s) -> p c s", c=4),
                                        f32(HIDT_HI[:, k, 0:rows]), ALU.subtract).then_inc(moe_split, 1)

            def one_expert(i, j, e):
                next_piece(dve, cur, 7)
                gate(e, 0)
                next_piece(dve, cur, 6)
                split_turned(e, 0)
                next_piece(dve, cur, 2)
                gate(e, 1)
                next_piece(dve, cur, 2)
                split_turned(e, 1)
                next_piece(dve, cur, 4)
                cur.p += 1
                dve.wait_ge(moe_y, CREDIT + 2 * e + 1)
                dve.sem_inc(piece_used[(cur.p - 1) % 4], 1)
                for s in range(st):
                    ins = nc.vector.tensor_copy(YE[CAP * j:CAP * (j + 1), s, one(i), 0:512],
                                                ps[CAP * s:CAP * (s + 1), 6:7, :])
                ins.then_inc(moe_saved[0], 1)
                split_lo(dve, cur)
                next_piece(dve, cur, 2)
            experts(dve, cur, one_expert)

        def experts_pool(pool, cur, steps, st):
            def one_expert(i, j, e):
                pool.wait_ge(moe_h, CREDIT + 2 * e - 2)
                hi, lo = split_place(XS_AT[j % 2])
                place = bass.ds(i * (4 * CAP) + j * CAP, CAP)
                for s in range(st):
                    ins = nc.gpsimd.tensor_copy(hi[:, :, CAP * s:CAP * (s + 1)], XIN[:, :, s, place])
                steps(ins)
                pool.sem_inc(pool_step, 1)
                steps.n += 1
                for s in range(st):
                    to = slice(CAP * s, CAP * (s + 1))
                    ins = nc.gpsimd.tensor_tensor(lo[:, :, to], XIN[:, :, s, place], f32(hi[:, :, to]), ALU.subtract)
                ins.then_inc(moe_staged, 1)
                cur.p += 24
            experts(pool, cur, one_expert, steps=steps, per=8)

        def scatter_pe(pe, cur, st):
            for c in range(DC):
                bank_parts(pe, cur, [(P, s * T, T, [(YE[:, s, g, c * P:(c + 1) * P], GT[:, s, g, :]) for g in range(4)])
                                     for s in range(st)])

        def scatter_dve(dve, cur, st):
            for c in range(DC):
                def op(bank, c=c):
                    for s in range(st):
                        tok = slice(s * T, (s + 1) * T)
                        ins = nc.vector.scalar_tensor_tensor(XT[:, c, tok], bank[:, tok], MOD[:, 5 * DC + c, s:s + 1],
                                                             XT[:, c, tok], ALU.mult, ALU.add)
                    return ins
                read_bank(dve, cur, True, op)

        OUT = wk(8192, TT, D)

        def turn_out_pe(pe, cur):
            for m in range(TT):
                for h in range(2):
                    bank_parts(pe, cur, [(P, c * P, P, [(HF[:, 4 * h + c, m * P:(m + 1) * P], ident)])
                                         for c in range(4)], turn=True)

        def turn_out_act(act, cur):
            for m in range(TT):
                for h in range(2):
                    read_bank(act, cur, True, lambda bank, m=m, h=h: nc.scalar.activation(
                        OUT[:, m, h * 512:(h + 1) * 512], bank, ACT.Copy))

        LOADS = {"start": 5, "cum_out": 6, "cum_in": 7, "lru_w": 8}
        LOADS["par"] = [10 + 5 * l for l in range(LAYERS)]
        LOADS["nab"] = [LOADS["par"][l] + 1 for l in range(LAYERS)]
        LOADS["ln"] = [LOADS["par"][l] + 4 for l in range(LAYERS)]

        block = ctx.enter_context(nc.Block())
        ended = []

        @block.sync
        def _(sp):
            def load(t, j):
                sp.dma_start(ring[:, j, :], a["stream"][one(t)].rearrange("a p w -> (a p) w")).then_inc(landed[j], 16)

            for j in range(R):
                load(j, j)
            with sp.Fori(0, N_SLOTS // R - 1) as i:
                for j in range(R):
                    q = 2 * j + 1
                    sp.wait_ge(piece_used[q % 4], i * 2 + (q // 4 + 1))
                    load(i * R + (R + j), j)
            turns = N_SLOTS // R - 1
            for j in range(N_SLOTS % R):
                q = 2 * j + 1
                sp.wait_ge(piece_used[q % 4], turns * 2 + q // 4 + 1)
                load(R * (turns + 1) + j, j)

        @block.tensor
        def _(pe):
            cur = Cursor("pe")
            pe.wait_ge(loads, 16 * LOADS["start"])
            turn_in_pe(pe, cur, range(4), 0)
            barrier(pe, cur)
            main_norm_pe(pe, cur, 2 * T)
            barrier(pe, cur)
            qkv_pe(pe, cur)
            forget_pe(pe, cur)
            barrier(pe, cur)
            head_norm_pe(pe, cur, fox_q_norm)
            barrier(pe, cur)
            head_norm_pe(pe, cur, fox_k_norm)
            barrier(pe, cur)
            att_pe(pe, cur, fox)
            barrier(pe, cur)
            fm_banks(pe, cur, in_a()(T), T, 2 * DC)
            barrier(pe, cur)
            lru_pe(pe, cur)
            barrier(pe, cur)
            qkv_pe(pe, cur)
            barrier(pe, cur)
            sb_pe(pe, cur)
            barrier(pe, cur)
            qkv_pe(pe, cur, 0, T, T)
            barrier(pe, cur)
            head_norm_pe(pe, cur, mem_q_norm)
            barrier(pe, cur)
            head_norm_pe(pe, cur, mem_k_norm)
            barrier(pe, cur)
            att_pe(pe, cur, mem_att)
            barrier(pe, cur)
            merge_pe(pe, cur, 4, DC, T)
            barrier(pe, cur)
            out_pe(pe, cur, T)
            barrier(pe, cur)
            main_norm_pe(pe, cur, T)
            barrier(pe, cur)
            up_pe(pe, cur)
            barrier(pe, cur)
            down_pe(pe, cur)
            barrier(pe, cur)
            pe.wait_ge(loads, 16 * LOADS["par"][0])
            turn_in_pe(pe, cur, range(2), T)
            barrier(pe, cur)
            for layer in range(LAYERS):
                n = T if layer == LAYERS - 1 else 2 * T
                ada_pe(pe, cur)
                barrier(pe, cur)
                main_norm_pe(pe, cur, 2 * T)
                barrier(pe, cur)
                proj2_pe(pe, cur, n)
                barrier(pe, cur)
                att_pe(pe, cur, na_x)
                barrier(pe, cur)
                if n > T:
                    att_pe(pe, cur, na_ctx)
                    barrier(pe, cur)
                proj2_pe(pe, cur, n)
                barrier(pe, cur)
                rope_pe(pe, cur)
                lam_pe(pe, cur)
                barrier(pe, cur)
                att_pe(pe, cur, da_x)
                barrier(pe, cur)
                if n > T:
                    att_pe(pe, cur, da_ctx)
                    barrier(pe, cur)
                head_norm_pe(pe, cur, da_norm(n, 0.0))
                barrier(pe, cur)
                gmlp_proj_pe(pe, cur, n // P)
                barrier(pe, cur)
                gmlp_mix_pe(pe, cur, n // P, layer)
                barrier(pe, cur)
                merge_pe(pe, cur, 3, BC, n)
                barrier(pe, cur)
                out_pe(pe, cur, n)
                barrier(pe, cur)
                main_norm_pe(pe, cur, n, split=False)
                barrier(pe, cur)
                route_pe(pe, cur, n // T)
                barrier(pe, cur)
                experts_pe(pe, cur, n // T)
                barrier(pe, cur)
                scatter_pe(pe, cur, n // T)
                barrier(pe, cur)
            main_norm_pe(pe, cur, T, split=False)
            barrier(pe, cur)
            turn_out_pe(pe, cur)
            barrier(pe, cur)
            ended.append((cur.stage, cur.p, cur.g))

        @block.scalar
        def _(act):
            cur = Cursor("act")
            steps = Steps(act, act_step)
            for _ in range(AHEAD):
                split_hi(act, cur)
            turn_in_read(act, "act", cur, range(4), 0)
            barrier(act, cur)
            main_norm_act(act, cur, steps, 2 * T)
            barrier(act, cur)
            qkv_read(act, "act", cur)
            forget_act(act, cur, steps)
            barrier(act, cur)
            head_norm_act(act, cur, steps, fox_q_norm)
            barrier(act, cur)
            head_norm_act(act, cur, steps, fox_k_norm)
            barrier(act, cur)
            att_act(act, cur, steps, fox)
            barrier(act, cur)
            for h in range(2):
                copies(act, "act", cur, lambda j, h=h: LX[:, 4 * h + j, :], 4, T)
            for h in range(2):
                copies(act, "act", cur, lambda j, h=h: LG[:, 4 * h + j, :], 4, T, func=ACT.Gelu_apprx_tanh)
            barrier(act, cur)
            lru_act(act, cur, steps)
            barrier(act, cur)
            qkv_read(act, "act", cur, HD ** -0.5)
            barrier(act, cur)
            sb_act(act, cur, steps)
            barrier(act, cur)
            qkv_read(act, "act", cur)
            barrier(act, cur)
            head_norm_act(act, cur, steps, mem_q_norm)
            barrier(act, cur)
            head_norm_act(act, cur, steps, mem_k_norm)
            barrier(act, cur)
            att_act(act, cur, steps, mem_att)
            barrier(act, cur)
            merge_act(act, cur, 4, DC, T, YT, lambda i, c: par[:, bass.ds(i * DC + (PAR1["b_gate"][0] + c), 1)])
            barrier(act, cur)
            out_act(act, cur, T)
            barrier(act, cur)
            main_norm_act(act, cur, steps, T)
            barrier(act, cur)
            up_act(act, cur, steps)
            barrier(act, cur)
            down_act(act, cur)
            barrier(act, cur)
            turn_in_read(act, "act", cur, range(2), T)
            barrier(act, cur)
            for layer in range(LAYERS):
                n = T if layer == LAYERS - 1 else 2 * T
                ada_act(act, cur, layer)
                barrier(act, cur)
                main_norm_act(act, cur, steps, 2 * T, shift=lambda c, s: MOD[:, c, s:s + 1])
                barrier(act, cur)
                proj2_read(act, "act", cur, n)
                barrier(act, cur)
                att_act(act, cur, steps, na_x)
                barrier(act, cur)
                if n > T:
                    att_act(act, cur, steps, na_ctx)
                    barrier(act, cur)
                proj2_read(act, "act", cur, n)
                barrier(act, cur)
                skip_banks(cur, 8)
                lam_act(act, cur)
                barrier(act, cur)
                att_act(act, cur, steps, da_x)
                barrier(act, cur)
                if n > T:
                    att_act(act, cur, steps, da_ctx)
                    barrier(act, cur)
                head_norm_act(act, cur, steps, da_norm(n, 0.0))
                barrier(act, cur)
                gmlp_proj_read(act, "act", cur, n // P)
                barrier(act, cur)
                gmlp_ln_act(act, n // P, layer)
                gmlp_mix_act(act, cur, n // P)
                barrier(act, cur)
                merge_act(act, cur, 3, BC, n, Y2, None)
                barrier(act, cur)
                out_act(act, cur, n)
                barrier(act, cur)
                main_norm_act(act, cur, steps, n, shift=lambda c, s: MOD[:, 3 * DC + c, s:s + 1], split=False)
                barrier(act, cur)
                route_act(act, cur, steps, n // T)
                barrier(act, cur)
                experts_act(act, cur, n // T)
                barrier(act, cur)
                skip_banks(cur, DC)
                barrier(act, cur)
            main_norm_act(act, cur, steps, T, split=False)
            barrier(act, cur)
            turn_out_act(act, cur)
            barrier(act, cur)
            ended.append((cur.stage, cur.p, cur.g))
            act.dma_start(out.rearrange("a (m p) d -> p (a m) d", p=P), OUT).then_inc(stored, 16)
            act.wait_ge(stored, 16)

        @block.vector
        def _(dve):
            cur = Cursor("dve")
            steps = Steps(dve, dve_step)
            for _ in range(AHEAD):
                split_lo(dve, cur)
            turn_in_read(dve, "dve", cur, range(4), 0)
            barrier(dve, cur)
            main_norm_dve(dve, cur, steps, 2 * T, lambda c, s: p1("attn_g" if s == 0 else "mem_g", c))
            barrier(dve, cur)
            qkv_read(dve, "dve", cur)
            forget_dve(dve, cur, steps)
            barrier(dve, cur)
            head_norm_dve(dve, cur, steps, fox_q_norm)
            barrier(dve, cur)
            head_norm_dve(dve, cur, steps, fox_k_norm)
            barrier(dve, cur)
            att_dve(dve, cur, steps, fox)
            barrier(dve, cur)
            for h in range(2):
                copies(dve, "dve", cur, lambda j, h=h: LX[:, 4 * h + j, :], 4, T)
            skip_fm(dve, cur, 8)
            barrier(dve, cur)
            lru_dve(dve, cur, steps)
            barrier(dve, cur)
            qkv_read(dve, "dve", cur, HD ** -0.5)
            barrier(dve, cur)
            sb_dve(dve, cur, steps)
            barrier(dve, cur)
            qkv_read(dve, "dve", cur)
            barrier(dve, cur)
            head_norm_dve(dve, cur, steps, mem_q_norm)
            barrier(dve, cur)
            head_norm_dve(dve, cur, steps, mem_k_norm)
            barrier(dve, cur)
            att_dve(dve, cur, steps, mem_att)
            barrier(dve, cur)
            merge_dve(dve, cur, steps, 4, DC, T, YT)
            barrier(dve, cur)
            out_dve(dve, cur, T)
            barrier(dve, cur)
            main_norm_dve(dve, cur, steps, T, lambda c, s: p1("ffn_g", c))
            barrier(dve, cur)
            up_dve(dve, cur, steps)
            barrier(dve, cur)
            down_dve(dve, cur)
            barrier(dve, cur)
            turn_in_read(dve, "dve", cur, range(2), T)
            barrier(dve, cur)
            for layer in range(LAYERS):
                n = T if layer == LAYERS - 1 else 2 * T
                lam_init = 0.8 - 0.6 * float(np.exp(-0.3 * layer))
                ada_dve(dve, cur, steps, layer)
                dve.drain().then_inc(dve_step, 1)
                steps.n += 1
                dve.wait_ge(dve_step, steps.n)
                gmod_dve(dve, steps, "g1", 1)
                barrier(dve, cur)
                main_norm_dve(dve, cur, steps, 2 * T, lambda c, s: gmod[:, c, s:s + 1],
                              shift=lambda c, s: MOD[:, c, s:s + 1])
                barrier(dve, cur)
                proj2_read(dve, "dve", cur, n)
                barrier(dve, cur)
                dve.wait_ge(loads, 16 * LOADS["nab"][layer])
                att_dve(dve, cur, steps, na_x)
                barrier(dve, cur)
                if n > T:
                    att_dve(dve, cur, steps, na_ctx)
                    barrier(dve, cur)
                proj2_read(dve, "dve", cur, n)
                barrier(dve, cur)
                rope_dve(dve, cur, steps)
                lam_dve(dve, cur, steps, lam_init)
                barrier(dve, cur)
                att_dve(dve, cur, steps, da_x)
                barrier(dve, cur)
                if n > T:
                    att_dve(dve, cur, steps, da_ctx)
                    barrier(dve, cur)
                head_norm_dve(dve, cur, steps, da_norm(n, lam_init))
                barrier(dve, cur)
                gmlp_proj_read(dve, "dve", cur, n // P)
                barrier(dve, cur)
                gmlp_ln_dve(dve, cur, steps, n // P, layer)
                gmlp_mix_dve(dve, cur, steps, n // P)
                barrier(dve, cur)
                merge_dve(dve, cur, steps, 3, BC, n, Y2)
                barrier(dve, cur)
                out_dve(dve, cur, n, gain=lambda c, s: MOD[:, 2 * DC + c, s:s + 1])
                gmod_dve(dve, steps, "g2", 4)
                barrier(dve, cur)
                main_norm_dve(dve, cur, steps, n, lambda c, s: gmod[:, c, s:s + 1], split=False)
                barrier(dve, cur)
                route_dve(dve, cur, steps, n // T)
                barrier(dve, cur)
                experts_dve(dve, cur, n // T)
                barrier(dve, cur)
                scatter_dve(dve, cur, n // T)
                barrier(dve, cur)
            main_norm_dve(dve, cur, steps, T, lambda c, s: p2("g_final", c), split=False)
            barrier(dve, cur)
            skip_banks(cur, 4)
            barrier(dve, cur)
            ended.append((cur.stage, cur.p, cur.g))
            assert len(set(ended)) == 1, ended

        @block.gpsimd
        def _(pool):
            cur = Cursor("pool")
            steps = Steps(pool, pool_step)
            for signal in looped:
                pool.sem_inc(signal, CREDIT)
            pool.dma_start(XIN_TM[:, 0:2, :], a["x"].rearrange("a (m p) d -> p (a m) d", p=P)).then_inc(loads, 16)
            pool.dma_start(XIN_TM[:, 2:4, :], a["mem"].rearrange("a (m p) d -> p (a m) d", p=P)).then_inc(loads, 16)
            pool.dma_start(const[:, :], a["const"]).then_inc(loads, 16)
            pool.dma_start(sel[:, :, :], a["sel"]).then_inc(loads, 16)
            pool.dma_start(par[:, 0:N_PAR1], a["par1"]).then_inc(loads, 16)
            pool.wait_ge(loads, 16 * LOADS["start"])
            steps(nc.gpsimd.memset(small[:, :], 0.0))
            barrier(pool, cur)
            barrier(pool, cur)
            forget_pool(pool, cur)
            barrier(pool, cur)
            barrier(pool, cur)
            barrier(pool, cur)
            barrier(pool, cur)
            pool.dma_start(LW, a["lru_w"]).then_inc(loads, 16)
            pool.wait_ge(loads, 16 * LOADS["lru_w"])
            barrier(pool, cur)
            barrier(pool, cur)
            barrier(pool, cur)
            barrier(pool, cur)
            for _ in range(3):
                barrier(pool, cur)
            barrier(pool, cur)
            for _ in range(5):
                barrier(pool, cur)
            pool.dma_start(XIN_TM[:, 0:2, :], a["ctx"].rearrange("a (m p) d -> p (a m) d", p=P)).then_inc(loads, 16)
            pool.dma_start(par[:, 0:N_PAR2], a["par2"][0]).then_inc(loads, 16)
            pool.wait_ge(loads, 16 * 10)
            barrier(pool, cur)
            n_loads = 10
            for layer in range(LAYERS):
                n = T if layer == LAYERS - 1 else 2 * T
                assert n_loads == LOADS["par"][layer], (n_loads, layer)
                pool.dma_start(NAB.rearrange("p a b c t -> p (a b c t)"), a["na_bias"][layer]).then_inc(loads, 16)
                barrier(pool, cur)
                barrier(pool, cur)
                barrier(pool, cur)
                pool.wait_ge(loads, 16 * (n_loads + 1))
                barrier(pool, cur)
                if n > T:
                    barrier(pool, cur)
                barrier(pool, cur)
                barrier(pool, cur)
                barrier(pool, cur)
                if n > T:
                    barrier(pool, cur)
                barrier(pool, cur)
                pool.dma_start(GWS, a["w_s"][layer]).then_inc(loads, 16)
                pool.dma_start(GLN[:, 0, :], a["ln_g"][layer].partition_broadcast(P)).then_inc(loads, 16)
                pool.dma_start(GLN[:, 1, :], a["ln_b"][layer].partition_broadcast(P)).then_inc(loads, 16)
                pool.wait_ge(loads, 16 * (n_loads + 4))
                barrier(pool, cur)
                barrier(pool, cur)
                barrier(pool, cur)
                barrier(pool, cur)
                barrier(pool, cur)
                barrier(pool, cur)
                experts_pool(pool, cur, steps, n // T)
                barrier(pool, cur)
                barrier(pool, cur)
                n_loads += 4
                if layer < LAYERS - 1:
                    pool.dma_start(par[:, 0:N_PAR2], a["par2"][layer + 1]).then_inc(loads, 16)
                    n_loads += 1
                    pool.wait_ge(loads, 16 * n_loads)
            barrier(pool, cur)
            barrier(pool, cur)
            assert cur.stage == ended[0][0], (cur.stage, ended)


def _chunks(v):
    return v.reshape(-1, P).T


def _rows(w):
    return w.reshape(-1, P, w.shape[1]).transpose(1, 0, 2)


def _stream(x):
    parts = []

    def put(w):
        parts.append(w.reshape(P, -1))

    def tm(w, lo, hi):
        w = _rows(w)
        for c in range(lo, hi, 512):
            put(w[:, :, c:c + 512])

    def fm(w, lo, hi):
        w = _rows(w)[:, :, lo:hi]
        put(w.reshape(P, w.shape[1], -1, P).transpose(0, 2, 1, 3))

    w_in = x["w_in"][0]
    f0 = 3 * D + HEADS
    g0 = f0 + 6 * D
    fm(w_in, 0, 2 * D)
    tm(w_in, 2 * D, 3 * D)
    fm(w_in, f0, f0 + 2 * D)
    fm(w_in, f0 + 2 * D, f0 + 4 * D)
    tm(w_in, f0 + 4 * D, f0 + 5 * D)
    fm(w_in, f0 + 5 * D, f0 + 6 * D)
    fm(x["w_mem_kv"][0], 0, D)
    tm(x["w_mem_kv"][0], D, 2 * D)
    for n in range(4):
        for h in range(2):
            fm(w_in, g0 + n * D + h * 512, g0 + n * D + h * 512 + 512)
            fm(x["w_branch"][0, n], h * 512, h * 512 + 512)
    fm(x["w_out"][0], 0, D)
    for j in range(FC // 2):
        fm(x["w_up"][0], j * 256, (j + 1) * 256)
        fm(x["w_up"][0], FF + j * 256, FF + (j + 1) * 256)
    fm(x["w_down"][0], 0, D)
    for l in range(LAYERS):
        tm(x["w_ada_2"][l], 0, 6 * D)
        w = x["w_in_2"][l]
        for at, f in ((4, fm), (0, fm), (1, tm), (5, fm), (2, fm), (3, tm), (6, tm), (7, tm)):
            f(w, at * BW, (at + 1) * BW)
        for n in range(3):
            for h in range(2):
                lo = 8 * BW + n * D + h * 512
                fm(w, lo, lo + 512)
                fm(x["w_branch_2"][l, n], h * 512, h * 512 + 512)
        fm(x["w_out_2"][l], 0, D)
        for e in range(EXPERTS):
            for h in range(2):
                tm(x["w_e1_2"][l, e], h * 512, h * 512 + 512)
                tm(x["w_e3_2"][l, e], h * 512, h * 512 + 512)
            for h in range(2):
                tm(x["w_e2_2"][l, e][h * 512:(h + 1) * 512], 0, D)
    assert sum(w.shape[1] for w in parts) == STREAM_WORDS, (sum(w.shape[1] for w in parts), STREAM_WORDS)
    stream = np.zeros((N_SLOTS, P, WORDS), np.float32)
    at = 0
    for w in parts:
        while w.shape[1]:
            n = min(WORDS - at % WORDS, w.shape[1])
            stream[at // WORDS, :, at % WORDS:at % WORDS + n] = w[:, :n]
            at, w = at + n, w[:, n:]
    return stream


def _constants():
    i = np.arange(P)
    t = np.arange(T)
    c = {}
    c["ident"] = np.eye(P)
    c["tri"] = (i[:, None] >= i[None, :])
    c["ones"] = np.ones((P, P))
    row = (i[:, None] + P * np.arange(2)[None, :])
    c["causal"] = np.where(t[None, None, :] <= row[:, :, None], 0.0, NEG)
    valid = row[:, :, None] < t[None, None, :]
    c["sb_add"] = np.where(valid, 0.0, NEG)
    c["sb_neg"] = np.where(valid, -1.0, 0.0)
    c["before"] = t[None, None, :] < row[:, :, None]
    f = i % 64
    inv = (np.float32(10000.0) ** (-np.arange(0, 32, 2, dtype=np.float32) / np.float32(32))).astype(np.float32)
    place = np.where((f < 32)[:, None], (t // GRID)[None, :], (t % GRID)[None, :]).astype(np.float32)
    ang = place * inv[f % 16][:, None]
    c["cos"], c["sin"] = np.cos(ang), np.sin(ang)
    swap = np.zeros((P, P))
    for p in range(P):
        first = p % 32 < 16
        swap[p + 16 if first else p - 16, p] = -1.0 if first else 1.0
    c["swap"] = swap
    c["slots"] = np.broadcast_to(np.arange(CAP), (P, CAP))
    c["pair_ones"] = (i[:, None] // HD == i[None, :] // HD)
    const = np.zeros((P, N_CONST), np.float32)
    for name, (lo, hi) in CONSTS.items():
        const[:, lo:hi] = np.asarray(c[name], np.float32).reshape(P, -1)
    sel = np.zeros((16, 16, P), np.float32)
    sel[np.arange(16), np.arange(16), :] = 1.0
    return const, sel


def _params(table, values, n):
    par = np.zeros((P, n), np.float32)
    for name, (lo, hi) in table.items():
        v = values[name]
        par[:v.shape[0], lo:hi] = v.reshape(v.shape[0], -1)
    return par


def _layout(x):
    const, sel = _constants()
    pair = lambda v: np.concatenate([v, v]).reshape(P, 1)
    chunk_rows = lambda w: np.concatenate([_chunks(r) for r in w], axis=1)
    w_in = x["w_in"][0]
    par1 = dict(attn_g=_chunks(x["attn_norm_g"][0]), mem_g=_chunks(x["mem_norm_g"][0]),
                ffn_g=_chunks(x["ffn_norm_g"][0]), fox_q_g=pair(x["fox_q_norm_g"][0]),
                fox_k_g=pair(x["fox_k_norm_g"][0]), mem_q_g=_chunks(x["mem_q_norm_g"][0]),
                mem_k_g=_chunks(x["mem_k_norm_g"][0]), conv_w=chunk_rows(x["lru_conv_w"][0]),
                conv_b=_chunks(x["lru_conv_b"][0]), b_a=_chunks(x["lru_b_a"][0]), b_x=_chunks(x["lru_b_x"][0]),
                lam=_chunks(x["lru_lambda"][0]), b_gate=chunk_rows(x["b_gate"][0]),
                ffn_w=chunk_rows(x["ffn_conv_w"][0]), ffn_b=_chunks(x["ffn_conv_b"][0]),
                b_forget=x["b_forget"][0].reshape(16, 1), w_forget=_rows(w_in[:, 3 * D:3 * D + HEADS]))
    lru_w = np.zeros((P, 2, DC, P), np.float32)
    for g, name in enumerate(("lru_w_a", "lru_w_x")):
        for b in range(16):
            o = 64 * (b % 2)
            lru_w[o:o + 64, g, b // 2, o:o + 64] = x[name][0, b]
    both = np.stack([_chunks(x["c_2"][0]), _chunks(x["c_ctx_2"])], axis=2)
    par2 = []
    q = np.arange(T)
    qr, qc, kr, kcol = q[:, None] // GRID, q[:, None] % GRID, q[None, :] // GRID, q[None, :] % GRID
    start = np.clip(qc - 8, 0, GRID - 16)
    inside = (kcol >= start) & (kcol < start + 16)
    dr, dc = kr - qr + 7, np.where(inside, kcol - qc + 15, 0)
    na = np.full((LAYERS, P, 8, 2, T), NEG, np.float32)
    for l in range(LAYERS):
        par2.append(_params(PAR2, dict(
            b_ada=_chunks(x["b_ada_2"][l]), g1=_chunks(x["g_norm1_2"][l]), g2=_chunks(x["g_norm2_2"][l]),
            subln=x["da_subln_g_2"][l].reshape(P, 1), b_s=x["gm_b_s_2"][l].T,
            lam_q=np.stack([x["da_lam_q1_2"][l], x["da_lam_q2_2"][l]], axis=1),
            lam_k=np.stack([x["da_lam_k1_2"][l], x["da_lam_k2_2"][l]], axis=1),
            w_router=_rows(x["w_router_2"][l]), g_final=_chunks(x["g_final_2"]), c=both), N_PAR2))
        b = np.where(inside[None], x["na_rpb_2"][l][:, dr, dc], np.float32(NEG))
        na[l] = b.reshape(8, 2, P, T).transpose(2, 0, 1, 3)
    return {
        "stream": _stream(x), "x": x["x"], "mem": x["mem"], "ctx": x["ctx_2"], "const": const, "sel": sel,
        "par1": _params(PAR1, par1, N_PAR1), "par2": np.stack(par2), "lru_w": lru_w,
        "na_bias": na.reshape(LAYERS, P, -1), "w_s": np.ascontiguousarray(x["gm_w_s_2"].transpose(0, 3, 1, 2)),
        "ln_g": x["gm_ln_g_2"], "ln_b": x["gm_ln_b_2"],
    }


def kernel(**inputs):
    import concourse.bacc as _bacc
    from concourse.bass_utils import run_bass_kernel_spmd as _run

    nc = _bacc.Bacc("TRN2", target_bir_lowering=False, num_devices=1)
    arrays, aps = {}, {}
    for name, v in _layout({k: np.asarray(v) for k, v in inputs.items()}).items():
        v = np.ascontiguousarray(v)
        arrays[f"in_{name}"] = v
        aps[name] = nc.dram_tensor(f"in_{name}", v.shape, mybir.dt.from_np(v.dtype), kind="ExternalInput").ap()
    aps["cum_scratch"] = nc.dram_tensor("cum_scratch", (HEADS, T), F32).ap()
    out = nc.dram_tensor("out_0", (1, T, D), F32, kind="ExternalOutput").ap()
    build(nc, aps, out)
    r = _run(nc, [arrays], core_ids=[0])
    return r.results[0]["out_0"]
```

```python
from contextlib import ExitStack, contextmanager

import numpy as np

import concourse.bass as bass
from concourse import mybir

F32 = mybir.dt.float32
F32R = mybir.dt.float32r
ACT = mybir.ActivationFunctionType
ALU = mybir.AluOpType
AX = mybir.AxisListType

P = 128
D = 1024
DC = D // P
T = 256
TT = T // P
HD = 64
HEADS = D // HD
FF = 2816
FC = FF // P
LAYERS = 2
BW = 512
BC = BW // P
NA_HEADS = BW // HD
EXPERTS = 16
CAP = 2 * T // EXPERTS
MODC = 6 * DC
GRID = 64
EPS = 1e-6
NEG = -1e30
LRU_C = 8.0

R = 4
PIECE = 1024
WORDS = 2 * PIECE
AHEAD = 3
NB = 8
CREDIT = 4
WK_WORDS = 20736
XS_CHUNK = 3 * 64
XS_WORDS = DC * XS_CHUNK

CONSTS = {}
_at = 0
for _name, _n in (("ident", P), ("tri", P), ("ones", P), ("swap", P), ("causal", 2 * T),
                  ("sb_add", 2 * T), ("sb_neg", 2 * T), ("cos", T), ("sin", T), ("before", 2 * T),
                  ("slots", CAP), ("head_sum", DC * 16), ("row_sum", 4 * 16)):
    CONSTS[_name] = (_at, _at + _n)
    _at += _n
N_CONST = _at

PAR1 = {}
_at = 0
for _name, _n in (("attn_g", DC), ("mem_g", DC), ("ffn_g", DC), ("fox_q_g", 1), ("fox_k_g", 1),
                  ("mem_q_g", 2), ("mem_k_g", 2), ("conv_w", 4 * DC), ("conv_b", DC), ("b_a", DC),
                  ("b_x", DC), ("lam", DC), ("b_gate", 4 * DC), ("ffn_w", 3 * FC), ("ffn_b", FC),
                  ("b_forget", 1), ("w_forget", DC * 16)):
    PAR1[_name] = (_at, _at + _n)
    _at += _n
N_PAR1 = _at

PAR2 = {}
_at = 0
for _name, _n in (("b_ada", MODC), ("g1", DC), ("g2", DC), ("subln", 1), ("b_s", 4), ("lam_q", 2),
                  ("lam_k", 2), ("w_router", DC * 16), ("g_final", DC), ("c", DC * 2)):
    PAR2[_name] = (_at, _at + _n)
    _at += _n
N_PAR2 = _at
N_PAR = max(N_PAR1, N_PAR2)

TILE = DC * 512
STREAM_WORDS = (6 + 4 + 6 + 6 + 16 + 2 + FC // 2) * TILE + FC * D \
    + LAYERS * ((12 + 8) * TILE + 3 * 2 * (TILE + BC * 512) + (2 + 6 * EXPERTS) * TILE)
N_SLOTS = STREAM_WORDS // WORDS + 2
assert STREAM_WORDS % WORDS == 0


class Cursor:

    def __init__(self, who):
        self.who = who
        self.p = 0
        self.s = 0
        self.g = 0
        self.i = None
        self.pieces_per = 0
        self.banks_per = 0
        self.rounds = {}
        self.stage = 0

    def base(self, kind):
        return self.rounds.get(kind, 0)

    def add(self, kind, n):
        self.rounds[kind] = self.base(kind) + n

    def piece_use(self, piece, k=0, unit=1, period=4):
        v = unit * (piece // period + k)
        return v if self.i is None else v + self.i * (unit * (self.pieces_per // period))

    def bank(self):
        return self.g % NB

    def bank_use(self, k=0):
        v = self.g // NB + k
        return v if self.i is None else v + self.i * self.banks_per


def one(i):
    return slice(i, i + 1) if isinstance(i, int) else bass.ds(i, 1)


def span(i, n):
    return slice(i * n, i * n + n) if isinstance(i, int) else bass.ds(i * n, n)


def build(nc, a, out):
    ctx = ExitStack()
    with ctx:
        sb = lambda name, shape: ctx.enter_context(nc.sbuf_tensor(name, shape, F32))
        sem = lambda name: ctx.enter_context(nc.semaphore(name))

        with ExitStack() as place:
            ring = place.enter_context(nc.sbuf_tensor("ring", [P, R, WORDS], F32))
            WK = place.enter_context(nc.sbuf_tensor("WK", [P, WK_WORDS], F32))
        ring_lo = ctx.enter_context(nc.sbuf_tensor("ring_lo", [P, R, WORDS], F32R))
        WKR = ctx.enter_context(nc.sbuf_tensor("WKR", [P, WK_WORDS], F32R))
        piece_hi = ctx.enter_context(nc.sbuf_tensor("piece_hi", [P, 4, PIECE], F32R))
        A = ctx.enter_context(nc.sbuf_tensor("A", [P, 2, DC, 2 * T], F32R))
        AH, AL = A[:, 0], A[:, 1]
        XT = sb("XT", [P, DC, 2 * T])
        const = sb("const", [P, N_CONST])
        sel = sb("sel", [16, 16, P])
        head_sel = sb("head_sel", [16, DC, P])
        par = sb("par", [P, N_PAR])
        MOD = sb("MOD", [P, MODC, 2])
        gmod = sb("gmod", [P, DC, 2])
        small = sb("small", [P, 64])
        rowst = sb("rowst", [16, 2 * T])
        ps = ctx.enter_context(nc.psum_tensor("ps", [P, 8, 512], F32))

        def cst(name):
            lo, hi = CONSTS[name]
            return const[:, lo:hi]

        def p1(name, c=0, n=1):
            lo = PAR1[name][0] + c
            return par[:, lo:lo + n]

        def p2(name, c=0, n=1):
            lo = PAR2[name][0] + c
            return par[:, lo:lo + n]

        ident = cst("ident")
        ones = cst("ones")

        def wk(at, *shape):
            n = int(np.prod(shape))
            v = WK[:, at:at + n]
            if len(shape) == 1:
                return v
            names = "abcd"[:len(shape)]
            return v.rearrange(f"p ({' '.join(names)}) -> p {' '.join(names)}",
                               **{x: s for x, s in zip(names[1:], shape[1:])})

        def f32(x):
            return x.bitcast(F32)

        landed = [sem(f"landed{s}") for s in range(R)]
        hi_done = [sem(f"hi_done{j}") for j in range(4)]
        lo_done = [sem(f"lo_done{j}") for j in range(4)]
        piece_used = [sem(f"piece_used{j}") for j in range(4)]
        bank_full = [sem(f"bank_full{b}") for b in range(NB)]
        bank_free = [sem(f"bank_free{b}") for b in range(NB)]
        stage_done = sem("stage_done")
        loads = sem("loads")
        first_loads = sem("first_loads")
        const_load = sem("const_load")
        stored = sem("stored")
        act_step = sem("act_step")
        dve_step = sem("dve_step")
        pool_step = sem("pool_step")
        att_scores = sem("att_scores")
        att_nmax = sem("att_nmax")
        att_read = sem("att_read")
        att_exp = sem("att_exp")
        att_probs = sem("att_probs")
        att_turned = sem("att_turned")
        att_copied = sem("att_copied")
        att_y = sem("att_y")
        att_saved = sem("att_saved")
        sb_y = sem("sb_y")
        sb_saved = sem("sb_saved")
        sb_z = sem("sb_z")
        sb_abs = sem("sb_abs")
        sb_ln = sem("sb_ln")
        sb_l = sem("sb_l")
        sb_incl = sem("sb_incl")
        sb_logw = sem("sb_logw")
        sb_w = sem("sb_w")
        norm_sq = sem("norm_sq")
        norm_sd = sem("norm_sd")
        norm_r = sem("norm_r")
        x_hi = sem("x_hi")
        x_lo = sem("x_lo")
        y_hi = sem("y_hi")
        y_lo = sem("y_lo")
        moe_staged = sem("moe_staged")
        moe_h = sem("moe_h")
        moe_silu = sem("moe_silu")
        moe_hid = sem("moe_hid")
        moe_turned = sem("moe_turned")
        moe_copied = sem("moe_copied")
        moe_split = sem("moe_split")
        moe_y = sem("moe_y")
        moe_saved = [sem(f"moe_saved{h}") for h in range(2)]
        lam_prod = sem("lam_prod")
        lru_xc = sem("lru_xc")
        lru_ri = sem("lru_ri")
        lru_gates = sem("lru_gates")
        lru_a = sem("lru_a")
        lru_om = sem("lru_om")
        lru_root = sem("lru_root")
        fox_z = sem("fox_z")
        fox_e = sem("fox_e")
        fox_cum = sem("fox_cum")
        rope_r = sem("rope_r")
        raw_gates = sem("raw_gates")
        silu_c = sem("silu_c")
        split_c = sem("split_c")
        normed = sem("normed")
        ln_var = sem("ln_var")
        ln_sd = sem("ln_sd")
        ln_done = sem("ln_done")
        aff_logits = sem("aff_logits")
        aff_exp = sem("aff_exp")
        affinities = sem("affinities")
        h2_hi = sem("h2_hi")
        h2_lo = sem("h2_lo")
        onehot = sem("onehot")
        conv_done = sem("conv_done")
        silu_done = sem("silu_done")
        gate_used = sem("gate_used")
        looped = [att_scores, att_nmax, att_read, att_exp, att_probs, att_turned, att_copied,
                  att_y, att_saved, sb_y, sb_saved, sb_z, sb_abs, sb_ln, sb_l,
                  sb_incl, sb_logw, sb_w, moe_staged, moe_h, moe_silu, moe_hid, moe_turned, moe_copied,
                  moe_split, moe_y, *moe_saved]

        class Steps:

            def __init__(self, eng, sem):
                self.eng, self.sem, self.n, self.i, self.per = eng, sem, 0, None, 0

            def __call__(self, ins):
                ins.then_inc(self.sem, 1)
                self.n += 1
                self.eng.wait_ge(self.sem, self.n if self.i is None else self.n + self.i * self.per)

        @contextmanager
        def loop(eng, cur, n, pieces=0, banks=0, steps=None, steps_per=0):
            assert pieces % (2 * R) == 0 and banks % NB == 0
            p0, g0, ahead = cur.p, cur.g, cur.s - cur.p
            with eng.Fori(0, n) as i:
                cur.i, cur.pieces_per, cur.banks_per = i, pieces, banks // NB
                if steps:
                    steps.i, steps.per, s0 = i, steps_per, steps.n
                yield i
            assert cur.p - p0 == pieces and cur.g - g0 == banks, (cur.p - p0, cur.g - g0)
            if steps:
                assert steps.n - s0 == steps_per, steps.n - s0
                steps.n += steps_per * (n - 1)
                steps.i = None
            cur.p += pieces * (n - 1)
            cur.s = cur.p + ahead
            cur.g += banks * (n - 1)
            cur.i = None

        def barrier(eng, cur):
            eng.drain().then_inc(stage_done, 1)
            cur.stage += 1
            eng.wait_ge(stage_done, 4 * cur.stage)

        def split_hi(act, cur):
            j, slot, at = cur.s % 4, cur.s // 2 % R, cur.s % 2 * PIECE
            act.wait_ge(landed[slot], cur.piece_use(cur.s, 1, 16, 2 * R))
            if cur.s >= 4:
                act.wait_ge(piece_used[j], cur.piece_use(cur.s))
            nc.scalar.activation(piece_hi[:, j, :], ring[:, slot, at:at + PIECE], ACT.Copy).then_inc(hi_done[j], 1)
            cur.s += 1

        def split_lo(dve, cur):
            j, slot, at = cur.s % 4, cur.s // 2 % R, cur.s % 2 * PIECE
            dve.wait_ge(hi_done[j], cur.piece_use(cur.s, 1))
            nc.vector.tensor_tensor(ring_lo[:, slot, at:at + PIECE], ring[:, slot, at:at + PIECE],
                                    f32(piece_hi[:, j, :]), ALU.subtract).then_inc(lo_done[j], 1)
            cur.s += 1

        def next_piece(eng, cur, n=1):
            for _ in range(n):
                cur.p += 1
                if cur.who == "act":
                    split_hi(eng, cur)
                if cur.who == "dve":
                    split_lo(eng, cur)

        def piece_of(pe, cur):
            j, slot, at = cur.p % 4, cur.p // 2 % R, cur.p % 2 * PIECE
            pe.wait_ge(lo_done[j], cur.piece_use(cur.p, 1))
            cur.p += 1
            return piece_hi[:, j, :], ring_lo[:, slot, at:at + PIECE]

        def three(out_, l, r, first, last):
            nc.tensor.matmul(out_, l[0], r[0], start=first, stop=False)
            nc.tensor.matmul(out_, l[0], r[1], start=False, stop=False)
            return nc.tensor.matmul(out_, l[1], r[0], start=False, stop=last)

        def bank_parts(pe, cur, parts, turn=False):
            b = cur.bank()
            if cur.g >= NB:
                pe.wait_ge(bank_free[b], cur.bank_use())
            for rows, at, n, pairs in parts:
                for k, (l, r) in enumerate(pairs):
                    if turn:
                        last = nc.tensor.transpose(ps[0:rows, b, at:at + n], l, r)
                    else:
                        last = nc.tensor.matmul(ps[0:rows, b, at:at + n], l, r,
                                                start=(k == 0), stop=(k == len(pairs) - 1))
            last.then_inc(bank_full[b], 1)
            cur.g += 1

        def read_bank(eng, cur, mine, op, piece=False):
            b = cur.bank()
            if mine:
                eng.wait_ge(bank_full[b], cur.bank_use(1))
                if piece:
                    eng.sem_inc(piece_used[cur.p % 4], 1)
                op(ps[:, b, :]).then_inc(bank_free[b], 1)
            cur.g += 1
            if piece:
                next_piece(eng, cur)

        def skip_fm(eng, cur, banks, kc=DC):
            for j in range(banks):
                read_bank(eng, cur, False, None, piece=(kc == DC or j % 2 == 1))

        def fm_banks(pe, cur, moving, n, banks, kc=DC, ready=None):
            for c in range(banks):
                b = cur.bank()
                if cur.g >= NB:
                    pe.wait_ge(bank_free[b], cur.bank_use())
                for k in range(kc):
                    block = c * kc + k
                    if block % 8 == 0:
                        hi, lo = piece_of(pe, cur)
                    if ready and c == 0:
                        ready(k)
                    at = slice(block % 8 * P, (block % 8 + 1) * P)
                    last = three(ps[:, b, 0:n], (hi[:, at], lo[:, at]), moving(k), k == 0, k == kc - 1)
                    if block % 8 == 7 and k < kc - 1:
                        last.then_inc(piece_used[(cur.p - 1) % 4], 1)
                last.then_inc(bank_full[b], 1)
                cur.g += 1

        def in_a(c0=0):
            return lambda n: lambda k: (AH[:, k, c0:c0 + n], AL[:, k, c0:c0 + n])

        def tm_tile(pe, cur, t0, tt):
            banks = [(cur.g + m) % NB for m in range(tt)]
            for j in range(4):
                hi, lo = piece_of(pe, cur)
                for m in range(tt):
                    if j == 0 and cur.g + m >= NB:
                        pe.wait_ge(bank_free[banks[m]], (cur.g + m) // NB)
                    tok = slice(t0 + m * P, t0 + (m + 1) * P)
                    for q in range(2):
                        k, w = 2 * j + q, slice(q * 512, q * 512 + 512)
                        last = three(ps[:, banks[m], :], (AH[:, k, tok], AL[:, k, tok]), (hi[:, w], lo[:, w]),
                                     k == 0, k == DC - 1)
                    if j == 3:
                        last.then_inc(bank_full[banks[m]], 1)
                if j < 3:
                    last.then_inc(piece_used[(cur.p - 1) % 4], 1)
            cur.g += tt

        def copies(eng, who, cur, dst, banks, n, scale=1.0, func=None, tm=False):
            if tm:
                next_piece(eng, cur, 3)
            for j in range(banks):
                def op(bank, j=j):
                    if who == "act":
                        return nc.scalar.activation(dst(j), bank[:, 0:n], func or ACT.Copy, scale=scale)
                    return nc.vector.tensor_scalar(dst(j), bank[:, 0:n], scale, None, ALU.mult)
                mine = who == "act" if func or j % 2 == 0 else who == "dve"
                read_bank(eng, cur, mine, op, piece=not tm or j == banks - 1)

        def split_x_act(act, cur, groups):
            for src_, hi in groups:
                nc.scalar.activation(hi, src_, ACT.Copy).then_inc(x_hi, 1)
            cur.add("x", len(groups))

        def split_x_dve(dve, cur, groups):
            for n, (src_, hi, lo) in enumerate(groups):
                dve.wait_ge(x_hi, cur.base("x") + n + 1)
                nc.vector.tensor_tensor(lo, src_, f32(hi), ALU.subtract).then_inc(x_lo, 1)
            cur.add("x", len(groups))

        SQ = wk(0, DC, 2 * T)
        RB = wk(4096, 2048)
        HF = SQ
        FG = wk(4608, 4, T)

        def skip_banks(cur, n):
            cur.g += n

        ATT_PT = 2048
        ATT_END = 6400
        SPARE = WK_WORDS - 2048
        pt_all = wk(ATT_PT, 2, 4, 256)

        def t_of(r, nk):
            if nk == T:
                return wk((0, 1024, 4096, 5120)[r % 4], 2, 2, T)
            return wk((0, 4096, SPARE)[r % 3], 2, 2, 2 * T)

        def t_places(nk):
            return 4 if nk == T else 3

        def scores_of(r, nk):
            if nk == T:
                return ps[:, 2 * (r % 2):2 * (r % 2) + 2, :].rearrange("p a (q k) -> p a q k", q=2)
            return ps[:, 0:4, :].rearrange("p (a q) k -> p a q k", a=2)

        nmax = [small[:, at:at + 4].rearrange("p (a b) -> p a b", a=2) for at in (0, 32)]
        sums_ = [small[:, at:at + 4].rearrange("p (a b) -> p a b", a=2) for at in (4, 36)]
        rcp = small[:, 8:12].rearrange("p (a b) -> p a b", a=2)
        nlam = small[:, 12:13]

        def att_chunks(at):
            if at["diff"]:
                return [[0]]
            return [[0, 1]] if at["nk"] == 256 else [[0], [1]]

        def att_pe(pe, cur, at):
            nk, n = at["nk"], at["n"]
            kc = nk // P
            base, cbase = cur.base("att"), cur.base("att_c")
            chunks = att_chunks(at)

            def scores(r):
                if at["bias"]:
                    pe.wait_ge(att_read, CREDIT + cur.base("att_b") + r - (nk == T))
                else:
                    pe.wait_ge(att_exp, CREDIT + base + r - (nk == T))
                dst = scores_of(r, nk)
                for a in range(2):
                    for qt in range(2):
                        pairs = at["qk"](r, a, qt)
                        for j, (l, m) in enumerate(pairs):
                            last = nc.tensor.matmul(dst[:, a, qt, :], l, m, start=(j == 0),
                                                    stop=(j == len(pairs) - 1))
                last.then_inc(att_scores, 1)

            def turn(r):
                t = t_of(r, nk)
                pe.wait_ge(att_probs, CREDIT + base + r + 1)
                for j, heads in enumerate(chunks):
                    pe.wait_ge(att_copied, CREDIT + cbase + r * len(chunks) + j)
                    col = 0
                    for a in heads:
                        for k in range(kc):
                            for qt in range(2):
                                b = 4 + col // 512
                                last = nc.tensor.transpose(ps[:, b, col % 512:col % 512 + P],
                                                           t[:, a, qt, k * P:(k + 1) * P], ident)
                                col += P
                    last.then_inc(att_turned, 1)

            def product(r):
                pe.wait_ge(att_saved, CREDIT + base + r)
                for a, rows, col, pairs in at["pv"](r):
                    if a < len(chunks):
                        pe.wait_ge(att_copied, CREDIT + cbase + r * len(chunks) + a + 1)
                    for j, (l, m) in enumerate(pairs):
                        last = nc.tensor.matmul(ps[rows, 6 + col // 512, col % 512:col % 512 + T], l, m,
                                                start=(j == 0), stop=(j == len(pairs) - 1))
                last.then_inc(att_y, 1)

            ahead = 2 if nk == T else 1
            for r in range(ahead):
                scores(r)
            for r in range(n):
                if r + ahead < n:
                    scores(r + ahead)
                turn(r)
                product(r)
            cur.add("att", n)
            cur.add("att_c", n * len(chunks))
            cur.add("att_b", n if at["bias"] else 0)

        def att_act(act, cur, steps, at):
            nk, n = at["nk"], at["n"]
            kc = nk // P
            base, cbase = cur.base("att"), cur.base("att_c")
            chunks = att_chunks(at)

            def exps(r):
                act.wait_ge(att_nmax, CREDIT + base + r + 1)
                t = t_of(r, nk)
                if not at["bias"]:
                    act.wait_ge(att_turned, CREDIT + cbase + (r + 1 - t_places(nk)) * len(chunks))
                for a in range(2):
                    for qt in range(2):
                        src = t[:, a, qt, :] if at["bias"] else scores_of(r, nk)[:, a, qt, :]
                        last = nc.scalar.activation(t[:, a, qt, :], src, ACT.Exp,
                                                    bias=nmax[r % 2][:, a, qt:qt + 1],
                                                    accum_out=sums_[r % 2][:, a, qt:qt + 1])
                last.then_inc(att_exp, 1)

            def copy(r):
                for j, heads in enumerate(chunks):
                    act.wait_ge(att_turned, CREDIT + cbase + r * len(chunks) + j + 1)
                    act.wait_ge(att_y, CREDIT + base + r)
                    words = len(heads) * kc * T
                    if words == 1024 and kc == 4:
                        dst, src = pt_all[:, heads[0], :, :], ps[:, 4:6, :]
                        dst = dst.rearrange("p (b k) q -> p b (k q)", b=2)
                    elif words == 1024:
                        dst, src = pt_all[:, 0:2, 0:2, :].rearrange("p a k q -> p a (k q)"), ps[:, 4:6, :]
                    else:
                        dst, src = pt_all[:, 0, 0:2, :].rearrange("p k q -> p (k q)"), ps[:, 4, :]
                    nc.scalar.activation(dst, src, ACT.Copy).then_inc(att_copied, 1)

            def save(r):
                act.wait_ge(att_y, CREDIT + base + r + 1)
                dst, src = at["save"](r)
                nc.scalar.activation(dst, src, ACT.Copy).then_inc(att_saved, 1)

            exps(0)
            for r in range(n):
                early = nk == T
                if early and r < n - 1:
                    exps(r + 1)
                copy(r)
                if not early and r < n - 1:
                    exps(r + 1)
                save(r)
            cur.add("att", n)
            cur.add("att_c", n * len(chunks))
            cur.add("att_b", n if at["bias"] else 0)

        def att_dve(dve, cur, steps, at):
            nk, n = at["nk"], at["n"]
            base, cbase = cur.base("att"), cur.base("att_c")
            nch = len(att_chunks(at))
            def maxima(r):
                def read(ins):
                    ins.then_inc(att_read, 1)
                    dve.wait_ge(att_read, CREDIT + cur.base("att_b") + r + 1)
                dve.wait_ge(att_scores, CREDIT + base + r + 1)
                dve.wait_ge(att_exp, CREDIT + base + r - 1)
                src = scores_of(r, nk)
                if at["bias"]:
                    dve.wait_ge(att_turned, CREDIT + cbase + (r + 1 - t_places(nk)) * nch)
                    at["bias"](r, src, steps, t_of(r, nk), read)
                    src = t_of(r, nk)
                nc.vector.tensor_reduce(nmax[r % 2], src, AX.X, ALU.max, negate=True).then_inc(att_nmax, 1)

            def probs(r):
                dve.wait_ge(att_exp, CREDIT + base + r + 1)
                dve.wait_ge(att_probs, CREDIT + base + r)
                steps(nc.vector.reciprocal(rcp, sums_[r % 2]))
                if at["diff"]:
                    steps(nc.vector.tensor_scalar(rcp[:, 1, :], rcp[:, 1, :], nlam, None, ALU.mult))
                t = t_of(r, nk)
                ins = nc.vector.tensor_tensor(t, t, rcp.unsqueeze(3).to_broadcast([P, 2, 2, nk]), ALU.mult)
                if at["diff"]:
                    steps(ins)
                    ins = nc.vector.tensor_tensor(t[:, 0], t[:, 0], t[:, 1], ALU.add)
                ins.then_inc(att_probs, 1)

            maxima(0)
            for r in range(n):
                early = nk == T
                if early and r < n - 1:
                    maxima(r + 1)
                probs(r)
                if not early and r < n - 1:
                    maxima(r + 1)
            cur.add("att", n)
            cur.add("att_c", n * nch)
            cur.add("att_b", n if at["bias"] else 0)

        def pair_att(n, nk, q, q0, k, k0, v, v0, y, y0, bias=None, diff=False):
            kc = nk // P

            def qk(r, a, qt):
                h = slice(64 * a, 64 * a + 64)
                return [(q[h, r, q0 + qt * P:q0 + (qt + 1) * P], k[h, r, k0:k0 + nk])]

            def pv(r):
                if diff:
                    return [(0, slice(0, P), 0, [(v[:, v0 + k_, r * P:(r + 1) * P], pt_all[:, 0, k_, :])
                                                 for k_ in range(kc)])]
                return [(a, slice(64 * a, 64 * a + 64), 0,
                         [(v[:, v0 + k_, r * P + 64 * a:r * P + 64 * a + 64], pt_all[:, a, k_, :])
                          for k_ in range(kc)]) for a in range(2)]

            def save(r):
                return y[:, r, y0:y0 + T], ps[:, 6, 0:T]

            return dict(n=n, nk=nk, diff=diff, bias=bias, qk=qk, pv=pv, save=save)

        YT = wk(6400 + 6144, 4, DC, T)
        QT, KT, VT = wk(6400, DC, T), wk(6400 + 2048, DC, T), wk(6400 + 4096, TT, D)
        CUM = wk(6400 + 6144 + 4096, 16, T)
        Q2, K2, V2 = wk(6400, BC, 2 * T), wk(6400 + 2048, BC, 2 * T), wk(6400 + 4096, 4, BW)
        Y2 = wk(6400 + 6144, 3, BC, 2 * T)
        NAB = wk(6400 + 6144 + 2048, 4, 2, 2, T)
        MIXT = wk(0, DC, 2 * T)
        GATE = wk(4096, 4, 2 * T)

        XIN_TM = wk(0, 4, D)
        CTX_TM = wk(SPARE, 2, D)

        def turn_in_pe(pe, cur, src, tiles):
            for c in range(DC):
                bank_parts(pe, cur, [(P, m * P, P, [(src[:, tt, c * P:(c + 1) * P], ident)])
                                     for m, tt in enumerate(tiles)], turn=True)

        def turn_in_read(eng, who, cur, tiles, col0):
            n = len(tiles) * P
            for c in range(DC):
                def op(bank, c=c):
                    dst = XT[:, c, col0:col0 + n]
                    if who == "act":
                        return nc.scalar.activation(dst, bank[:, 0:n], ACT.Copy)
                    return nc.vector.tensor_copy(dst, bank[:, 0:n])
                read_bank(eng, cur, (who == "act") == (c % 2 == 0), op)

        def main_norm_pe(pe, cur, n, split=True):
            b = cur.bank()
            if cur.g >= NB:
                pe.wait_ge(bank_free[b], cur.bank_use())
            for c in range(DC):
                if c % 4 == 0:
                    pe.wait_ge(norm_sq, cur.base("sq") + c // 4 + 1)
                last = nc.tensor.matmul(ps[:, b, 0:n], ones, SQ[:, c, 0:n], start=(c == 0), stop=(c == DC - 1))
            last.then_inc(bank_full[b], 1)
            cur.g += 1
            cur.add("sq", 2)

        def main_norm_act(act, cur, steps, n, shift=None, split=True):
            for h in range(2):
                c = slice(4 * h, 4 * h + 4)
                nc.scalar.activation(SQ[:, c, 0:n], XT[:, c, 0:n], ACT.Square).then_inc(norm_sq, 1)
            g = cur.g
            act.wait_ge(bank_free[g % NB], g // NB + 1)
            nc.scalar.activation(RB[:, 0:n], RB[:, 0:n], ACT.Sqrt).then_inc(norm_sd, 1)
            skip_banks(cur, 1)
            for c in range(DC):
                for st in range(n // T):
                    tok = slice(st * T, (st + 1) * T)
                    if split or shift:
                        act.wait_ge(normed, cur.base("normed") + 1)
                    if split and shift:
                        nc.scalar.activation(AH[:, c, tok], HF[:, c, tok], ACT.Identity, bias=shift(c, st))\
                            .then_inc(x_hi, 1)
                    elif split:
                        nc.scalar.activation(AH[:, c, tok], HF[:, c, tok], ACT.Copy).then_inc(x_hi, 1)
                    elif shift:
                        nc.scalar.activation(HF[:, c, tok], HF[:, c, tok], ACT.Identity, bias=shift(c, st))
                    cur.add("normed", 1)
            cur.add("x", DC * n // T if split else 0)

        def main_norm_dve(dve, cur, steps, n, gain, shift=None, split=True):
            read_bank(dve, cur, True, lambda bank: nc.vector.tensor_scalar(
                RB[:, 0:n], bank[:, 0:n], 1.0 / D, EPS, ALU.mult, ALU.add))
            dve.wait_ge(norm_sd, cur.base("sd") + 1)
            steps(nc.vector.reciprocal(RB[:, 0:n], RB[:, 0:n]))

            def low(c):
                for st in range(n // T):
                    tok = slice(st * T, (st + 1) * T)
                    dve.wait_ge(x_hi, cur.base("x") + 1)
                    if shift:
                        nc.vector.scalar_tensor_tensor(AL[:, c, tok], HF[:, c, tok], shift(c, st), f32(AH[:, c, tok]),
                                                       ALU.add, ALU.subtract).then_inc(x_lo, 1)
                    else:
                        nc.vector.tensor_tensor(AL[:, c, tok], HF[:, c, tok], f32(AH[:, c, tok]), ALU.subtract)\
                            .then_inc(x_lo, 1)
                    cur.add("x", 1)

            for c in range(DC):
                for st in range(n // T):
                    tok = slice(st * T, (st + 1) * T)
                    nc.vector.scalar_tensor_tensor(HF[:, c, tok], XT[:, c, tok], gain(c, st), RB[:, tok],
                                                   ALU.mult, ALU.mult).then_inc(normed, 1)
                if split and c > 0:
                    low(c - 1)
            if split:
                low(DC - 1)
            cur.add("sd", 1)

        def norm_ready(pe, cur, n):
            base, per = cur.base("x"), n // T

            def ready(k):
                pe.wait_ge(x_lo, base + per * (k + 1))
            cur.add("x", DC * per)
            return ready

        def head_norm(parts, chunks, width, sums, spread):
            at, placed = 0, []
            for j, (x, n, gain, post) in enumerate(parts):
                placed.append((x[:, :, 0:n], wk(2048 * j, chunks, n), slice(at, at + n), gain, post))
                at += n
            return dict(parts=placed, cols=at, chunks=chunks, width=width, sums=sums, spread=spread)

        def head_norm_pe(pe, cur, h, between=lambda: None):
            b = cur.bank()
            pe.wait_ge(bank_free[b], cur.bank_use())
            for j, (_, sq, cols, _, _) in enumerate(h["parts"]):
                pe.wait_ge(norm_sq, cur.base("sq") + j + 1)
                for c in range(h["chunks"]):
                    last = nc.tensor.matmul(ps[0:16, b, cols], h["sums"](c), sq[:, c, :], start=(c == 0),
                                            stop=(c == h["chunks"] - 1))
            last.then_inc(bank_full[b], 1)
            cur.g += 1
            between()
            pe.wait_ge(norm_r, cur.base("r") + 1)
            for c in range(h["chunks"]):
                bank_parts(pe, cur, [(P, 0, h["cols"], [(h["spread"](c), rowst[:, 0:h["cols"]])])])
            cur.add("sq", len(h["parts"]))
            cur.add("r", 1)

        def head_norm_act(act, cur, steps, h, after_squares=lambda: None, between=lambda: None):
            for x, sq, _, _, _ in h["parts"]:
                nc.scalar.activation(sq, x, ACT.Square).then_inc(norm_sq, 1)
            after_squares()
            r = rowst[:, 0:h["cols"]]
            act.wait_ge(bank_free[cur.bank()], cur.bank_use(1))
            nc.scalar.activation(r, r, ACT.Sqrt).then_inc(norm_sd, 1)
            skip_banks(cur, 1)
            between()
            skip_banks(cur, h["chunks"])

        def qk_written(eng, cur, behind=0):
            for g in (cur.g - behind - 2, cur.g - behind - 1):
                eng.wait_ge(bank_free[g % NB], g // NB + 1)

        def head_norm_dve(dve, cur, steps, h, between=lambda: None):
            def means(bank):
                for _, _, cols, _, post in h["parts"]:
                    ins = nc.vector.tensor_scalar(rowst[:, cols], bank[0:16, cols], 1.0 / (h["width"] * post * post),
                                                  EPS / (post * post), ALU.mult, ALU.add)
                return ins
            read_bank(dve, cur, True, means)
            dve.wait_ge(norm_sd, cur.base("sd") + 1)
            r = rowst[:, 0:h["cols"]]
            nc.vector.reciprocal(r, r).then_inc(norm_r, 1)
            between()
            for c in range(h["chunks"]):
                def op(bank, c=c):
                    for x, _, cols, gain, _ in h["parts"]:
                        ins = nc.vector.scalar_tensor_tensor(x[:, c, :], x[:, c, :], gain(c), bank[:, cols],
                                                             ALU.mult, ALU.mult)
                    return ins
                read_bank(dve, cur, True, op)
            cur.add("sd", 1)

        row_sum = lambda j: cst("row_sum")[:, 16 * j:16 * j + 16]
        fox_norm = head_norm([(QT, T, lambda c: p1("fox_q_g"), HD ** -0.5), (KT, T, lambda c: p1("fox_k_g"), 1.0)],
                             DC, HD, lambda c: cst("head_sum")[:, 16 * c:16 * c + 16], lambda c: head_sel[:, c, :])
        mem_norm = head_norm([(QT, T, lambda c: p1("mem_q_g", c % 2), 256 ** -0.5),
                              (KT, T, lambda c: p1("mem_k_g", c % 2), 1.0)],
                             DC, 256, lambda c: row_sum(c // 2), lambda c: sel[:, c // 2, :])

        def qk_pe(pe, cur, kq=0, kk=0, ready=None):
            fm_banks(pe, cur, in_a(kq)(T), T, DC, ready=ready)
            fm_banks(pe, cur, in_a(kk)(T), T, DC)

        def v_pe(pe, cur, kv=0):
            for _ in range(2):
                tm_tile(pe, cur, kv, TT)

        def qk_read(eng, who, cur, q_scale=1.0):
            for dst, scale in ((QT, q_scale), (KT, 1.0)):
                for h in range(2):
                    copies(eng, who, cur, lambda j, h=h, dst=dst: dst[:, 4 * h + j, :], 4, T, scale)

        def v_read(eng, who, cur):
            for h in range(2):
                copies(eng, who, cur, lambda j, h=h: VT[:, j, h * 512:(h + 1) * 512], TT, 512, tm=True)


        def forget_pe(pe, cur):
            wf = p1("w_forget", 0, DC * 16).rearrange("p (k h) -> p k h", k=DC)
            bank_parts(pe, cur, [(16, 0, T, [(wf[:, k, :], HF[:, k, 0:T]) for k in range(DC)])])

        def forget_act(act, cur, steps):
            act.wait_ge(fox_z, 1)
            steps(nc.scalar.activation(FG[0:16, 1, :], FG[0:16, 0, :], ACT.Abs))
            steps(nc.scalar.activation(FG[0:16, 1, :], FG[0:16, 1, :], ACT.Exp, scale=-1.0))
            nc.scalar.activation(FG[0:16, 1, :], FG[0:16, 1, :], ACT.Ln, bias=1.0).then_inc(fox_e, 1)

        def forget_dve(dve, cur, steps):
            read_bank(dve, cur, True, lambda bank: nc.vector.tensor_scalar(
                FG[0:16, 0, :], bank[0:16, 0:T], p1("b_forget")[0:16], None, ALU.add))
            steps(nc.vector.memset(FG[0:16, 3, :], 1.0))
            dve.wait_ge(bank_free[(cur.g - 1) % NB], (cur.g - 1) // NB + 1)
            dve.drain().then_inc(fox_z, 1)
            dve.wait_ge(fox_e, 1)
            steps(nc.vector.scalar_tensor_tensor(FG[0:16, 2, :], FG[0:16, 0, :], 0.0, FG[0:16, 1, :],
                                                 ALU.min, ALU.subtract))
            nc.vector.tensor_tensor_scan(FG[0:16, 0, :], FG[0:16, 3, :], FG[0:16, 2, :], 0.0, ALU.mult, ALU.add)\
                .then_inc(fox_cum, 1)

        def forget_pool(pool, cur):
            pool.wait_ge(fox_cum, 1)
            pool.dma_start(a["cum_scratch"], FG[0:16, 0, :]).then_inc(loads, 16)
            pool.wait_ge(loads, 16 * LOADS["cum_out"])
            src = a["cum_scratch"].rearrange("h t -> (h t)").partition_broadcast(P)
            pool.dma_start(CUM.rearrange("p h t -> p (h t)"), src).then_inc(loads, 16)
            pool.wait_ge(loads, 16 * LOADS["cum_in"])

        def fox_bias(r, s4, steps, t, read):
            mask = cst("causal").rearrange("p (a b k) -> p a b k", a=1, b=2).to_broadcast([P, 2, 2, T])
            read(nc.vector.tensor_tensor(t, s4, mask, ALU.add))
            cum = CUM[:, 2 * r:2 * r + 2, :].unsqueeze(2).to_broadcast([P, 2, 2, T])
            steps(nc.vector.tensor_tensor(t, t, cum, ALU.subtract))

        fox = pair_att(HEADS // 2, T, QT, 0, KT, 0, VT, 0, YT[:, 0], 0, bias=fox_bias)

        def mem_qk(r, a_, qt):
            c = 4 * r + 2 * a_
            return [(QT[:, c + j, qt * P:(qt + 1) * P], KT[:, c + j, :]) for j in range(2)]

        def mem_pv(r):
            return [(a_ if d == 0 else 2, slice(0, P), (2 * a_ + d) * T, [(VT[:, k, (4 * r + 2 * a_ + d) * P:(4 * r + 2 * a_ + d + 1) * P],
                                         pt_all[:, a_, k, :]) for k in range(2)])
                    for a_ in range(2) for d in range(2)]

        def mem_save(r):
            return (YT[:, 3, 4 * r:4 * r + 4, :].rearrange("p (b c) t -> p b (c t)", b=2), ps[:, 6:8, :])

        mem_att = dict(n=2, nk=T, diff=False, bias=None, qk=mem_qk, pv=mem_pv, save=mem_save)

        SB_Z = [wk(at, 2, 2, T) for at in (0, 1024, SPARE, SPARE + 1024)]
        SB_L, SB_LN = ([wk(at, 2, 2, T), wk(at + 1024, 2, 2, T)] for at in (2048, 4096))
        z_ps = [ps[:, b:b + 2, :].rearrange("p a (k t) -> p a k t", k=2) for b in (0, 2)]
        incl_ps = ps[:, 4:6, :].rearrange("p a (k t) -> p a k t", k=2)
        SB_ROUNDS = HEADS // 2

        def sb_pe(pe, cur):
            def scores(r):
                pe.wait_ge(sb_l, CREDIT + r - 1)
                for a in range(2):
                    h = slice(64 * a, 64 * a + 64)
                    for kt in range(2):
                        last = nc.tensor.matmul(z_ps[r % 2][:, a, kt, :], KT[h, r, kt * P:(kt + 1) * P], QT[h, r, :],
                                                start=True, stop=True)
                last.then_inc(sb_z, 1)

            def sums(r):
                L = SB_L[r % 2]
                pe.wait_ge(sb_l, CREDIT + r + 1)
                pe.wait_ge(sb_logw, CREDIT + r)
                for a in range(2):
                    nc.tensor.matmul(incl_ps[:, a, 0, :], cst("tri"), L[:, a, 0, :], start=True, stop=False)
                    nc.tensor.matmul(incl_ps[:, a, 0, :], ones, L[:, a, 1, :], start=False, stop=True)
                    last = nc.tensor.matmul(incl_ps[:, a, 1, :], cst("tri"), L[:, a, 1, :], start=True, stop=True)
                last.then_inc(sb_incl, 1)

            def product(r):
                W = SB_Z[r % 4]
                pe.wait_ge(sb_w, CREDIT + r + 1)
                pe.wait_ge(sb_saved, CREDIT + r - 1)
                for a in range(2):
                    for kt in range(2):
                        last = nc.tensor.matmul(ps[64 * a:64 * a + 64, 6 + r % 2, 0:T],
                                                VT[:, kt, r * P + 64 * a:r * P + 64 * a + 64], W[:, a, kt, :],
                                                start=(kt == 0), stop=(kt == 1))
                last.then_inc(sb_y, 1)

            scores(0)
            scores(1)
            for r in range(SB_ROUNDS):
                sums(r)
                if r + 2 < SB_ROUNDS:
                    scores(r + 2)
                if r > 0:
                    product(r - 1)
            product(SB_ROUNDS - 1)

        def sb_act(act, cur, steps):
            for r in range(-1, SB_ROUNDS + 2):
                if r + 1 < SB_ROUNDS:
                    LN = SB_LN[(r + 1) % 2]
                    act.wait_ge(sb_z, CREDIT + r + 2)
                    act.wait_ge(sb_l, CREDIT + r)
                    nc.scalar.activation(LN, z_ps[(r + 1) % 2], ACT.Abs).then_inc(sb_abs, 1)
                    act.wait_ge(sb_abs, CREDIT + r + 2)
                    steps(nc.scalar.activation(LN, LN, ACT.Exp, scale=-1.0))
                if 0 <= r - 1 < SB_ROUNDS:
                    Z = SB_Z[(r - 1) % 4]
                    act.wait_ge(sb_logw, CREDIT + r)
                    nc.scalar.activation(Z, Z, ACT.Exp).then_inc(sb_w, 1)
                if r + 1 < SB_ROUNDS:
                    nc.scalar.activation(LN, LN, ACT.Ln, bias=1.0).then_inc(sb_ln, 1)
                if r - 2 >= 0:
                    act.wait_ge(sb_y, CREDIT + r - 1)
                    nc.scalar.activation(YT[:, 2, r - 2, :], ps[:, 6 + r % 2, 0:T], ACT.Copy).then_inc(sb_saved, 1)

        def sb_dve(dve, cur, steps):
            add = cst("sb_add").rearrange("p (a k t) -> p a k t", a=1, k=2).to_broadcast([P, 2, 2, T])
            neg = cst("sb_neg").rearrange("p (a k t) -> p a k t", a=1, k=2).to_broadcast([P, 2, 2, T])
            flat = lambda x: x.rearrange("p a k t -> p (a k t)")

            for r in range(-1, SB_ROUNDS):
                if r + 1 < SB_ROUNDS:
                    L, z = SB_L[(r + 1) % 2], z_ps[(r + 1) % 2]
                    dve.wait_ge(sb_y, CREDIT + r - 2)
                    dve.wait_ge(sb_abs, CREDIT + r + 2)
                    steps(nc.vector.tensor_tensor(SB_Z[(r + 1) % 4], z, add, ALU.add))
                if r >= 0:
                    Z = SB_Z[r % 4]
                    dve.wait_ge(sb_incl, CREDIT + r + 1)
                    nc.vector.tensor_tensor(Z, Z, incl_ps, ALU.add).then_inc(sb_logw, 1)
                if r + 1 < SB_ROUNDS:
                    dve.wait_ge(sb_ln, CREDIT + r + 2)
                    dve.wait_ge(sb_incl, CREDIT + r)
                    steps(nc.vector.scalar_tensor_tensor(flat(L), flat(z), 0.0, flat(SB_LN[(r + 1) % 2]), ALU.max,
                                                         ALU.add))
                    nc.vector.tensor_tensor(L, L, neg, ALU.mult).then_inc(sb_l, 1)

        LX, LG, LXC, LR, LI, LA = (wk(2048 * j, DC, T) for j in range(6))
        LW = wk(18688, 2, DC, P)
        LY = YT[:, 1]
        sp8 = small[:, 16:24]

        def lru_pe(pe, cur):
            pe.wait_ge(loads, 16 * LOADS["lru_w"])
            for c in range(DC):
                pe.wait_ge(lru_xc, c + 1)
                bank_parts(pe, cur, [(P, g * T, T, [(LW[:, g, c, :], LXC[:, c, :])]) for g in range(2)])

        def lru_start_act(act, cur, steps):
            tmp = small[:, 24:32]
            steps(nc.scalar.activation(tmp, p1("lam", 0, DC), ACT.Abs))
            steps(nc.scalar.activation(tmp, tmp, ACT.Exp, scale=-1.0))
            nc.scalar.activation(tmp, tmp, ACT.Ln, bias=1.0).then_inc(lru_ri, 1)

        def lru_act(act, cur, steps):
            for c in range(DC):
                def op(bank, c=c):
                    nc.scalar.activation(LR[:, c, :], bank[:, 0:T], ACT.Sigmoid, bias=p1("b_a", c))
                    return nc.scalar.activation(LI[:, c, :], bank[:, T:2 * T], ACT.Sigmoid, bias=p1("b_x", c))
                read_bank(act, cur, True, op)
            act.drain().then_inc(lru_gates, 1)
            act.wait_ge(lru_om, 1)
            nc.scalar.activation(LA[:, :, :], LR[:, :, :], ACT.Exp).then_inc(lru_a, 1)
            steps(nc.scalar.activation(LR[:, :, :], LR[:, :, :], ACT.Tanh, scale=-1.0))
            act.drain().then_inc(lru_a, 1)
            act.wait_ge(lru_om, 2)
            nc.scalar.activation(LR[:, :, :], LR[:, :, :], ACT.Sqrt).then_inc(lru_root, 1)

        def lru_start_dve(dve, cur, steps):
            nlm = small[:, 32:40]
            steps(nc.vector.tensor_scalar(nlm, p1("lam", 0, DC), -1.0, 0.0, ALU.mult, ALU.max))
            dve.wait_ge(lru_ri, 1)
            steps(nc.vector.tensor_tensor(sp8, nlm, small[:, 24:32], ALU.add))
            steps(nc.vector.tensor_scalar(sp8, sp8, -LRU_C, None, ALU.mult))

        def lru_conv_dve(dve, cur, steps, g, c):
            dve.wait_ge(bank_free[g % NB], g // NB + 1)
            steps(nc.vector.tensor_scalar(LXC[:, c, :], LX[:, c, :], p1("conv_w", 3 * DC + c),
                                          p1("conv_b", c), ALU.mult, ALU.add))
            for j in range(1, 4):
                ins = nc.vector.scalar_tensor_tensor(
                    LXC[:, c, j:T], LX[:, c, 0:T - j], p1("conv_w", (3 - j) * DC + c), LXC[:, c, j:T],
                    ALU.mult, ALU.add)
                if j < 3:
                    steps(ins)
            ins.then_inc(lru_xc, 1)

        def lru_dve(dve, cur, steps):
            skip_banks(cur, DC)
            dve.wait_ge(lru_gates, 1)
            for c in range(DC):
                ins = nc.vector.tensor_scalar(LR[:, c, :], LR[:, c, :], sp8[:, c:c + 1], None, ALU.mult)
            ins.then_inc(lru_om, 1)
            dve.wait_ge(lru_xc, DC)
            steps(nc.vector.tensor_tensor(LI[:, :, :], LI[:, :, :], LXC[:, :, :], ALU.mult))
            dve.wait_ge(lru_a, 2)
            steps(nc.vector.tensor_tensor(LXC[:, :, :], LA[:, :, :], LA[:, :, :], ALU.mult))
            flat = lambda x: x.rearrange("p a t -> p (a t)")
            nc.vector.scalar_tensor_tensor(flat(LR), flat(LXC), 1.0, flat(LR), ALU.add, ALU.mult)\
                .then_inc(lru_om, 1)
            dve.wait_ge(lru_root, 1)
            steps(nc.vector.tensor_tensor(LI[:, :, :], LI[:, :, :], LR[:, :, :], ALU.mult))
            for c in range(DC):
                ins = nc.vector.tensor_tensor_scan(LXC[:, c, :], LA[:, c, :], LI[:, c, :], 0.0, ALU.mult, ALU.add)
            steps(ins)
            steps(nc.vector.tensor_tensor(LY, LXC[:, :, :], LG[:, :, :], ALU.mult))

        def merge_loop(eng, cur, branches, kc, one_branch, steps=None, per=0):
            if 2 * (4 + kc // 2) % (2 * R) == 0:
                with loop(eng, cur, branches, pieces=2 * (4 + kc // 2), banks=16, steps=steps, steps_per=per) as i:
                    one_branch(i)
            else:
                for i in range(branches):
                    one_branch(i)

        def y_split(kc, n):
            v = WKR[:, 6400:6400 + 4096].rearrange("p (s k t) -> p s k t", s=2, k=kc)
            return v[:, 0, :, 0:n], v[:, 1, :, 0:n]

        def merge_pe(pe, cur, branches, kc, n):
            yh, yl = y_split(kc, n)

            def one_branch(i):
                for h in range(2):
                    fm_banks(pe, cur, in_a()(n), n, 4)
                    if h == 0:
                        pe.wait_ge(y_lo, cur.base("y") + 1 + i)
                    fm_banks(pe, cur, lambda k: (yh[:, k, :], yl[:, k, :]), n, 4, kc)
            merge_loop(pe, cur, branches, kc, one_branch)
            cur.add("y", branches)

        def merge_act(act, cur, branches, kc, n, y, bias):
            yh, _ = y_split(kc, n)

            def one_branch(i):
                for h in range(2):
                    act.wait_ge(gate_used, cur.base("merge") + 1 + h + i * 2)
                    if h == 0:
                        nc.scalar.activation(yh, y[:, one(i), :, 0:n].squeeze(1), ACT.Copy).then_inc(y_hi, 1)
                    for j in range(4):
                        def op(bank, j=j):
                            b = {} if bias is None else {"bias": bias(i, 4 * h + j)}
                            return nc.scalar.activation(GATE[:, j, 0:n], bank[:, 0:n], ACT.Sigmoid, **b)
                        read_bank(act, cur, True, op, piece=True)
                    skip_fm(act, cur, 4, kc)
            merge_loop(act, cur, branches, kc, one_branch)
            cur.add("merge", 2 * branches + 1)

        def merge_dve(dve, cur, steps, branches, kc, n, y):
            yh, yl = y_split(kc, n)
            steps(nc.vector.memset(MIXT[:, :, 0:n], 0.0))
            dve.drain().then_inc(gate_used, 1)
            cur.add("merge", 1)

            def one_branch(i):
                dve.wait_ge(y_hi, cur.base("y") + 1 + i)
                nc.vector.tensor_tensor(yl, y[:, one(i), :, 0:n].squeeze(1), f32(yh), ALU.subtract).then_inc(y_lo, 1)
                for h in range(2):
                    skip_fm(dve, cur, 4)
                    dve.wait_ge(bank_free[(cur.g - 1) % NB], cur.bank_use(0 if cur.g % NB == 0 else 1))
                    for j in range(4):
                        def op(bank, j=j):
                            steps(nc.vector.tensor_tensor(GATE[:, j, 0:n], GATE[:, j, 0:n], bank[:, 0:n], ALU.mult))
                            m = MIXT[:, 4 * h + j, 0:n]
                            return nc.vector.tensor_tensor(m, m, GATE[:, j, 0:n], ALU.add)
                        read_bank(dve, cur, True, op, piece=(kc == DC or j % 2 == 1))
                    dve.drain().then_inc(gate_used, 1)
            merge_loop(dve, cur, branches, kc, one_branch, steps=steps, per=8)
            cur.add("merge", 2 * branches)
            cur.add("y", branches)

        def out_pe(pe, cur, n):
            def ready(k):
                if k % 4 == 0:
                    pe.wait_ge(x_lo, cur.base("x") + k // 4 + 1)
            fm_banks(pe, cur, in_a()(n), n, DC, ready=ready)
            cur.add("x", 2)

        def out_act(act, cur, n):
            split_x_act(act, cur, [(MIXT[:, c:c + 4, 0:n], AH[:, c:c + 4, 0:n]) for c in (0, 4)])
            skip_fm(act, cur, DC)

        def out_dve(dve, cur, n, gain=None):
            split_x_dve(dve, cur, [(MIXT[:, c:c + 4, 0:n], AH[:, c:c + 4, 0:n], AL[:, c:c + 4, 0:n]) for c in (0, 4)])
            for h in range(2):
                for j in range(4):
                    c = 4 * h + j
                    def op(bank, c=c):
                        if gain is None:
                            return nc.vector.tensor_tensor(XT[:, c, 0:n], XT[:, c, 0:n], bank[:, 0:n], ALU.add)
                        for st in range(n // T):
                            tok = slice(st * T, (st + 1) * T)
                            ins = nc.vector.scalar_tensor_tensor(XT[:, c, tok], bank[:, tok], gain(c, st),
                                                                 XT[:, c, tok], ALU.mult, ALU.add)
                        return ins
                    read_bank(dve, cur, True, op, piece=True)

        FG_RAW = wk(0, 2, T)
        FH = wk(512, FC, T)
        UPS = FC // 2

        def up_pe(pe, cur):
            def tile_(_):
                fm_banks(pe, cur, in_a()(T), T, 4)
            up_loop(pe, cur, tile_)

        def up_loop(eng, cur, tile_, steps=None, per=0):
            with loop(eng, cur, 2, pieces=16, banks=16, steps=steps, steps_per=4 * per) as i:
                for j in range(4):
                    tile_(i * 4 + j)
            for j in range(8, UPS):
                tile_(j)

        def up_act(act, cur, steps):
            def tile_(n):
                skip_fm(act, cur, 3)
                for j in range(2):
                    act.wait_ge(conv_done, 2 * n + j + 1)
                    f = FH[:, one(2 * n + j), :]
                    nc.scalar.activation(f, f, ACT.Silu).then_inc(silu_done, 1)
                skip_fm(act, cur, 1)
            up_loop(act, cur, tile_)

        def up_dve(dve, cur, steps):
            def par1(name, i):
                lo = PAR1[name][0] + i
                return par[:, lo:lo + 1] if isinstance(lo, int) else par[:, bass.ds(lo, 1)]

            def tile_(n):
                for j in range(2):
                    f = FH[:, one(2 * n + j), :].squeeze(1)
                    def op(bank, j=j):
                        return nc.vector.tensor_copy(FG_RAW[:, j, :], bank[:, 0:T])
                    read_bank(dve, cur, True, op, piece=True)
                for j in range(2):
                    f = FH[:, one(2 * n + j), :].squeeze(1)
                    if j == 0:
                        dve.drain().then_inc(raw_gates, 1)
                        dve.wait_ge(raw_gates, n + 1)
                    steps(nc.vector.tensor_scalar(f, FG_RAW[:, j, :], par1("ffn_w", 2 * FC + 2 * n + j),
                                                  par1("ffn_b", 2 * n + j), ALU.mult, ALU.add))
                    steps(nc.vector.scalar_tensor_tensor(f[:, 1:T], FG_RAW[:, j, 0:T - 1], par1("ffn_w", FC + 2 * n + j),
                                                         f[:, 1:T], ALU.mult, ALU.add))
                    nc.vector.scalar_tensor_tensor(f[:, 2:T], FG_RAW[:, j, 0:T - 2], par1("ffn_w", 2 * n + j),
                                                   f[:, 2:T], ALU.mult, ALU.add).then_inc(conv_done, 1)
                    g = cur.g + j
                    dve.wait_ge(bank_full[g % NB], cur.bank_use(1 + g // NB - cur.g // NB))
                    dve.sem_inc(piece_used[cur.p % 4], 1)
                    next_piece(dve, cur)
                for j in range(2):
                    f = FH[:, one(2 * n + j), :].squeeze(1)
                    def op(bank, f=f):
                        return nc.vector.tensor_tensor(f, f, bank[:, 0:T], ALU.mult)
                    dve.wait_ge(silu_done, 2 * n + j + 1)
                    read_bank(dve, cur, True, op)
            up_loop(dve, cur, tile_, steps=steps, per=4)

        FHR = WKR[:, 6400:6400 + 2 * FC * T].rearrange("p (s k t) -> p s k t", s=2, k=FC)
        FGROUPS = [slice(0, 4), slice(4, 10), slice(10, 16), slice(16, FC)]

        def down_pe(pe, cur):
            def ready(k):
                for n, group in enumerate(FGROUPS):
                    if k == group.start:
                        pe.wait_ge(x_lo, cur.base("x") + n + 1)
            fm_banks(pe, cur, lambda k: (FHR[:, 0, k, :], FHR[:, 1, k, :]), T, DC, FC, ready=ready)
            cur.add("x", len(FGROUPS))

        def down_read(eng, cur, read):
            for piece in range(FC):
                c = (piece * 8 + 8) // FC - 1
                both = (piece * 8 + 8) % FC == 0
                if (piece * 8 + 8) // FC > piece * 8 // FC:
                    read_bank(eng, cur, read is not None, read and read(c), piece=both)
                if not both:
                    next_piece(eng, cur)

        def down_act(act, cur):
            split_x_act(act, cur, [(FH[:, s, :], FHR[:, 0, s, :]) for s in FGROUPS])
            down_read(act, cur, None)

        def down_dve(dve, cur):
            split_x_dve(dve, cur, [(FH[:, s, :], FHR[:, 0, s, :], FHR[:, 1, s, :]) for s in FGROUPS])

            def read(c):
                return lambda bank: nc.vector.tensor_tensor(XT[:, c, 0:T], XT[:, c, 0:T], bank[:, 0:T], ALU.add)
            down_read(dve, cur, read)

        cs = small[:, 40:56].rearrange("p (k s) -> p k s", k=DC)
        AF = A.rearrange("p a k t -> p (a k t)")
        ROWS = wk(0, 4, 512)

        def split_place(at):
            v = AF[:, at:at + XS_WORDS].rearrange("p (k c) -> p k c", k=DC)
            return v[:, :, 0:64], v[:, :, 64:128]

        def stationary(at, k):
            at = at + k * XS_CHUNK
            return AF[:, at:at + P], AF[:, at + 64:at + 64 + P]

        CS_HI, CS_LO = split_place(0)

        def rows_tile(pe, cur, xs, bank):
            for j in range(4):
                hi, lo = piece_of(pe, cur)
                for q in range(2):
                    k, w = 2 * j + q, slice(q * 512, q * 512 + 512)
                    last = three(ps[:, bank, :], xs(k), (hi[:, w], lo[:, w]), k == 0, k == DC - 1)
                if j < 3:
                    last.then_inc(piece_used[(cur.p - 1) % 4], 1)
            return last

        def ada_pe(pe, cur):
            pe.wait_ge(split_c, cur.base("ada") + 1)
            with loop(pe, cur, 3, pieces=16, banks=8):
                rows_in = {}

                def product(j):
                    b = cur.bank()
                    if cur.g >= NB:
                        pe.wait_ge(bank_free[b], cur.bank_use())
                    rows_tile(pe, cur, lambda k: stationary(0, k), b).then_inc(bank_full[b], 1)
                    rows_in[j] = b, cur.bank_use(1)
                    cur.g += 1

                def turn(j):
                    b, use = rows_in[j]
                    pe.wait_ge(bank_free[b], use)
                    bank_parts(pe, cur, [(P, 2 * c, 2, [(ROWS[0:2, j, c * P:(c + 1) * P], ident[0:2, 0:2])])
                                         for c in range(4)])
                product(0)
                for j in range(1, 4):
                    product(j)
                    turn(j - 1)
                turn(3)
            cur.add("ada", 1)

        def ada_act(act, cur, layer):
            act.wait_ge(loads, 16 * LOADS["par"][layer])
            nc.scalar.activation(cs, p2("c", 0, 2 * DC).rearrange("p (k s) -> p k s", k=DC), ACT.Silu)\
                .then_inc(silu_c, 1)
            act.wait_ge(silu_c, 2 * cur.base("ada") + 1)
            nc.scalar.activation(CS_HI[:, :, 0:2], cs, ACT.Copy).then_inc(silu_c, 1)
            with loop(act, cur, 3, pieces=16, banks=8):
                for _ in range(16):
                    next_piece(act, cur)
                skip_banks(cur, 8)
            cur.add("ada", 1)

        def ada_dve(dve, cur, steps, layer):
            dve.wait_ge(loads, 16 * LOADS["par"][layer])
            dve.wait_ge(silu_c, 2 * cur.base("ada") + 2)
            nc.vector.tensor_tensor(CS_LO[:, :, 0:2], cs, f32(CS_HI[:, :, 0:2]), ALU.subtract).then_inc(split_c, 1)
            with loop(dve, cur, 3, pieces=16, banks=8) as i:
                def rows(j):
                    next_piece(dve, cur, 3)
                    read_bank(dve, cur, True, lambda bank: nc.vector.tensor_copy(ROWS[0:2, j, :], bank[0:2, :]),
                              piece=True)

                def add_bias(j):
                    def op(bank):
                        lo = i * 16 + 4 * j
                        b = par[:, bass.ds(lo + PAR2["b_ada"][0], 4)].unsqueeze(2).to_broadcast([P, 4, 2])
                        return nc.vector.tensor_tensor(MOD[:, bass.ds(lo, 4), :],
                                                       bank[:, 0:8].rearrange("p (c s) -> p c s", c=4), b, ALU.add)
                    read_bank(dve, cur, True, op)
                rows(0)
                for j in range(1, 4):
                    rows(j)
                    add_bias(j - 1)
                add_bias(3)
            cur.add("ada", 1)

        def gmod_dve(dve, steps, g, which):
            gb = p2(g, 0, DC).unsqueeze(2).to_broadcast([P, DC, 2])
            steps(nc.vector.tensor_scalar(gmod[:, :, :], MOD[:, which * DC:(which + 1) * DC, :], 1.0, None, ALU.add))
            steps(nc.vector.tensor_tensor(gmod[:, :, :], gmod[:, :, :], gb, ALU.mult))

        def proj2_pe(pe, cur, nq, ready=None, between=lambda: None):
            fm_banks(pe, cur, in_a()(nq), nq, BC, ready=ready)
            fm_banks(pe, cur, in_a()(2 * T), 2 * T, BC)
            between()
            tm_tile(pe, cur, 0, 4)

        def proj2_read(eng, who, cur, nq, between=lambda: None):
            copies(eng, who, cur, lambda j: Q2[:, j, 0:nq], 4, nq, HD ** -0.5)
            copies(eng, who, cur, lambda j: K2[:, j, :], 4, 2 * T)
            between()
            copies(eng, who, cur, lambda j: V2[:, j, :], 4, BW, tm=True)

        def na_bias(r, s4, steps, t, read):
            steps(nc.vector.tensor_tensor(t[:, :, :, 0:T], s4[:, :, :, 0:T], NAB[:, r], ALU.add))
            read(nc.vector.tensor_copy(t[:, :, :, T:2 * T], s4[:, :, :, T:2 * T]))

        na_x = pair_att(4, 2 * T, Q2, 0, K2, 0, V2, 0, Y2[:, 0], 0, bias=na_bias)
        na_ctx = pair_att(4, T, Q2, T, K2, T, V2, 2, Y2[:, 0], T)
        da_x = pair_att(4, 2 * T, Q2, 0, K2, 0, V2, 0, Y2[:, 1], 0, diff=True)
        da_ctx = pair_att(4, T, Q2, T, K2, T, V2, 2, Y2[:, 1], T, diff=True)

        ROT = wk(0, BC, T)

        def rope_pe(pe, cur):
            assert NB == 2 * BC
            for x in (Q2, K2):
                for c in range(BC):
                    bank_parts(pe, cur, [(P, 0, T, [(cst("swap"), x[:, c, 0:T])])])

        def rope_dve(dve, cur, steps):
            for x in (Q2, K2):
                for c in range(BC):
                    def op(bank, c=c):
                        return nc.vector.tensor_tensor(ROT[:, c, :], bank[:, 0:T], cst("sin"), ALU.mult)
                    read_bank(dve, cur, True, op)
                dve.drain().then_inc(rope_r, 1)
                cur.add("rope", 1)
                dve.wait_ge(rope_r, cur.base("rope"))
                cos = cst("cos").unsqueeze(1).to_broadcast([P, BC, T])
                steps(nc.vector.tensor_tensor(x[:, :, 0:T], x[:, :, 0:T], cos, ALU.mult))
                steps(nc.vector.tensor_tensor(x[:, :, 0:T], x[:, :, 0:T], ROT, ALU.add))

        lamp = small[:, 56:58]

        def lam_pe(pe, cur):
            pe.wait_ge(lam_prod, cur.base("lam") * 2 + 1)
            bank_parts(pe, cur, [(P, 0, 2, [(ones, lamp)])])
            cur.add("lam", 1)

        def lam_act(act, cur):
            read_bank(act, cur, True, lambda bank: nc.scalar.activation(small[:, 58:60], bank[:, 0:2], ACT.Exp))

        def lam_start_dve(dve):
            nc.vector.tensor_tensor(lamp, p2("lam_q", 0, 2), p2("lam_k", 0, 2), ALU.mult).then_inc(lam_prod, 1)

        def lam_dve(dve, cur, steps, lam_init, g):
            dve.wait_ge(bank_free[g % NB], g // NB + 1)
            steps(nc.vector.tensor_tensor(nlam, small[:, 59:60], small[:, 58:59], ALU.subtract))
            steps(nc.vector.tensor_scalar(nlam, nlam, -lam_init, None, ALU.add))
            dve.drain().then_inc(lam_prod, 1)

        def da_norm(n, lam_init):
            return head_norm([(Y2[:, 1], n, lambda c: p2("subln"), 1.0 - lam_init)], BC, P, row_sum,
                             lambda c: sel[:, c, :])

        GU, GV = wk(0, 4, BW), wk(2048, 4, BW)
        GWS = wk(6400, 4, P)
        GLN = wk(6400 + 512, 2, BW)
        GST = wk(6400 + 1536, 4, 8)

        def gmlp_read(eng, who, cur, tt, dst):
            copies(eng, who, cur, lambda j: dst[:, j, :], tt, BW, func=ACT.Gelu_apprx_tanh, tm=True)

        def gmlp_ln_dve(dve, cur, steps, tt, layer):
            for m in range(tt):
                steps(nc.vector.bn_stats(GST[:, m, 0:6], GV[:, m, :]))
                steps(nc.vector.bn_aggr(GST[:, m, 6:8], GST[:, m, 0:6]))
            var = GST[:, 0:tt, 7:8]
            nc.vector.tensor_scalar(var, var, EPS, None, ALU.add).then_inc(ln_var, 1)
            dve.wait_ge(ln_sd, layer + 1)
            steps(nc.vector.reciprocal(var, var))
            dve.wait_ge(loads, 16 * LOADS["ln"][layer])
            for m in range(tt):
                v = GV[:, m, :]
                steps(nc.vector.tensor_scalar(v, v, GST[:, m, 6:7], GST[:, m, 7:8], ALU.subtract, ALU.mult))
                steps(nc.vector.tensor_tensor(v, v, GLN[:, 0, :], ALU.mult))
                ins = nc.vector.tensor_tensor(v, v, GLN[:, 1, :], ALU.add)
            ins.then_inc(ln_done, 1)

        def gmlp_ln_act(act, tt, layer):
            act.wait_ge(ln_var, layer + 1)
            var = GST[:, 0:tt, 7:8]
            nc.scalar.activation(var, var, ACT.Sqrt).then_inc(ln_sd, 1)

        def gmlp_mix_pe(pe, cur, tt, layer):
            pe.wait_ge(loads, 16 * LOADS["ln"][layer])
            pe.wait_ge(ln_done, layer + 1)
            for m in range(tt):
                bank_parts(pe, cur, [(P, g * P, P, [(GWS[:, g, :], GV[:, m, g * P:(g + 1) * P])]) for g in range(4)])
            for m in range(tt):
                g = cur.g - tt
                pe.wait_ge(bank_free[g % NB], g // NB + 1)
                bank_parts(pe, cur, [(P, c * P, P, [(GU[:, m, c * P:(c + 1) * P], ident)]) for c in range(BC)], turn=True)

        def gmlp_mix_dve(dve, cur, steps, tt):
            for m in range(tt):
                def op(bank, m=m):
                    for g in range(4):
                        u = GU[:, m, g * P:(g + 1) * P]
                        ins = nc.vector.scalar_tensor_tensor(u, bank[:, g * P:(g + 1) * P], p2("b_s", g), u,
                                                             ALU.add, ALU.mult)
                    return ins
                read_bank(dve, cur, True, op)
            skip_banks(cur, tt)

        def gmlp_mix_act(act, cur, tt):
            skip_banks(cur, tt)
            for m in range(tt):
                read_bank(act, cur, True, lambda bank, m=m: nc.scalar.activation(
                    Y2[:, 2, :, m * P:(m + 1) * P], bank.rearrange("p (c t) -> p c t", c=BC), ACT.Copy))

        XIN = wk(0, DC, 2, EXPERTS * CAP)
        YE = wk(8192, 2, 4, D)
        H2 = wk(8192, 4, D)
        GT = wk(16384, 2, 4, T)
        PH = wk(18432, 4, EXPERTS * CAP)
        AFF = small[:, 0:64].rearrange("p (m e) -> p m e", m=4)
        H2_HI, H2_LO = (A[:, j].rearrange("p k t -> p (k t)").rearrange("p (m d) -> p m d", m=4) for j in range(2))
        ONE = WKR[:, 18432:18432 + 4 * EXPERTS * CAP].rearrange("p (m e) -> p m e", m=4)
        XS_AT = [0, XS_WORDS]
        HIDT_AT = 2 * XS_WORDS
        HIDT_HI, HIDT_LO = split_place(HIDT_AT)
        SG, HID = wk(18432, 2, 512), wk(18432 + 1024, 2, 512)
        CMP, RANKS, AUX = wk(16384, 2, 8, T), wk(4096, 2, 4, EXPERTS), wk(4224, 8)
        AFFT = rowst

        def route_pe(pe, cur, st):
            tt = 2 * st
            wr = p2("w_router", 0, DC * 16).rearrange("p (k e) -> p k e", k=DC)
            bank_parts(pe, cur, [(P, m * 16, 16, [(HF[:, k, m * P:(m + 1) * P], wr[:, k, :]) for k in range(DC)])
                                 for m in range(tt)])
            for m in range(tt):
                for h in range(2):
                    bank_parts(pe, cur, [(P, c * P, P, [(HF[:, 4 * h + c, m * P:(m + 1) * P], ident)])
                                         for c in range(4)], turn=True)
            pe.wait_ge(affinities, cur.base("route") + 1)
            bank_parts(pe, cur, [(16, m * P, P, [(AFF[:, m, :], ident)]) for m in range(tt)], turn=True)
            g = cur.g - 1
            pe.wait_ge(bank_free[g % NB], g // NB + 1)
            for e in range(EXPERTS):
                bank_parts(pe, cur, [(P, 0, st * T, [(sel[:, e, :], AFFT[:, 0:st * T])])])
            pe.wait_ge(onehot, 2 * cur.base("route") + 1)
            pe.wait_ge(h2_lo, cur.base("h2") + tt)
            for s in range(st):
                for c in range(DC):
                    bank_parts(pe, cur, [(P, 0, 512, [(part[:, 2 * s + m, c * P:(c + 1) * P], ONE[:, 2 * s + m, :])
                                                      for m in range(2) for part in (H2_HI, H2_LO)])])
            cur.add("h2", tt)
            pe.wait_ge(onehot, 2 * cur.base("route") + 2)
            for s in range(st):
                for half in range(2):
                    bank_parts(pe, cur, [(P, g_ * T + m * P, P, [(PH[:, 2 * s + m, (2 * half + g_) * P:(2 * half + g_ + 1) * P], ident)])
                                         for g_ in range(2) for m in range(2)], turn=True)
            cur.add("route", 1)

        def route_act(act, cur, steps, st):
            tt = 2 * st
            act.wait_ge(aff_logits, cur.base("route") + 1)
            skip_banks(cur, 1)
            nc.scalar.activation(AFF[:, 0:tt, :], AFF[:, 0:tt, :], ACT.Exp).then_inc(aff_exp, 1)
            for m in range(tt):
                for h in range(2):
                    read_bank(act, cur, True, lambda bank, m=m, h=h: nc.scalar.activation(
                        H2[:, m, h * 512:(h + 1) * 512], bank, ACT.Copy))
            read_bank(act, cur, True, lambda bank: nc.scalar.activation(AFFT[:, 0:st * T], bank[0:16, 0:st * T], ACT.Copy))
            for m in range(tt):
                if m == 0:
                    act.wait_ge(bank_free[(cur.g - 1) % NB], (cur.g - 1) // NB + 1)
                nc.scalar.activation(H2_HI[:, m, :], H2[:, m, :], ACT.Copy).then_inc(h2_hi, 1)
            skip_banks(cur, EXPERTS)
            for s in range(st):
                for c in range(DC):
                    read_bank(act, cur, c % 2 == 0, lambda bank, s=s, c=c: nc.scalar.activation(XIN[:, c, s, :], bank, ACT.Copy))
            for s in range(st):
                for half in range(2):
                    read_bank(act, cur, True, lambda bank, s=s, half=half: nc.scalar.activation(
                        GT[:, s, 2 * half:2 * half + 2, :], bank.rearrange("p (g t) -> p g t", g=2), ACT.Copy))
            cur.add("route", 1)

        def route_pool(pool, cur, st):
            for m in range(2 * st):
                pool.wait_ge(h2_hi, cur.base("h2") + m + 1)
                nc.gpsimd.tensor_tensor(H2_LO[:, m, :], H2[:, m, :], f32(H2_HI[:, m, :]), ALU.subtract).then_inc(h2_lo, 1)
            cur.add("h2", 2 * st)

        def route_dve(dve, cur, steps, st):
            tt = 2 * st
            aff = AFF[:, 0:tt, :]
            aux = AUX[:, 0:tt]
            wide = lambda x: x.unsqueeze(2).to_broadcast([P, tt, 16])
            g = cur.g
            dve.wait_ge(bank_full[g % NB], g // NB + 1)
            lg = ps[:, g % NB, 0:16 * tt].rearrange("p (m e) -> p m e", m=tt)
            steps(nc.vector.tensor_reduce(aux, lg, AX.X, ALU.max))
            read_bank(dve, cur, True, lambda bank: nc.vector.tensor_tensor(aff, lg, wide(aux), ALU.subtract))
            dve.drain().then_inc(aff_logits, 1)
            dve.wait_ge(aff_exp, cur.base("route") + 1)
            steps(nc.vector.tensor_reduce(aux, aff, AX.X, ALU.add))
            steps(nc.vector.reciprocal(aux, aux))
            nc.vector.tensor_tensor(aff, aff, wide(aux), ALU.mult).then_inc(affinities, 1)
            dve.wait_ge(affinities, cur.base("route") + 1)
            skip_banks(cur, 2 * tt + 1)
            before = cst("before").rearrange("p (m t) -> p m t", m=2)
            for e in range(EXPERTS):
                if e >= 2:
                    dve.wait_ge(bank_free[(cur.g - 2) % NB], (cur.g - 2) // NB + 1)

                def op(bank, e=e):
                    for s in range(st):
                        for m in range(2):
                            row, av = bank[:, s * T:(s + 1) * T], AFF[:, 2 * s + m, e:e + 1]
                            nc.vector.tensor_scalar(CMP[:, e % 2, 4 * s + 2 * m, :], row, av, 0.0, ALU.is_gt, ALU.add,
                                                    accum_out=RANKS[:, 0, 2 * s + m, e:e + 1])
                            k = (m + 1) * P
                            ins = nc.vector.scalar_tensor_tensor(CMP[:, e % 2, 4 * s + 2 * m + 1, 0:k], row[:, 0:k], av,
                                                                 before[:, m, 0:k],
                                                                 ALU.is_equal, ALU.mult,
                                                                 accum_out=RANKS[:, 1, 2 * s + m, e:e + 1])
                    return ins
                read_bank(dve, cur, True, op)
            dve.wait_ge(bank_free[(cur.g - 1) % NB], (cur.g - 1) // NB + 1)
            steps(nc.vector.tensor_tensor(RANKS[:, 0, 0:tt], RANKS[:, 0, 0:tt], RANKS[:, 1, 0:tt], ALU.add))
            slots = cst("slots").unsqueeze(1).to_broadcast([P, EXPERTS, CAP])
            one_hot = ONE.rearrange("p m (e s) -> p m e s", e=EXPERTS)
            ph = PH.rearrange("p m (e s) -> p m e s", e=EXPERTS)
            for m in range(tt):
                ins = nc.vector.tensor_tensor(one_hot[:, m], slots, RANKS[:, 0, m, :].unsqueeze(2).to_broadcast([P, EXPERTS, CAP]),
                                              ALU.is_equal)
            ins.then_inc(onehot, 1)
            for s in range(st):
                for c in range(DC):
                    read_bank(dve, cur, c % 2 == 1, lambda bank, s=s, c=c: nc.vector.tensor_copy(XIN[:, c, s, :], bank))
            for b in range(NB):
                last = cur.g - 1 - (cur.g - 1 - b) % NB
                dve.wait_ge(bank_full[b], last // NB + 1)
            for m in range(tt):
                ins = nc.vector.tensor_tensor(ph[:, m], f32(one_hot[:, m]), AFF[:, m, :].unsqueeze(2).to_broadcast([P, EXPERTS, CAP]),
                                              ALU.mult)
            ins.then_inc(onehot, 1)
            skip_banks(cur, 2 * st)
            cur.add("route", 1)

        HB = [0, 2]
        def experts(eng, cur, one_expert, steps=None, per=0):
            with loop(eng, cur, EXPERTS // 4, pieces=96, steps=steps, steps_per=per) as i:
                for j in range(4):
                    one_expert(i, j, cur.base("moe") + j + i * 4)
            cur.add("moe", EXPERTS)

        def experts_pe(pe, cur, st):
            rows = CAP * st

            def turn(e, h):
                pe.wait_ge(moe_hid, CREDIT + 2 * e + h + 1)
                pe.wait_ge(moe_split, CREDIT + 2 * e + h - 1)
                for c in range(4):
                    last = nc.tensor.matmul(ps[:, 4 + h, c * rows:(c + 1) * rows],
                                            HID[0:rows, h, c * P:(c + 1) * P], ident[0:rows, 0:rows],
                                            start=True, stop=True)
                last.then_inc(moe_turned, 1)

            def down(n, j):
                hi, lo = piece_of(pe, cur)
                for q in range(2):
                    k, w = 2 * j + q, slice(q * 512, q * 512 + 512)
                    last = three(ps[:, 6 + n, :], stationary(HIDT_AT, k), (hi[:, w], lo[:, w]), k == 0, k == DC - 1)
                if j < 3:
                    last.then_inc(piece_used[(cur.p - 1) % 4], 1)
                else:
                    last.then_inc(moe_y, 1)

            def one_expert(i, j, e):
                xs = lambda k: stationary(XS_AT[j % 2], k)
                pe.wait_ge(moe_staged, CREDIT + e + 1)
                for h in range(2):
                    pe.wait_ge(moe_hid, CREDIT + 2 * e + h - 1)
                    rows_tile(pe, cur, xs, HB[h]).then_inc(piece_used[(cur.p - 1) % 4], 1)
                    if h == 1:
                        turn(e, 0)
                    rows_tile(pe, cur, xs, HB[h] + 1).then_inc(moe_h, 1)
                pe.wait_ge(moe_split, CREDIT + 2 * e + 1)
                pe.wait_ge(moe_saved[0], CREDIT + e)
                down(0, 0)
                down(0, 1)
                turn(e, 1)
                pe.wait_ge(moe_saved[1], CREDIT + e)
                down(1, 0)
                down(1, 1)
                pe.wait_ge(moe_split, CREDIT + 2 * e + 2)
                down(0, 2)
                down(0, 3)
                down(1, 2)
                down(1, 3)
            experts(pe, cur, one_expert)

        def experts_act(act, cur, st):
            rows = CAP * st

            def silu(e, h):
                act.wait_ge(moe_h, CREDIT + 2 * e + h + 1)
                act.sem_inc(piece_used[(cur.p - 1) % 4], 1)
                act.wait_ge(moe_hid, CREDIT + 2 * e + h - 1)
                nc.scalar.activation(SG[0:rows, h, :], ps[0:rows, HB[h], :], ACT.Silu).then_inc(moe_silu, 1)

            def copy_turned(e, h):
                act.wait_ge(moe_turned, CREDIT + 2 * e + h + 1)
                act.wait_ge(moe_y, CREDIT + 2 * e)
                nc.scalar.activation(HIDT_HI[:, 4 * h:4 * h + 4, 0:rows],
                                     ps[:, 4 + h, 0:4 * rows].rearrange("p (c s) -> p c s", c=4), ACT.Copy)\
                    .then_inc(moe_copied, 1)

            def one_expert(i, j, e):
                next_piece(act, cur, 7)
                cur.p += 1
                silu(e, 0)
                split_hi(act, cur)
                next_piece(act, cur, 5)
                copy_turned(e, 0)
                next_piece(act, cur, 2)
                cur.p += 1
                silu(e, 1)
                split_hi(act, cur)
                next_piece(act, cur, 1)
                copy_turned(e, 1)
                next_piece(act, cur, 6)
                cur.p += 1
                act.wait_ge(moe_y, CREDIT + 2 * e + 2)
                act.sem_inc(piece_used[(cur.p - 1) % 4], 1)
                for s in range(st):
                    ins = nc.scalar.activation(YE[CAP * j:CAP * (j + 1), s, one(i), 512:1024],
                                               ps[CAP * s:CAP * (s + 1), 7:8, :], ACT.Copy)
                ins.then_inc(moe_saved[1], 1)
                split_hi(act, cur)
            experts(act, cur, one_expert)

        def experts_dve(dve, cur, st):
            rows = CAP * st

            def gate(e, h):
                dve.wait_ge(moe_silu, CREDIT + 2 * e + h + 1)
                dve.wait_ge(moe_turned, CREDIT + 2 * e + h - 1)
                nc.vector.tensor_tensor(HID[0:rows, h, :], SG[0:rows, h, :], ps[0:rows, HB[h] + 1, :], ALU.mult)\
                    .then_inc(moe_hid, 1)

            def split_turned(e, h):
                dve.wait_ge(moe_copied, CREDIT + 2 * e + h + 1)
                k = slice(4 * h, 4 * h + 4)
                nc.vector.tensor_tensor(HIDT_LO[:, k, 0:rows],
                                        ps[:, 4 + h, 0:4 * rows].rearrange("p (c s) -> p c s", c=4),
                                        f32(HIDT_HI[:, k, 0:rows]), ALU.subtract).then_inc(moe_split, 1)

            def one_expert(i, j, e):
                next_piece(dve, cur, 7)
                gate(e, 0)
                next_piece(dve, cur, 6)
                split_turned(e, 0)
                next_piece(dve, cur, 2)
                gate(e, 1)
                next_piece(dve, cur, 2)
                split_turned(e, 1)
                next_piece(dve, cur, 4)
                cur.p += 1
                dve.wait_ge(moe_y, CREDIT + 2 * e + 1)
                dve.sem_inc(piece_used[(cur.p - 1) % 4], 1)
                for s in range(st):
                    ins = nc.vector.tensor_copy(YE[CAP * j:CAP * (j + 1), s, one(i), 0:512],
                                                ps[CAP * s:CAP * (s + 1), 6:7, :])
                ins.then_inc(moe_saved[0], 1)
                split_lo(dve, cur)
                next_piece(dve, cur, 2)
            experts(dve, cur, one_expert)

        def experts_pool(pool, cur, steps, st):
            def one_expert(i, j, e):
                pool.wait_ge(moe_h, CREDIT + 2 * e - 2)
                hi, lo = split_place(XS_AT[j % 2])
                place = bass.ds(i * (4 * CAP) + j * CAP, CAP)
                for s in range(st):
                    ins = nc.gpsimd.tensor_copy(hi[:, :, CAP * s:CAP * (s + 1)], XIN[:, :, s, place])
                steps(ins)
                pool.sem_inc(pool_step, 1)
                steps.n += 1
                for s in range(st):
                    to = slice(CAP * s, CAP * (s + 1))
                    ins = nc.gpsimd.tensor_tensor(lo[:, :, to], XIN[:, :, s, place], f32(hi[:, :, to]), ALU.subtract)
                ins.then_inc(moe_staged, 1)
                cur.p += 24
            experts(pool, cur, one_expert, steps=steps, per=8)

        def scatter_pe(pe, cur, st):
            for c in range(DC):
                bank_parts(pe, cur, [(P, s * T, T, [(YE[:, s, g, c * P:(c + 1) * P], GT[:, s, g, :]) for g in range(4)])
                                     for s in range(st)])

        def scatter_dve(dve, cur, st):
            for c in range(DC):
                def op(bank, c=c):
                    for s in range(st):
                        tok = slice(s * T, (s + 1) * T)
                        ins = nc.vector.scalar_tensor_tensor(XT[:, c, tok], bank[:, tok], MOD[:, 5 * DC + c, s:s + 1],
                                                             XT[:, c, tok], ALU.mult, ALU.add)
                    return ins
                read_bank(dve, cur, True, op)

        OUT = wk(8192, TT, D)

        def turn_out_pe(pe, cur):
            for m in range(TT):
                for h in range(2):
                    bank_parts(pe, cur, [(P, c * P, P, [(HF[:, 4 * h + c, m * P:(m + 1) * P], ident)])
                                         for c in range(4)], turn=True)

        def turn_out_act(act, cur):
            for m in range(TT):
                for h in range(2):
                    read_bank(act, cur, True, lambda bank, m=m, h=h: nc.scalar.activation(
                        OUT[:, m, h * 512:(h + 1) * 512], bank, ACT.Copy))

        LOADS = {"start": 3, "cum_out": 4, "cum_in": 5, "lru_w": 6}
        LOADS["par"] = [8 + 5 * l for l in range(LAYERS)]
        LOADS["nab"] = [LOADS["par"][l] + 1 for l in range(LAYERS)]
        LOADS["ln"] = [LOADS["par"][l] + 4 for l in range(LAYERS)]

        block = ctx.enter_context(nc.Block())
        ended = []

        @block.sync
        def _(sp):
            def load(t, j):
                sp.dma_start(ring[:, j, :], a["stream"][one(t)].rearrange("a p w -> (a p) w")).then_inc(landed[j], 16)

            sp.dma_start(const[:, 0:P], a["const"][:, 0:P]).then_inc(first_loads, 16)
            sp.dma_start(XIN_TM[:, 0:2, :], a["x"].rearrange("a (m p) d -> p (a m) d", p=P)).then_inc(first_loads, 16)
            sp.dma_start(XIN_TM[:, 2:4, :], a["mem"].rearrange("a (m p) d -> p (a m) d", p=P)).then_inc(first_loads, 16)
            sp.dma_start(const[:, P:], a["const"][:, P:]).then_inc(const_load, 16)
            for j in range(R):
                load(j, j)
            with sp.Fori(0, N_SLOTS // R - 1) as i:
                for j in range(R):
                    q = 2 * j + 1
                    sp.wait_ge(piece_used[q % 4], i * 2 + (q // 4 + 1))
                    load(i * R + (R + j), j)
            turns = N_SLOTS // R - 1
            for j in range(N_SLOTS % R):
                q = 2 * j + 1
                sp.wait_ge(piece_used[q % 4], turns * 2 + q // 4 + 1)
                load(R * (turns + 1) + j, j)

        @block.tensor
        def _(pe):
            cur = Cursor("pe")
            pe.wait_ge(first_loads, 16 * 3)
            turn_in_pe(pe, cur, XIN_TM, range(4))
            barrier(pe, cur)
            main_norm_pe(pe, cur, 2 * T)
            qk_pe(pe, cur, ready=norm_ready(pe, cur, 2 * T))
            forget_pe(pe, cur)
            head_norm_pe(pe, cur, fox_norm, between=lambda: v_pe(pe, cur))
            barrier(pe, cur)
            att_pe(pe, cur, fox)
            barrier(pe, cur)
            fm_banks(pe, cur, in_a()(T), T, 2 * DC)
            lru_pe(pe, cur)
            barrier(pe, cur)
            qk_pe(pe, cur)
            v_pe(pe, cur)
            barrier(pe, cur)
            sb_pe(pe, cur)
            barrier(pe, cur)
            qk_pe(pe, cur, 0, T)
            head_norm_pe(pe, cur, mem_norm, between=lambda: v_pe(pe, cur, T))
            barrier(pe, cur)
            att_pe(pe, cur, mem_att)
            barrier(pe, cur)
            merge_pe(pe, cur, 4, DC, T)
            barrier(pe, cur)
            out_pe(pe, cur, T)
            barrier(pe, cur)
            main_norm_pe(pe, cur, T)
            norm_ready(pe, cur, T)(DC - 1)
            up_pe(pe, cur)
            barrier(pe, cur)
            down_pe(pe, cur)
            barrier(pe, cur)
            pe.wait_ge(loads, 16 * LOADS["par"][0])
            turn_in_pe(pe, cur, CTX_TM, range(2))
            for layer in range(LAYERS):
                n = T if layer == LAYERS - 1 else 2 * T
                ada_pe(pe, cur)
                barrier(pe, cur)
                main_norm_pe(pe, cur, 2 * T)
                proj2_pe(pe, cur, n, ready=norm_ready(pe, cur, 2 * T))
                barrier(pe, cur)
                att_pe(pe, cur, na_x)
                barrier(pe, cur)
                if n > T:
                    att_pe(pe, cur, na_ctx)
                    barrier(pe, cur)
                proj2_pe(pe, cur, n, between=lambda: (rope_pe(pe, cur), lam_pe(pe, cur)))
                barrier(pe, cur)
                att_pe(pe, cur, da_x)
                barrier(pe, cur)
                if n > T:
                    att_pe(pe, cur, da_ctx)
                    barrier(pe, cur)
                head_norm_pe(pe, cur, da_norm(n, 0.0), between=lambda: tm_tile(pe, cur, 0, n // P))
                tm_tile(pe, cur, 0, n // P)
                barrier(pe, cur)
                gmlp_mix_pe(pe, cur, n // P, layer)
                barrier(pe, cur)
                merge_pe(pe, cur, 3, BC, n)
                barrier(pe, cur)
                out_pe(pe, cur, n)
                barrier(pe, cur)
                main_norm_pe(pe, cur, n, split=False)
                barrier(pe, cur)
                route_pe(pe, cur, n // T)
                barrier(pe, cur)
                experts_pe(pe, cur, n // T)
                barrier(pe, cur)
                scatter_pe(pe, cur, n // T)
                barrier(pe, cur)
            main_norm_pe(pe, cur, T, split=False)
            barrier(pe, cur)
            turn_out_pe(pe, cur)
            barrier(pe, cur)
            ended.append((cur.stage, cur.p, cur.g))

        @block.scalar
        def _(act):
            cur = Cursor("act")
            steps = Steps(act, act_step)
            turn_in_read(act, "act", cur, range(4), 0)
            for _ in range(AHEAD):
                split_hi(act, cur)
            barrier(act, cur)
            main_norm_act(act, cur, steps, 2 * T)
            qk_read(act, "act", cur)
            skip_banks(cur, 1)
            qk_written(act, cur, 1)
            act.wait_ge(bank_full[(cur.g - 1) % NB], (cur.g - 1) // NB + 1)
            head_norm_act(act, cur, steps, fox_norm, after_squares=lambda: forget_act(act, cur, steps),
                          between=lambda: v_read(act, "act", cur))
            barrier(act, cur)
            att_act(act, cur, steps, fox)
            barrier(act, cur)
            lru_start_act(act, cur, steps)
            for h in range(2):
                copies(act, "act", cur, lambda j, h=h: LX[:, 4 * h + j, :], 4, T)
            for h in range(2):
                copies(act, "act", cur, lambda j, h=h: LG[:, 4 * h + j, :], 4, T, func=ACT.Gelu_apprx_tanh)
            lru_act(act, cur, steps)
            barrier(act, cur)
            qk_read(act, "act", cur, HD ** -0.5)
            v_read(act, "act", cur)
            barrier(act, cur)
            sb_act(act, cur, steps)
            barrier(act, cur)
            qk_read(act, "act", cur)
            qk_written(act, cur)
            head_norm_act(act, cur, steps, mem_norm, between=lambda: v_read(act, "act", cur))
            barrier(act, cur)
            att_act(act, cur, steps, mem_att)
            barrier(act, cur)
            merge_act(act, cur, 4, DC, T, YT, lambda i, c: par[:, bass.ds(i * DC + (PAR1["b_gate"][0] + c), 1)])
            barrier(act, cur)
            out_act(act, cur, T)
            barrier(act, cur)
            main_norm_act(act, cur, steps, T)
            up_act(act, cur, steps)
            barrier(act, cur)
            down_act(act, cur)
            barrier(act, cur)
            turn_in_read(act, "act", cur, range(2), T)
            for layer in range(LAYERS):
                n = T if layer == LAYERS - 1 else 2 * T
                ada_act(act, cur, layer)
                barrier(act, cur)
                main_norm_act(act, cur, steps, 2 * T, shift=lambda c, s: MOD[:, c, s:s + 1])
                proj2_read(act, "act", cur, n)
                barrier(act, cur)
                att_act(act, cur, steps, na_x)
                barrier(act, cur)
                if n > T:
                    att_act(act, cur, steps, na_ctx)
                    barrier(act, cur)
                proj2_read(act, "act", cur, n, between=lambda: (skip_banks(cur, 8), lam_act(act, cur)))
                barrier(act, cur)
                att_act(act, cur, steps, da_x)
                barrier(act, cur)
                if n > T:
                    att_act(act, cur, steps, da_ctx)
                    barrier(act, cur)
                head_norm_act(act, cur, steps, da_norm(n, 0.0), between=lambda: gmlp_read(act, "act", cur, n // P, GU))
                gmlp_read(act, "act", cur, n // P, GV)
                barrier(act, cur)
                gmlp_ln_act(act, n // P, layer)
                gmlp_mix_act(act, cur, n // P)
                barrier(act, cur)
                merge_act(act, cur, 3, BC, n, Y2, None)
                barrier(act, cur)
                out_act(act, cur, n)
                barrier(act, cur)
                main_norm_act(act, cur, steps, n, shift=lambda c, s: MOD[:, 3 * DC + c, s:s + 1], split=False)
                barrier(act, cur)
                route_act(act, cur, steps, n // T)
                barrier(act, cur)
                experts_act(act, cur, n // T)
                barrier(act, cur)
                skip_banks(cur, DC)
                barrier(act, cur)
            main_norm_act(act, cur, steps, T, split=False)
            barrier(act, cur)
            turn_out_act(act, cur)
            barrier(act, cur)
            ended.append((cur.stage, cur.p, cur.g))
            act.dma_start(out.rearrange("a (m p) d -> p (a m) d", p=P), OUT).then_inc(stored, 16)
            act.wait_ge(stored, 16)

        @block.vector
        def _(dve):
            cur = Cursor("dve")
            steps = Steps(dve, dve_step)
            turn_in_read(dve, "dve", cur, range(4), 0)
            for _ in range(AHEAD):
                split_lo(dve, cur)
            barrier(dve, cur)
            main_norm_dve(dve, cur, steps, 2 * T, lambda c, s: p1("attn_g" if s == 0 else "mem_g", c))
            qk_read(dve, "dve", cur)
            forget_dve(dve, cur, steps)
            head_norm_dve(dve, cur, steps, fox_norm, between=lambda: v_read(dve, "dve", cur))
            barrier(dve, cur)
            att_dve(dve, cur, steps, fox)
            barrier(dve, cur)
            lru_start_dve(dve, cur, steps)
            g_lx = cur.g
            for h in range(2):
                copies(dve, "dve", cur, lambda j, h=h: LX[:, 4 * h + j, :], 4, T)
            for c in range(DC):
                skip_fm(dve, cur, 1)
                lru_conv_dve(dve, cur, steps, g_lx + c, c)
            lru_dve(dve, cur, steps)
            barrier(dve, cur)
            qk_read(dve, "dve", cur, HD ** -0.5)
            v_read(dve, "dve", cur)
            barrier(dve, cur)
            sb_dve(dve, cur, steps)
            barrier(dve, cur)
            qk_read(dve, "dve", cur)
            head_norm_dve(dve, cur, steps, mem_norm, between=lambda: v_read(dve, "dve", cur))
            barrier(dve, cur)
            att_dve(dve, cur, steps, mem_att)
            barrier(dve, cur)
            merge_dve(dve, cur, steps, 4, DC, T, YT)
            barrier(dve, cur)
            out_dve(dve, cur, T)
            barrier(dve, cur)
            main_norm_dve(dve, cur, steps, T, lambda c, s: p1("ffn_g", c))
            up_dve(dve, cur, steps)
            barrier(dve, cur)
            down_dve(dve, cur)
            barrier(dve, cur)
            turn_in_read(dve, "dve", cur, range(2), T)
            for layer in range(LAYERS):
                n = T if layer == LAYERS - 1 else 2 * T
                lam_init = 0.8 - 0.6 * float(np.exp(-0.3 * layer))
                ada_dve(dve, cur, steps, layer)
                dve.drain().then_inc(dve_step, 1)
                steps.n += 1
                dve.wait_ge(dve_step, steps.n)
                gmod_dve(dve, steps, "g1", 1)
                barrier(dve, cur)
                main_norm_dve(dve, cur, steps, 2 * T, lambda c, s: gmod[:, c, s:s + 1],
                              shift=lambda c, s: MOD[:, c, s:s + 1])
                proj2_read(dve, "dve", cur, n)
                barrier(dve, cur)
                dve.wait_ge(loads, 16 * LOADS["nab"][layer])
                att_dve(dve, cur, steps, na_x)
                barrier(dve, cur)
                if n > T:
                    att_dve(dve, cur, steps, na_ctx)
                    barrier(dve, cur)
                lam_start_dve(dve)
                proj2_read(dve, "dve", cur, n, between=lambda: (rope_dve(dve, cur, steps), skip_banks(cur, 1)))
                lam_dve(dve, cur, steps, lam_init, cur.g - BC - 1)
                barrier(dve, cur)
                att_dve(dve, cur, steps, da_x)
                barrier(dve, cur)
                if n > T:
                    att_dve(dve, cur, steps, da_ctx)
                    barrier(dve, cur)
                head_norm_dve(dve, cur, steps, da_norm(n, lam_init),
                              between=lambda: gmlp_read(dve, "dve", cur, n // P, GU))
                gmlp_read(dve, "dve", cur, n // P, GV)
                barrier(dve, cur)
                gmlp_ln_dve(dve, cur, steps, n // P, layer)
                gmlp_mix_dve(dve, cur, steps, n // P)
                barrier(dve, cur)
                merge_dve(dve, cur, steps, 3, BC, n, Y2)
                barrier(dve, cur)
                out_dve(dve, cur, n, gain=lambda c, s: MOD[:, 2 * DC + c, s:s + 1])
                gmod_dve(dve, steps, "g2", 4)
                barrier(dve, cur)
                main_norm_dve(dve, cur, steps, n, lambda c, s: gmod[:, c, s:s + 1], split=False)
                barrier(dve, cur)
                route_dve(dve, cur, steps, n // T)
                barrier(dve, cur)
                experts_dve(dve, cur, n // T)
                barrier(dve, cur)
                scatter_dve(dve, cur, n // T)
                barrier(dve, cur)
            main_norm_dve(dve, cur, steps, T, lambda c, s: p2("g_final", c), split=False)
            barrier(dve, cur)
            skip_banks(cur, 4)
            barrier(dve, cur)
            ended.append((cur.stage, cur.p, cur.g))
            assert len(set(ended)) == 1, ended

        @block.gpsimd
        def _(pool):
            cur = Cursor("pool")
            steps = Steps(pool, pool_step)
            for signal in looped:
                pool.sem_inc(signal, CREDIT)
            pool.dma_start(sel[:, :, :], a["sel"]).then_inc(loads, 16)
            pool.dma_start(head_sel[:, :, :], a["head_sel"]).then_inc(loads, 16)
            pool.dma_start(par[:, 0:N_PAR1], a["par1"]).then_inc(loads, 16)
            pool.wait_ge(loads, 16 * LOADS["start"])
            pool.wait_ge(const_load, 16)
            steps(nc.gpsimd.memset(small[:, :], 0.0))
            barrier(pool, cur)
            forget_pool(pool, cur)
            barrier(pool, cur)
            barrier(pool, cur)
            pool.dma_start(LW, a["lru_w"]).then_inc(loads, 16)
            pool.wait_ge(loads, 16 * LOADS["lru_w"])
            barrier(pool, cur)
            barrier(pool, cur)
            barrier(pool, cur)
            barrier(pool, cur)
            barrier(pool, cur)
            barrier(pool, cur)
            pool.dma_start(CTX_TM, a["ctx"].rearrange("a (m p) d -> p (a m) d", p=P)).then_inc(loads, 16)
            barrier(pool, cur)
            barrier(pool, cur)
            pool.dma_start(par[:, 0:N_PAR2], a["par2"][0]).then_inc(loads, 16)
            pool.wait_ge(loads, 16 * 8)
            barrier(pool, cur)
            n_loads = 8
            for layer in range(LAYERS):
                n = T if layer == LAYERS - 1 else 2 * T
                assert n_loads == LOADS["par"][layer], (n_loads, layer)
                pool.dma_start(NAB.rearrange("p a b c t -> p (a b c t)"), a["na_bias"][layer]).then_inc(loads, 16)
                barrier(pool, cur)
                barrier(pool, cur)
                pool.wait_ge(loads, 16 * (n_loads + 1))
                barrier(pool, cur)
                if n > T:
                    barrier(pool, cur)
                barrier(pool, cur)
                barrier(pool, cur)
                if n > T:
                    barrier(pool, cur)
                pool.dma_start(GWS, a["w_s"][layer]).then_inc(loads, 16)
                pool.dma_start(GLN[:, 0, :], a["ln_g"][layer].partition_broadcast(P)).then_inc(loads, 16)
                pool.dma_start(GLN[:, 1, :], a["ln_b"][layer].partition_broadcast(P)).then_inc(loads, 16)
                pool.wait_ge(loads, 16 * (n_loads + 4))
                barrier(pool, cur)
                barrier(pool, cur)
                barrier(pool, cur)
                barrier(pool, cur)
                barrier(pool, cur)
                route_pool(pool, cur, n // T)
                barrier(pool, cur)
                experts_pool(pool, cur, steps, n // T)
                barrier(pool, cur)
                barrier(pool, cur)
                n_loads += 4
                if layer < LAYERS - 1:
                    pool.dma_start(par[:, 0:N_PAR2], a["par2"][layer + 1]).then_inc(loads, 16)
                    n_loads += 1
                    pool.wait_ge(loads, 16 * n_loads)
            barrier(pool, cur)
            barrier(pool, cur)
            assert cur.stage == ended[0][0], (cur.stage, ended)


def _chunks(v):
    return v.reshape(-1, P).T


def _rows(w):
    return w.reshape(-1, P, w.shape[1]).transpose(1, 0, 2)


def _stream(x):
    parts = []

    def put(w):
        parts.append(w.reshape(P, -1))

    def tm(w, lo, hi):
        w = _rows(w)
        for c in range(lo, hi, 512):
            put(w[:, :, c:c + 512])

    def fm(w, lo, hi):
        w = _rows(w)[:, :, lo:hi]
        put(w.reshape(P, w.shape[1], -1, P).transpose(0, 2, 1, 3))

    w_in = x["w_in"][0]
    f0 = 3 * D + HEADS
    g0 = f0 + 6 * D
    fm(w_in, 0, 2 * D)
    tm(w_in, 2 * D, 3 * D)
    fm(w_in, f0, f0 + 2 * D)
    fm(w_in, f0 + 2 * D, f0 + 4 * D)
    tm(w_in, f0 + 4 * D, f0 + 5 * D)
    fm(w_in, f0 + 5 * D, f0 + 6 * D)
    fm(x["w_mem_kv"][0], 0, D)
    tm(x["w_mem_kv"][0], D, 2 * D)
    for n in range(4):
        for h in range(2):
            fm(w_in, g0 + n * D + h * 512, g0 + n * D + h * 512 + 512)
            fm(x["w_branch"][0, n], h * 512, h * 512 + 512)
    fm(x["w_out"][0], 0, D)
    for j in range(FC // 2):
        fm(x["w_up"][0], j * 256, (j + 1) * 256)
        fm(x["w_up"][0], FF + j * 256, FF + (j + 1) * 256)
    fm(x["w_down"][0], 0, D)
    for l in range(LAYERS):
        tm(x["w_ada_2"][l], 0, 6 * D)
        w = x["w_in_2"][l]
        for at, f in ((4, fm), (0, fm), (1, tm), (5, fm), (2, fm), (3, tm), (6, tm), (7, tm)):
            f(w, at * BW, (at + 1) * BW)
        for n in range(3):
            for h in range(2):
                lo = 8 * BW + n * D + h * 512
                fm(w, lo, lo + 512)
                fm(x["w_branch_2"][l, n], h * 512, h * 512 + 512)
        fm(x["w_out_2"][l], 0, D)
        for e in range(EXPERTS):
            for h in range(2):
                tm(x["w_e1_2"][l, e], h * 512, h * 512 + 512)
                tm(x["w_e3_2"][l, e], h * 512, h * 512 + 512)
            for h in range(2):
                tm(x["w_e2_2"][l, e][h * 512:(h + 1) * 512], 0, D)
    assert sum(w.shape[1] for w in parts) == STREAM_WORDS, (sum(w.shape[1] for w in parts), STREAM_WORDS)
    stream = np.zeros((N_SLOTS, P, WORDS), np.float32)
    at = 0
    for w in parts:
        while w.shape[1]:
            n = min(WORDS - at % WORDS, w.shape[1])
            stream[at // WORDS, :, at % WORDS:at % WORDS + n] = w[:, :n]
            at, w = at + n, w[:, n:]
    return stream


def _constants():
    i = np.arange(P)
    t = np.arange(T)
    c = {}
    c["ident"] = np.eye(P)
    c["tri"] = (i[:, None] >= i[None, :])
    c["ones"] = np.ones((P, P))
    row = (i[:, None] + P * np.arange(2)[None, :])
    c["causal"] = np.where(t[None, None, :] <= row[:, :, None], 0.0, NEG)
    valid = row[:, :, None] < t[None, None, :]
    c["sb_add"] = np.where(valid, 0.0, NEG)
    c["sb_neg"] = np.where(valid, -1.0, 0.0)
    c["before"] = t[None, None, :] < row[:, :, None]
    f = i % 64
    inv = (np.float32(10000.0) ** (-np.arange(0, 32, 2, dtype=np.float32) / np.float32(32))).astype(np.float32)
    place = np.where((f < 32)[:, None], (t // GRID)[None, :], (t % GRID)[None, :]).astype(np.float32)
    ang = place * inv[f % 16][:, None]
    c["cos"], c["sin"] = np.cos(ang), np.sin(ang)
    swap = np.zeros((P, P))
    for p in range(P):
        first = p % 32 < 16
        swap[p + 16 if first else p - 16, p] = -1.0 if first else 1.0
    c["swap"] = swap
    c["slots"] = np.broadcast_to(np.arange(CAP), (P, CAP))
    hs = np.zeros((P, DC, 16))
    for k in range(DC):
        hs[i, k, 2 * k + i // HD] = 1.0
    c["head_sum"] = hs
    rs = np.zeros((P, 4, 16))
    for k in range(4):
        rs[:, k, k] = 1.0
    c["row_sum"] = rs
    const = np.zeros((P, N_CONST), np.float32)
    for name, (lo, hi) in CONSTS.items():
        const[:, lo:hi] = np.asarray(c[name], np.float32).reshape(P, -1)
    sel = np.zeros((16, 16, P), np.float32)
    sel[np.arange(16), np.arange(16), :] = 1.0
    return const, sel, np.ascontiguousarray(hs.transpose(2, 1, 0)).astype(np.float32)


def _params(table, values, n):
    par = np.zeros((P, n), np.float32)
    for name, (lo, hi) in table.items():
        v = values[name]
        par[:v.shape[0], lo:hi] = v.reshape(v.shape[0], -1)
    return par


def _layout(x):
    const, sel, head_sel = _constants()
    pair = lambda v: np.concatenate([v, v]).reshape(P, 1)
    chunk_rows = lambda w: np.concatenate([_chunks(r) for r in w], axis=1)
    w_in = x["w_in"][0]
    par1 = dict(attn_g=_chunks(x["attn_norm_g"][0]), mem_g=_chunks(x["mem_norm_g"][0]),
                ffn_g=_chunks(x["ffn_norm_g"][0]), fox_q_g=pair(x["fox_q_norm_g"][0]),
                fox_k_g=pair(x["fox_k_norm_g"][0]), mem_q_g=_chunks(x["mem_q_norm_g"][0]),
                mem_k_g=_chunks(x["mem_k_norm_g"][0]), conv_w=chunk_rows(x["lru_conv_w"][0]),
                conv_b=_chunks(x["lru_conv_b"][0]), b_a=_chunks(x["lru_b_a"][0]), b_x=_chunks(x["lru_b_x"][0]),
                lam=_chunks(x["lru_lambda"][0]), b_gate=chunk_rows(x["b_gate"][0]),
                ffn_w=chunk_rows(x["ffn_conv_w"][0]), ffn_b=_chunks(x["ffn_conv_b"][0]),
                b_forget=x["b_forget"][0].reshape(16, 1), w_forget=_rows(w_in[:, 3 * D:3 * D + HEADS]))
    lru_w = np.zeros((P, 2, DC, P), np.float32)
    for g, name in enumerate(("lru_w_a", "lru_w_x")):
        for b in range(16):
            o = 64 * (b % 2)
            lru_w[o:o + 64, g, b // 2, o:o + 64] = x[name][0, b]
    both = np.stack([_chunks(x["c_2"][0]), _chunks(x["c_ctx_2"])], axis=2)
    par2 = []
    q = np.arange(T)
    qr, qc, kr, kcol = q[:, None] // GRID, q[:, None] % GRID, q[None, :] // GRID, q[None, :] % GRID
    start = np.clip(qc - 8, 0, GRID - 16)
    inside = (kcol >= start) & (kcol < start + 16)
    dr, dc = kr - qr + 7, np.where(inside, kcol - qc + 15, 0)
    na = np.full((LAYERS, P, 8, 2, T), NEG, np.float32)
    for l in range(LAYERS):
        par2.append(_params(PAR2, dict(
            b_ada=_chunks(x["b_ada_2"][l]), g1=_chunks(x["g_norm1_2"][l]), g2=_chunks(x["g_norm2_2"][l]),
            subln=x["da_subln_g_2"][l].reshape(P, 1), b_s=x["gm_b_s_2"][l].T,
            lam_q=np.stack([x["da_lam_q1_2"][l], x["da_lam_q2_2"][l]], axis=1),
            lam_k=np.stack([x["da_lam_k1_2"][l], x["da_lam_k2_2"][l]], axis=1),
            w_router=_rows(x["w_router_2"][l]), g_final=_chunks(x["g_final_2"]), c=both), N_PAR2))
        b = np.where(inside[None], x["na_rpb_2"][l][:, dr, dc], np.float32(NEG))
        na[l] = b.reshape(8, 2, P, T).transpose(2, 0, 1, 3)
    return {
        "stream": _stream(x), "x": x["x"], "mem": x["mem"], "ctx": x["ctx_2"], "const": const, "sel": sel,
        "head_sel": head_sel, "par1": _params(PAR1, par1, N_PAR1), "par2": np.stack(par2), "lru_w": lru_w,
        "na_bias": na.reshape(LAYERS, P, -1), "w_s": np.ascontiguousarray(x["gm_w_s_2"].transpose(0, 3, 1, 2)),
        "ln_g": x["gm_ln_g_2"], "ln_b": x["gm_ln_b_2"],
    }


def kernel(**inputs):
    import concourse.bacc as _bacc
    from concourse.bass_utils import run_bass_kernel_spmd as _run

    nc = _bacc.Bacc("TRN2", target_bir_lowering=False, num_devices=1)
    arrays, aps = {}, {}
    for name, v in _layout({k: np.asarray(v) for k, v in inputs.items()}).items():
        v = np.ascontiguousarray(v)
        arrays[f"in_{name}"] = v
        aps[name] = nc.dram_tensor(f"in_{name}", v.shape, mybir.dt.from_np(v.dtype), kind="ExternalInput").ap()
    aps["cum_scratch"] = nc.dram_tensor("cum_scratch", (HEADS, T), F32).ap()
    out = nc.dram_tensor("out_0", (1, T, D), F32, kind="ExternalOutput").ap()
    build(nc, aps, out)
    r = _run(nc, [arrays], core_ids=[0])
    return r.results[0]["out_0"]
```
